# Optimizing a Trainium2 kernel written in Bass

```python
import jax
import jax.numpy as jnp
from jax import lax
import numpy as np

D_MODEL = 1024
BATCH = 1
SEQ = 128
DEPTH = 2
DEC_BATCH = 1
DEC_SEQ = 512
PAST_LEN = 128

GRID_W = 64
HEAD_DIM = 64
N_GROUPS = 4
GROUP_W = D_MODEL // N_GROUPS
MIX_W = N_GROUPS * GROUP_W
GROUP_HEADS = GROUP_W // HEAD_DIM
CHUNK = 128
NA_KH = 8
NA_KW = 16
NA_QB_W = 16
NA_KB_W = 2 * NA_KW
MLA_Q_RANK = D_MODEL // 4
MLA_KV_RANK = D_MODEL // 8
MLA_NOPE = 64
MLA_ROPE = 32
MLA_V = 64
MLA_SCALE = (MLA_NOPE + MLA_ROPE) ** -0.5
SWA_KV_HEADS = GROUP_HEADS // 2
SWA_GROUP = GROUP_HEADS // SWA_KV_HEADS
SWA_WIN = 128
PEER_HEADS = 8
PEER_N_KEYS = 128
PEER_TOPK = 16
PEER_HALF = 128
N_EXPERTS = PEER_N_KEYS * PEER_N_KEYS
Q_BLOCK = 128
TOKEN_BLOCK = 128
ROPE_BASE = 10000.0
LN_EPS = 1e-5
NEG_INF = -1e30
ALPHA = (2 * DEPTH) ** 0.25
BETA = (8 * DEPTH) ** -0.25
A_COLS = 2 * GROUP_W
B_COLS = 3 * GROUP_W
C_COLS = MLA_Q_RANK + MLA_KV_RANK + MLA_ROPE
D_COLS = (GROUP_HEADS + 2 * SWA_KV_HEADS) * HEAD_DIM
IN_COLS = A_COLS + B_COLS + C_COLS + D_COLS

kernel_name = 'hybrid_flow_prefix_peer_step'

def layer_norm(x, g, b):
    xf = x.astype(jnp.float32)
    mu = jnp.mean(xf, -1, keepdims=True)
    var = jnp.mean(jnp.square(xf - mu), -1, keepdims=True)
    return ((xf - mu) * lax.rsqrt(var + LN_EPS) * g + b).astype(x.dtype)

def rms_norm(x, g):
    xf = x.astype(jnp.float32)
    return (xf * lax.rsqrt(jnp.mean(jnp.square(xf), -1, keepdims=True) + LN_EPS) * g).astype(x.dtype)

def axial_rope(n_tok, rot_dim):
    t = jnp.arange(n_tok)
    row = (t // GRID_W).astype(jnp.float32)
    col = (t % GRID_W).astype(jnp.float32)
    nf = rot_dim // 4
    freqs = ROPE_BASE ** (-jnp.arange(nf, dtype=jnp.float32) / nf)
    ang = jnp.concatenate([row[:, None] * freqs, col[:, None] * freqs], -1)
    return jnp.cos(ang), jnp.sin(ang)

def apply_rope(x, cos, sin):
    half = x.shape[-1] // 2
    shape = (x.shape[1],) + (1,) * (x.ndim - 3) + (half,)
    cos = cos.reshape(shape).astype(x.dtype)
    sin = sin.reshape(shape).astype(x.dtype)
    x1, x2 = x[..., :half], x[..., half:]
    return jnp.concatenate([x1 * cos - x2 * sin, x2 * cos + x1 * sin], -1)

def heads(t, n):
    return t.reshape(t.shape[0], t.shape[1], n, -1)

def modulation(cond, w_ada, b_ada):
    m = (jax.nn.silu(cond) @ w_ada + b_ada).reshape(cond.shape[0], 1, 6, D_MODEL)
    return [m[:, :, i] for i in range(6)]

def split_proj(h, w_in):
    z = h @ w_in
    return jnp.split(z, [A_COLS, A_COLS + B_COLS, A_COLS + B_COLS + C_COLS], axis=-1)

def split_mla(hC):
    return (hC[..., :MLA_Q_RANK], hC[..., MLA_Q_RANK:MLA_Q_RANK + MLA_KV_RANK],
            hC[..., MLA_Q_RANK + MLA_KV_RANK:])

def split_swa(hD):
    nq = GROUP_HEADS * HEAD_DIM
    nk = SWA_KV_HEADS * HEAD_DIM
    return (heads(hD[..., :nq], GROUP_HEADS), heads(hD[..., nq:nq + nk], SWA_KV_HEADS),
            heads(hD[..., nq + nk:], SWA_KV_HEADS))

def chunk_mlp(hA, p):
    B, L, _ = hA.shape
    u, v = jnp.split(jax.nn.gelu(hA), 2, axis=-1)
    v = layer_norm(v, p['a_norm_g'], p['a_norm_b'])
    vc = v.reshape(B, L // CHUNK, CHUNK, GROUP_HEADS, GROUP_W // GROUP_HEADS)
    mixed = jnp.einsum('hpq,bcqhd->bcphd', p['a_w_s'], vc) + p['a_b_s'].T[None, None, :, :, None]
    return u * mixed.reshape(B, L, GROUP_W)

def dense_attention(q, k, v, scale, sinks=None):
    B, Lq, H, dq = q.shape
    qb = jnp.moveaxis(q.reshape(B, Lq // Q_BLOCK, Q_BLOCK, H, dq), 1, 0)

    def one_block(qblk):
        s = jnp.einsum('bqhd,bkhd->bhqk', qblk, k, preferred_element_type=jnp.float32) * scale
        if sinks is not None:
            sk = jnp.broadcast_to(sinks.astype(jnp.float32)[None, :, None, None], s.shape[:-1] + (1,))
            pr = jax.nn.softmax(jnp.concatenate([s, sk], -1), -1)[..., :-1]
        else:
            pr = jax.nn.softmax(s, -1)
        return jnp.einsum('bhqk,bkhd->bqhd', pr.astype(v.dtype), v)

    out = lax.map(one_block, qb)
    return jnp.moveaxis(out, 0, 1).reshape(B, Lq, H * v.shape[-1])

def neighbourhood_attention(q, k, v, ck, cv, rpb):
    B, L, H, dh = q.shape
    rows = L // GRID_W
    kh = min(NA_KH, rows)
    ncb = GRID_W // NA_QB_W
    nk = kh * NA_KB_W
    r = jnp.arange(rows)
    row_idx = jnp.clip(r - kh // 2, 0, rows - kh)[:, None] + jnp.arange(kh)[None, :]
    cb = jnp.arange(ncb)
    col_idx = (jnp.clip(cb * NA_QB_W - NA_KW // 2, 0, GRID_W - NA_KB_W)[:, None]
               + jnp.arange(NA_KB_W)[None, :])
    qcol = cb[:, None] * NA_QB_W + jnp.arange(NA_QB_W)[None, :]
    cstart = jnp.clip(qcol - NA_KW // 2, 0, GRID_W - NA_KW)
    kc = col_idx[:, None, :]
    col_ok = (kc >= cstart[..., None]) & (kc < cstart[..., None] + NA_KW)
    mask = jnp.broadcast_to(col_ok[:, :, None, :], (ncb, NA_QB_W, kh, NA_KB_W)).reshape(ncb, NA_QB_W, nk)
    dr = row_idx - r[:, None] + NA_KH - 1
    dc = jnp.clip(kc - qcol[..., None] + NA_KW - 1, 0, 2 * NA_KW - 2)
    bias = rpb[:, dr[:, None, None, :, None], dc[None, :, :, None, :]].reshape(H, rows, ncb, NA_QB_W, nk)
    ri = row_idx[:, None, :, None]
    ci = col_idx[None, :, None, :]
    k_loc = k.reshape(B, rows, GRID_W, H, dh)[:, ri, ci].reshape(B, rows, ncb, nk, H, dh)
    v_loc = v.reshape(B, rows, GRID_W, H, dh)[:, ri, ci].reshape(B, rows, ncb, nk, H, dh)
    qb = q.reshape(B, rows, ncb, NA_QB_W, H, dh)
    scale = dh ** -0.5
    s_loc = (jnp.einsum('brcqhd,brckhd->bhrcqk', qb, k_loc, preferred_element_type=jnp.float32) * scale
             + bias.astype(jnp.float32)[None])
    s_loc = jnp.where(mask, s_loc, NEG_INF)
    s_ctx = jnp.einsum('brcqhd,bhkd->bhrcqk', qb, ck, preferred_element_type=jnp.float32) * scale
    pr = jax.nn.softmax(jnp.concatenate([s_loc, s_ctx], -1), -1).astype(v.dtype)
    out = (jnp.einsum('bhrcqk,brckhd->brcqhd', pr[..., :nk], v_loc)
           + jnp.einsum('bhrcqk,bhkd->brcqhd', pr[..., nk:], cv))
    return out.reshape(B, L, H * dh)

def sliding_window_attention(q, k, v, ck, cv, sinks):
    B, L, Hq, dh = q.shape
    nb = L // SWA_WIN
    pad = ((0, 0), (SWA_WIN, SWA_WIN), (0, 0), (0, 0))
    kp = jnp.pad(k, pad).reshape(B, nb + 2, SWA_WIN, SWA_KV_HEADS, dh)
    vp = jnp.pad(v, pad).reshape(B, nb + 2, SWA_WIN, SWA_KV_HEADS, dh)
    kband = jnp.concatenate([kp[:, :-2], kp[:, 1:-1], kp[:, 2:]], axis=2)
    vband = jnp.concatenate([vp[:, :-2], vp[:, 1:-1], vp[:, 2:]], axis=2)
    qg = q.reshape(B, nb, SWA_WIN, SWA_KV_HEADS, SWA_GROUP, dh)
    scale = dh ** -0.5
    nband = 3 * SWA_WIN
    s = jnp.einsum('bnqkgd,bnjkd->bkgnqj', qg, kband, preferred_element_type=jnp.float32) * scale
    qi = jnp.arange(SWA_WIN)
    kj = jnp.arange(nband)
    in_win = jnp.abs(kj[None, :] - SWA_WIN - qi[:, None]) <= SWA_WIN
    kpos = jnp.arange(nb)[:, None] * SWA_WIN - SWA_WIN + kj[None, :]
    in_seq = (kpos >= 0) & (kpos < L)
    s = jnp.where(in_win[None] & in_seq[:, None, :], s, NEG_INF)
    s_ctx = jnp.einsum('bnqkgd,bkcd->bkgnqc', qg, ck, preferred_element_type=jnp.float32) * scale
    sk = jnp.broadcast_to(sinks.astype(jnp.float32).reshape(SWA_KV_HEADS, SWA_GROUP)[None, :, :, None, None, None],
                          s.shape[:-1] + (1,))
    pr = jax.nn.softmax(jnp.concatenate([s, s_ctx, sk], -1), -1).astype(v.dtype)
    nctx = ck.shape[2]
    out = (jnp.einsum('bkgnqj,bnjkd->bnqkgd', pr[..., :nband], vband)
           + jnp.einsum('bkgnqc,bkcd->bnqkgd', pr[..., nband:nband + nctx], cv))
    return out.reshape(B, L, Hq * dh)

def mla_query(cq, p):
    q = rms_norm(cq, p['mla_q_norm_g']) @ p['mla_w_uq']
    return heads(q, GROUP_HEADS)

def mla_expand_kv(ckv_n, krope, w_ukv):
    B, L, _ = ckv_n.shape
    kv = (ckv_n @ w_ukv).reshape(B, L, GROUP_HEADS, MLA_NOPE + MLA_V)
    k = jnp.concatenate([kv[..., :MLA_NOPE],
                         jnp.broadcast_to(krope[:, :, None, :], (B, L, GROUP_HEADS, MLA_ROPE))], -1)
    return k, kv[..., MLA_NOPE:]

def merge_groups(outs, g, w_out):
    o = jnp.concatenate(outs, -1)
    B, L, _ = o.shape
    o = rms_norm(o.reshape(B, L, N_GROUPS, GROUP_W), g.reshape(N_GROUPS, GROUP_W)).reshape(B, L, MIX_W)
    return o @ w_out

def peer_ffn(h, p):
    B, L, D = h.shape
    xt = h.reshape(B * L // TOKEN_BLOCK, TOKEN_BLOCK, D)

    def one_block(xb):
        q = (xb @ p['peer_w_q']).reshape(TOKEN_BLOCK, PEER_HEADS, 2, PEER_HALF)
        s = jnp.einsum('thpd,pnd->thpn', q, p['peer_sub_keys'], preferred_element_type=jnp.float32)
        sv, si = lax.top_k(s, PEER_TOPK)
        cand = (sv[:, :, 0, :, None] + sv[:, :, 1, None, :]).reshape(TOKEN_BLOCK, PEER_HEADS, PEER_TOPK * PEER_TOPK)
        cid = (si[:, :, 0, :, None] * PEER_N_KEYS + si[:, :, 1, None, :]).reshape(TOKEN_BLOCK, PEER_HEADS, PEER_TOPK * PEER_TOPK)
        fv, fi = lax.top_k(cand, PEER_TOPK)
        eid = jnp.take_along_axis(cid, fi, -1)
        gate = jax.nn.softmax(fv, -1)
        act = jax.nn.gelu(jnp.einsum('thkd,td->thk', p['peer_u'][eid], xb, preferred_element_type=jnp.float32))
        return jnp.einsum('thk,thkd->td', (gate * act).astype(xb.dtype), p['peer_v'][eid])

    return lax.map(one_block, xt).reshape(B, L, D)

def context_mixer(h, p):
    hA, hB, hC, hD = split_proj(h, p['w_in'])
    oA = chunk_mlp(hA, p)
    qB, kB, vB = [heads(t, GROUP_HEADS) for t in jnp.split(hB, 3, axis=-1)]
    oB = dense_attention(qB, kB, vB, HEAD_DIM ** -0.5)
    cq, ckv, krope = split_mla(hC)
    qC = mla_query(cq, p)
    ckv_n = rms_norm(ckv, p['mla_kv_norm_g'])
    kC, vC = mla_expand_kv(ckv_n, krope, p['mla_w_ukv'])
    oC = dense_attention(qC, kC, vC, MLA_SCALE)
    qD, kD, vD = split_swa(hD)
    oD = dense_attention(qD, jnp.repeat(kD, SWA_GROUP, axis=2), jnp.repeat(vD, SWA_GROUP, axis=2),
                         HEAD_DIM ** -0.5, p['swa_sinks'])
    state = (kB.transpose(0, 2, 1, 3), vB.transpose(0, 2, 1, 3), ckv_n, krope,
             kD.transpose(0, 2, 1, 3), vD.transpose(0, 2, 1, 3))
    return [oA, oB, oC, oD], state

def latent_mixer(h, p, ctx, rope):
    nat_k, nat_v, mla_ckv, mla_krope, swa_k, swa_v = ctx
    cos_c, sin_c, cos_d, sin_d = rope
    hA, hB, hC, hD = split_proj(h, p['w_in'])
    oA = chunk_mlp(hA, p)
    qB, kB, vB = [heads(t, GROUP_HEADS) for t in jnp.split(hB, 3, axis=-1)]
    oB = neighbourhood_attention(qB, kB, vB, nat_k, nat_v, p['nat_rpb'])
    cq, ckv, krope = split_mla(hC)
    qC = mla_query(cq, p)
    qC = jnp.concatenate([qC[..., :MLA_NOPE], apply_rope(qC[..., MLA_NOPE:], cos_c, sin_c)], -1)
    kC, vC = mla_expand_kv(rms_norm(ckv, p['mla_kv_norm_g']), apply_rope(krope, cos_c, sin_c), p['mla_w_ukv'])
    kX, vX = mla_expand_kv(mla_ckv, mla_krope, p['mla_w_ukv'])
    oC = dense_attention(qC, jnp.concatenate([kX, kC], 1), jnp.concatenate([vX, vC], 1), MLA_SCALE)
    qD, kD, vD = split_swa(hD)
    oD = sliding_window_attention(apply_rope(qD, cos_d, sin_d), apply_rope(kD, cos_d, sin_d), vD,
                                  swa_k, swa_v, p['swa_sinks'])
    return [oA, oB, oC, oD], None

def trunk_layer(x, cond, p, token_mixer):
    sh1, sc1, g1, sh2, sc2, g2 = modulation(cond, p['w_ada'], p['b_ada'])
    outs, state = token_mixer(x * (1 + sc1) + sh1, p)
    x = layer_norm(ALPHA * x + g1 * merge_groups(outs, p['out_norm_g'], p['w_out']), p['ln1_g'], p['ln1_b'])
    x = layer_norm(ALPHA * x + g2 * peer_ffn(x * (1 + sc2) + sh2, p), p['ln2_g'], p['ln2_b'])
    return x, state

def setup_inputs(seed: int = 0) -> dict:
    key = jax.random.key(seed)
    ks = iter(jax.random.split(key, 40))

    def nrm(shape, s=1.0):
        return jax.random.normal(next(ks), shape, jnp.float32) * s

    def gain(shape):
        return 1.0 + nrm(shape, 0.02)

    return {
        'x_prompt': nrm((BATCH, SEQ, D_MODEL)),
        'x_sample': nrm((DEC_BATCH, DEC_SEQ, D_MODEL)),
        'cache_nat_k': nrm((DEC_BATCH, DEPTH, GROUP_HEADS, PAST_LEN, HEAD_DIM)),
        'cache_nat_v': nrm((DEC_BATCH, DEPTH, GROUP_HEADS, PAST_LEN, HEAD_DIM)),
        'cache_mla_ckv': nrm((DEC_BATCH, DEPTH, PAST_LEN, MLA_KV_RANK)),
        'cache_mla_krope': nrm((DEC_BATCH, DEPTH, PAST_LEN, MLA_ROPE)),
        'cache_swa_k': nrm((DEC_BATCH, DEPTH, SWA_KV_HEADS, PAST_LEN, HEAD_DIM)),
        'cache_swa_v': nrm((DEC_BATCH, DEPTH, SWA_KV_HEADS, PAST_LEN, HEAD_DIM)),
        'c': nrm((DEC_BATCH, D_MODEL)),
        'c_ctx': nrm((D_MODEL,)),
        'w_in': nrm((DEPTH, D_MODEL, IN_COLS), D_MODEL ** -0.5),
        'w_out': nrm((DEPTH, MIX_W, D_MODEL), BETA * MIX_W ** -0.5),
        'out_norm_g': gain((DEPTH, MIX_W)),
        'w_ada': nrm((DEPTH, D_MODEL, 6 * D_MODEL), 0.5 * D_MODEL ** -0.5),
        'b_ada': nrm((DEPTH, 6 * D_MODEL), 0.02),
        'ln1_g': gain((DEPTH, D_MODEL)),
        'ln1_b': nrm((DEPTH, D_MODEL), 0.02),
        'ln2_g': gain((DEPTH, D_MODEL)),
        'ln2_b': nrm((DEPTH, D_MODEL), 0.02),
        'a_norm_g': gain((DEPTH, GROUP_W)),
        'a_norm_b': nrm((DEPTH, GROUP_W), 0.02),
        'a_w_s': nrm((DEPTH, GROUP_HEADS, CHUNK, CHUNK), CHUNK ** -0.5),
        'a_b_s': gain((DEPTH, GROUP_HEADS, CHUNK)),
        'nat_rpb': nrm((DEPTH, GROUP_HEADS, 2 * NA_KH - 1, 2 * NA_KW - 1), 0.1),
        'mla_q_norm_g': gain((DEPTH, MLA_Q_RANK)),
        'mla_w_uq': nrm((DEPTH, MLA_Q_RANK, GROUP_HEADS * (MLA_NOPE + MLA_ROPE)), MLA_Q_RANK ** -0.5),
        'mla_kv_norm_g': gain((DEPTH, MLA_KV_RANK)),
        'mla_w_ukv': nrm((DEPTH, MLA_KV_RANK, GROUP_HEADS * (MLA_NOPE + MLA_V)), MLA_KV_RANK ** -0.5),
        'swa_sinks': nrm((DEPTH, GROUP_HEADS), 0.5),
        'peer_w_q': nrm((DEPTH, D_MODEL, PEER_HEADS * 2 * PEER_HALF), D_MODEL ** -0.5),
        'peer_sub_keys': nrm((DEPTH, 2, PEER_N_KEYS, PEER_HALF), PEER_HALF ** -0.5),
        'peer_u': nrm((DEPTH, N_EXPERTS, D_MODEL), D_MODEL ** -0.5),
        'peer_v': nrm((DEPTH, N_EXPERTS, D_MODEL), BETA),
    }

def reference(x_prompt, x_sample, cache_nat_k, cache_nat_v, cache_mla_ckv, cache_mla_krope,
              cache_swa_k, cache_swa_v, c, c_ctx, w_in, w_out, out_norm_g, w_ada, b_ada,
              ln1_g, ln1_b, ln2_g, ln2_b, a_norm_g, a_norm_b, a_w_s, a_b_s, nat_rpb,
              mla_q_norm_g, mla_w_uq, mla_kv_norm_g, mla_w_ukv, swa_sinks,
              peer_w_q, peer_sub_keys, peer_u, peer_v):
    lat_len = x_sample.shape[1]
    cos_c, sin_c = axial_rope(lat_len, MLA_ROPE)
    cos_d, sin_d = axial_rope(lat_len, HEAD_DIM)
    rope = (cos_c, sin_c, cos_d, sin_d)
    y_prompt = x_prompt
    y_sample = x_sample
    st_nat_k, st_nat_v, st_ckv, st_krope, st_swa_k, st_swa_v = [], [], [], [], [], []
    for l in range(DEPTH):
        p = {
            'w_in': w_in[l], 'w_out': w_out[l], 'out_norm_g': out_norm_g[l],
            'w_ada': w_ada[l], 'b_ada': b_ada[l],
            'ln1_g': ln1_g[l], 'ln1_b': ln1_b[l], 'ln2_g': ln2_g[l], 'ln2_b': ln2_b[l],
            'a_norm_g': a_norm_g[l], 'a_norm_b': a_norm_b[l], 'a_w_s': a_w_s[l], 'a_b_s': a_b_s[l],
            'nat_rpb': nat_rpb[l],
            'mla_q_norm_g': mla_q_norm_g[l], 'mla_w_uq': mla_w_uq[l],
            'mla_kv_norm_g': mla_kv_norm_g[l], 'mla_w_ukv': mla_w_ukv[l],
            'swa_sinks': swa_sinks[l],
            'peer_w_q': peer_w_q[l], 'peer_sub_keys': peer_sub_keys[l],
            'peer_u': peer_u[l], 'peer_v': peer_v[l],
        }
        y_prompt, st = trunk_layer(y_prompt, c_ctx[None, :], p, context_mixer)
        st_nat_k.append(st[0]); st_nat_v.append(st[1]); st_ckv.append(st[2])
        st_krope.append(st[3]); st_swa_k.append(st[4]); st_swa_v.append(st[5])
        ctx = (cache_nat_k[:, l], cache_nat_v[:, l], cache_mla_ckv[:, l], cache_mla_krope[:, l],
               cache_swa_k[:, l], cache_swa_v[:, l])
        y_sample, _ = trunk_layer(y_sample, c, p,
                                  lambda hh, pp: latent_mixer(hh, pp, ctx, rope))
    new_nat_k = jnp.stack(st_nat_k, axis=1)
    new_nat_v = jnp.stack(st_nat_v, axis=1)
    new_mla_ckv = jnp.stack(st_ckv, axis=1)
    new_mla_krope = jnp.stack(st_krope, axis=1)
    new_swa_k = jnp.stack(st_swa_k, axis=1)
    new_swa_v = jnp.stack(st_swa_v, axis=1)
    return (y_prompt, y_sample, new_nat_k, new_nat_v, new_mla_ckv, new_mla_krope, new_swa_k, new_swa_v)


_drawn_inputs = setup_inputs


def setup_inputs(seed=0):
    import zlib

    import numpy as np

    out = dict(_drawn_inputs(seed))
    spreads = {}
    factors = {'cache_mla_ckv': 4.717,
     'cache_mla_krope': 7.274,
     'cache_swa_k': 2.963,
     'out_norm_g': 8.0,
     'a_norm_g': 8.0,
     'a_norm_b': 8.0,
     'a_b_s': 8.0,
     'nat_rpb': 8.0,
     'mla_q_norm_g': 8.0,
     'mla_kv_norm_g': 3.047,
     'swa_sinks': 8.0}
    for name, (base, spread) in spreads.items():
        noise = np.random.default_rng([zlib.crc32(name.encode()), seed]).standard_normal(out[name].shape)
        drawn = base * np.exp(spread * noise) if base else spread * noise
        out[name] = jnp.asarray(drawn.astype(out[name].dtype))
    for name, factor in factors.items():
        out[name] = (out[name] * factor).astype(out[name].dtype)
    return out
```

```python
from contextlib import ExitStack

import numpy as np

import concourse.bass as bass
from concourse import mybir

F32 = mybir.dt.float32
U32 = mybir.dt.uint32
ACT = mybir.ActivationFunctionType
ALU = mybir.AluOpType
AX = mybir.AxisListType.X
ds = bass.ds

P = 128
DEPTH, D = 2, 1024
KD = D // P
SEQ, DEC_SEQ, GRID_W = 128, 512, 64
NLAT = DEC_SEQ // P
NBLK = 1 + NLAT
NSLOT = NBLK + 1
CTX = NSLOT - 1
H, HD, GW = 4, 64, 256
QR, KVR, NOPE, ROPE, VD = 256, 128, 64, 32, 64
CH = NOPE + ROPE
IN_COLS = 2 * GW + 3 * GW + QR + KVR + ROPE + 8 * HD
C_B, C_C, C_D = 2 * GW, 5 * GW, 5 * GW + QR + KVR + ROPE
ROWS = DEC_SEQ // GRID_W
NA_KH, NA_KW = 8, 16
NDR = 2 * NA_KH - 2
RPB_PAD = GRID_W
RPB_ROW = 160
PH, PK, TOPK = 8, 128, 16
NSEL = PH * TOPK
NEXP = PK * PK
ALPHA = (2 * DEPTH) ** 0.25
EPS = 1e-5
SCALE = HD ** -0.5
MLA_SCALE = CH ** -0.5
MASKED = -1e30
MOD = 6 * KD
ADA_COLS = 512
ADA_PIECES = 6 * D // ADA_COLS
ROPE_COLS = 2 * ROPE + 2 * HD

SP_B, SP_D, SP_A, SP_C = 0, 2 * P, 4 * P, 4 * P + GW
SP_COLS = SP_C + H * P

W_COLS = 24576
W_IN = KD * IN_COLS
RING = W_COLS // D


def build(nc, a):
    es = ExitStack()
    with es:
        def sb(name, shape, dt=F32):
            return es.enter_context(nc.sbuf_tensor(name, shape, dt))

        sems = []

        def sem(name):
            s = es.enter_context(nc.semaphore(name))
            sems.append(s)
            return s

        x_dram = nc.dram_tensor("x_state", [NBLK, P, D], F32).ap()
        x2_dram = nc.dram_tensor("x2_state", [NBLK, P, D], F32).ap()
        mod_dram = nc.dram_tensor("mod_rows", [NBLK, MOD, P], F32).ap()
        spill_dram = nc.dram_tensor("spill_state", [NBLK, P, SP_COLS], F32).ap()
        eid_dram = nc.dram_tensor("expert_ids", [NBLK, P, NSEL], U32).ap()
        toep_dram = nc.dram_tensor("bias_rows", [DEPTH, P, H * NDR * GRID_W], F32).ap()
        gate_dram = nc.dram_tensor("gate_state", [NBLK, P, NSEL], F32).ap()

        W = sb("W", [P, W_COLS])
        ktB = sb("ktB", [P, 2, NSLOT * P])
        ktC = sb("ktC", [CH, H, NSLOT * P])
        ktD = sb("ktD", [P, NSLOT * P])
        vB = sb("vB", [P, NSLOT, GW])
        vC = sb("vC", [P, NSLOT, GW])
        vD = sb("vD", [P, NSLOT, 2 * HD])
        toep = sb("toep", [P, H, NDR, GRID_W])
        band = sb("band", [P, 7 * P])
        natmask = sb("natmask", [P, GRID_W])
        ident = sb("ident", [P, P])
        iota16 = sb("iota16", [P, TOPK], U32)
        bc = sb("bc", [P, 3, D])
        big = sb("big", [P, 4864])
        hT = sb("hT", [P, KD, P])
        xs = sb("xs", [P, D])
        xa = sb("xa", [P, D])
        ob = sb("ob", [P, D])
        condT = sb("condT", [P, KD, 2])
        condS = sb("condS", [P, KD, 2])
        b_ada = sb("b_ada", [P, MOD])
        mod = sb("mod", [P, 2, MOD])
        modb = sb("modb", [P, NBLK, 2 * KD])
        modT = sb("modT", [2 * MOD, P])
        sinks = sb("sinks", [P, H])
        a_b = sb("a_b", [P, H])
        neg_half = sb("neg_half", [P, 4])
        small = sb("small", [P, 64])
        first_row = sb("first_row", [P, 1])
        st12 = sb("st12", [P, 2, 6])
        mv = sb("mv", [P, 2])
        ve = sb("ve", [P, 4])
        rstd = sb("rstd", [P, 4])
        gates = sb("gates", [P, NSEL])
        eid = sb("eid", [P, NSEL], U32)
        eid_s = sb("eid_s", [P, 2, TOPK], U32)
        dots = sb("dots", [P, 2, TOPK])
        gel = sb("gel", [P, 2, TOPK])
        wsel = sb("wsel", [P, 2, TOPK])

        w_in = W[:, 0:W_IN].rearrange("p (k n) -> p k n", k=KD)
        at = [W_IN]

        def tail(n):
            v = W[:, at[0]:at[0] + n]
            at[0] += n
            assert at[0] <= W_COLS
            return v

        w_uq = tail(2 * H * CH).rearrange("p (k n) -> p k n", k=2)
        w_ukv = tail(H * (NOPE + VD)).rearrange("p (h n) -> p h n", h=H)
        a_wT = tail(H * P).rearrange("p (h n) -> p h n", h=H)
        a_g, a_bb = tail(GW), tail(GW)
        mq_g, mkv_g = tail(QR), tail(KVR)
        rope_t = tail(NBLK * ROPE_COLS).rearrange("p (b n) -> p b n", b=NBLK)
        gz = tail(2 * GW)
        vn = tail(GW)
        ckvT = tail(P)
        cqT = tail(2 * P).rearrange("p (k n) -> p k n", k=2)
        kr = tail(CH)
        cqn = tail(QR)
        ckvn = tail(KVR)
        ropeA = tail(6 * HD)
        z = big[:, 0:IN_COLS]
        spill = big[:, IN_COLS:IN_COLS + SP_COLS]
        qc = big[:, IN_COLS + SP_COLS:IN_COLS + SP_COLS + H * CH]
        ropeB = big[:, IN_COLS + SP_COLS + H * CH:IN_COLS + SP_COLS + H * CH + 6 * HD]
        zr = big[:, IN_COLS + SP_COLS + H * CH + 6 * HD:IN_COLS + SP_COLS + H * CH + 12 * HD]
        KEYS = (NLAT + 1) * P
        qT = big[:, 0:SP_A]
        qTC = big[0:CH, SP_A:SP_A + H * P]
        sS = big[:, 1024:1024 + 2 * KEYS].rearrange("p (a n) -> p a n", a=2)
        pr = big[:, 2304:2304 + 2 * KEYS].rearrange("p (a n) -> p a n", a=2)
        prT = big[:, 3584:3584 + 2 * KEYS].rearrange("p (a n) -> p a n", a=2)
        w_out = W[:, 0:KD * D].rearrange("p (k n) -> p k n", k=KD)
        og_bc = W[:, KD * D:KD * D + D]
        sc2_bc = W[:, KD * D + D:KD * D + 2 * D]
        sh2_bc = W[:, KD * D + 2 * D:KD * D + 3 * D]
        RC = 2 * PH * P
        w_q = W[:, 0:KD * RC].rearrange("p (k n) -> p k n", k=KD)
        rt = W[:, KD * RC:KD * RC + 4 * RC].rearrange("p (a n) -> p a n", a=4)
        scores = rt[:, 0, :].rearrange("p (g n) -> p g n", n=PK)
        scores2 = rt[:, 1, :].rearrange("p (g n) -> p g n", n=PK)
        cand = rt[:, 2, :].rearrange("p (h n) -> p h n", h=PH)
        cand2 = rt[:, 3, :].rearrange("p (h n) -> p h n", h=PH)
        onehot = rt[:, 1, :].rearrange("p (s j) -> p s j", j=TOPK)
        qsel = bc[:, 0:2, :].rearrange("p a (g t) -> p (a g) t", t=P)
        skT = bc[:, 2, 0:2 * PK].rearrange("p (s n) -> p s n", s=2)
        sv = big[:, 0:256].rearrange("p (g k) -> p g k", k=TOPK)
        si = big[:, 256:512].bitcast(U32).rearrange("p (g k) -> p g k", k=TOPK)
        sif = big[:, 512:768].rearrange("p (g k) -> p g k", k=TOPK)
        fv = big[:, 768:896].rearrange("p (h k) -> p h k", k=TOPK)
        fi = big[:, 896:1024].bitcast(U32).rearrange("p (h k) -> p h k", k=TOPK)
        fpart = big[:, 1024:1280].bitcast(U32).rearrange("p (a s) -> p a s", a=2)
        id_rc = big[:, 1280:1536].rearrange("p (a s) -> p a s", a=2)
        eidf = big[:, 1536:1664]
        fe = big[:, 1664:1792].rearrange("p (h k) -> p h k", k=TOPK)
        ring = W[:, :].rearrange("p (r n) -> p r n", n=D)
        junk = big[:, 0:2 * D].rearrange("p (a n) -> p a n", a=2)
        accs = big[:, 2 * D:4 * D].rearrange("p (a n) -> p a n", a=2)

        ps = es.enter_context(nc.psum_tensor("ps", [P, 8 * 512], F32))

        def bank(i, n=512, parts=P):
            return ps[0:parts, i * 512:i * 512 + n]

        loaded = sem("loaded")
        loaded2 = sem("loaded2")
        stored = sem("stored")
        piece_in = [sem(f"piece_in{i}") for i in range(3)]
        slots_free = sem("slots_free")
        turn = sem("turn")
        cache_in = sem("cache_in")
        dve_chain = sem("dve_chain")
        pool_chain = sem("pool_chain")
        act_chain = sem("act_chain")
        const_done = sem("const_done")
        cond_done = sem("cond_done")
        mod_done = sem("mod_done")
        mod_sb = sem("mod_sb")
        modT_done = sem("modT_done")
        modT_sb = sem("modT_sb")
        kv_ctx = sem("kv_ctx")
        kv_evac = sem("kv_evac")
        xT_done = sem("xT_done")
        hT_sb = sem("hT_sb")
        z_done = sem("z_done")
        gelu_done = sem("gelu_done")
        z_act = sem("z_act")
        z_dve = sem("z_dve")
        var_done = sem("var_done")
        rstd_done = sem("rstd_done")
        vn_done = sem("vn_done")
        mix_done = sem("mix_done")
        qkB_T = sem("qkB_T")
        qkB_sb = sem("qkB_sb")
        rope_done = sem("rope_done")
        qkD_T = sem("qkD_T")
        latent_n = sem("latent_n")
        latent_T = sem("latent_T")
        latent_sb = sem("latent_sb")
        up_done = sem("up_done")
        up_sb = sem("up_sb")
        qc_roped = sem("qc_roped")
        qcT_done = sem("qcT_done")
        spilled = sem("spilled")
        s_done = sem("s_done")
        biased = sem("biased")
        negmax = sem("negmax")
        exp_done = sem("exp_done")
        sink_done = sem("sink_done")
        prT_done = sem("prT_done")
        prT_sb = sem("prT_sb")
        pv_done = sem("pv_done")
        pv_used = sem("pv_used")
        on_done = sem("on_done")
        oT_done = sem("oT_done")
        oT_sb = sem("oT_sb")
        y_done = sem("y_done")
        xnew_done = sem("xnew_done")
        x2_done = sem("x2_done")
        q_done = sem("q_done")
        q_sb = sem("q_sb")
        sc_done = sem("sc_done")
        sc_sb = sem("sc_sb")
        cent_done = sem("cent_done")
        expf_done = sem("expf_done")
        route_done = sem("route_done")
        rows_used = sem("rows_used")
        ids_staged = sem("ids_staged")
        dots_done = sem("dots_done")
        gelu_sel = sem("gelu_sel")
        w_ready = sem("w_ready")
        acc_step = sem("acc_step")
        all_sems = range(sems[0].num, sems[-1].num + 1)
        assert [s.num for s in sems] == list(all_sems)
        bias_stored = es.enter_context(nc.semaphore("bias_stored"))
        gath = [es.enter_context(nc.semaphore(f"gathered{i}")) for i in range(16)]

        def end_step():
            nc.all_engine_barrier(sems_to_clear=all_sems)

        def chain(eng, s):
            n = [0]

            def link(ins):
                n[0] += 1
                ins.then_inc(s, 1)
                eng.wait_ge(s, n[0])
            return link

        def row(ap):
            return ap.broadcast_to([P, ap.shape[-1]])

        with nc.Block() as block:
            @block.sync
            def _(sp):
                sp.dma_start(ident[:, :], a["c_ident"]).then_inc(loaded, 16)
                sp.dma_start(natmask[:, :], a["c_natmask"]).then_inc(loaded, 16)
                sp.dma_start(band[:, :], a["c_band"]).then_inc(loaded, 16)
                sp.dma_start(iota16[:, :], a["c_iota"]).then_inc(loaded, 16)
                sp.dma_start(condT[:, :, :], a["condT"]).then_inc(loaded2, 16)
                sp.dma_start(x_dram, a["x0"]).then_inc(stored, 16)
                sp.wait_ge(loaded, 64)
                sp.wait_ge(stored, 16)

            @block.gpsimd
            def _(pool):
                for l in range(DEPTH):
                    for h in range(H):
                        for half in range(2):
                            first = ((l * H + h) * (2 * NA_KH - 1) + 1 - half) * RPB_ROW + RPB_PAD + NA_KW - 1
                            pool.dma_start(toep_dram[l, half * GRID_W:(half + 1) * GRID_W, h * NDR * GRID_W:(h + 1) * NDR * GRID_W]
                                           .rearrange("p (r c) -> r p c", c=GRID_W),
                                           bass.AP(a["rpb"].tensor, first, [[RPB_ROW, NDR], [-1, GRID_W], [1, GRID_W]])).then_inc(bias_stored, 16)
                pool.wait_ge(bias_stored, 16 * DEPTH * H * 2)

            @block.vector
            def _(dve):
                dve.memset(neg_half[:, :], -0.5)

            @block.scalar
            def _(act):
                act.wait_ge(loaded2, 16)
                act.activation(condS[:, :, :], condT[:, :, :], ACT.Silu)
        end_step()

        def step_modulation(L):
            ada = W[:, 0:3 * KD * ADA_COLS].rearrange("p (r k n) -> p r k n", r=3, k=KD)
            w_kv = W[:, 3 * KD * ADA_COLS:3 * KD * ADA_COLS + H * P].rearrange("p (h n) -> p h n", h=H)
            ckvT_c = W[:, 3 * KD * ADA_COLS + H * P:3 * KD * ADA_COLS + (H + 1) * P]
            CC = ADA_COLS // P
            with nc.Block() as block:
                @block.sync
                def _(sp):
                    with sp.Fori(0, ADA_PIECES // 3) as i:
                        for j in range(3):
                            sp.wait_ge(slots_free, i * 3 + (j + 1))
                            sp.dma_start(ada[:, j, :, :].rearrange("p k n -> p (k n)"),
                                         a["w_ada"][ds(L, 1), ds(i * 3 + j, 1), :, :]
                                         .rearrange("l c p n -> (l c p) n")).then_inc(piece_in[j], 16)
                    sp.wait_ge(modT_sb, 1)
                    for b in range(NBLK):
                        s = min(b, 1)
                        sp.dma_start(mod_dram[b, :, :], modT[s * MOD:(s + 1) * MOD, :]).then_inc(stored, 16)
                    sp.wait_ge(stored, 16 * NBLK)

                @block.scalar
                def _(act):
                    act.dma_start(b_ada[:, :], a["b_ada"][ds(L, 1), :, :].rearrange("l p n -> (l p) n")).then_inc(loaded, 16)
                    act.dma_start(w_kv, a["w_ukv"][ds(L, 1), :, :].rearrange("l p (h n) -> (l p) h n", h=H)).then_inc(loaded2, 16)
                    act.dma_start(ckvT_c, a["ckvT"][ds(L, 1), :, :].rearrange("l p n -> (l p) n")).then_inc(loaded2, 16)
                    c0, c1 = CTX * P, (CTX + 1) * P
                    act.dma_start(ktB[:, :, c0:c1], a["natkT"][ds(L, 1), :, :, :].rearrange("l p g n -> (l p) g n")).then_inc(cache_in, 16)
                    act.dma_start(vB[:, CTX, :], a["natv"][ds(L, 1), :, :].rearrange("l p n -> (l p) n")).then_inc(cache_in, 16)
                    act.dma_start(ktD[:, c0:c1], a["swakT"][ds(L, 1), :, :].rearrange("l p n -> (l p) n")).then_inc(cache_in, 16)
                    act.dma_start(vD[:, CTX, :], a["swav"][ds(L, 1), :, :].rearrange("l p n -> (l p) n")).then_inc(cache_in, 16)
                    act.dma_start(sinks[:, :], a["sinks"][ds(L, 1), :].broadcast_to([P, H])).then_inc(cache_in, 16)
                    act.dma_start(a_b[:, :], a["a_bT"][ds(L, 1), :, :].rearrange("l p n -> (l p) n")).then_inc(cache_in, 16)
                    for h in range(H):
                        act.dma_start(ktC[NOPE:CH, h, c0:c1], a["kropeT"][ds(L, 1), :, :].rearrange("l p n -> (l p) n")).then_inc(cache_in, 16)
                    act.dma_start(toep[:, :, :, :].rearrange("p h r c -> p (h r c)"), toep_dram[ds(L, 1), :, :].rearrange("l p n -> (l p) n")).then_inc(const_done, 16)
                    act.wait_ge(cache_in, 16 * (6 + H))

                @block.tensor
                def _(pe):
                    pe.sem_inc(slots_free, 3)
                    pe.wait_ge(loaded2, 32)
                    for h in range(H):
                        pe.matmul(bank(1, parts=NOPE)[:, h * P:(h + 1) * P], w_kv[:, h, 0:NOPE], ckvT_c, start=True, stop=True)
                    pe.matmul(bank(2, GW).rearrange("p (h n) -> p h n", h=H), ckvT_c, w_kv[:, :, NOPE:NOPE + VD],
                              start=True, stop=True).then_inc(kv_ctx, 1)
                    with pe.Fori(0, ADA_PIECES // 3) as i:
                        for j in range(3):
                            pe.wait_ge(piece_in[j], i * 16 + 16)
                            for c in range(CC):
                                for k in range(KD):
                                    last = pe.matmul(ps[:, ds(i * (3 * CC * 2) + (j * CC + c) * 2, 2)],
                                                     ada[:, j, k, c * P:(c + 1) * P], condS[:, k, :],
                                                     start=(k == 0), stop=(k == KD - 1))
                            last.then_inc(slots_free, 1)
                    pe.wait_ge(mod_sb, 1)
                    pe.transpose(bank(3, P, 2 * MOD), mod[:, :, :].rearrange("p s m -> p (s m)"), ident[:, :]).then_inc(modT_done, 1)

                @block.vector
                def _(dve):
                    link = chain(dve, dve_chain)
                    dve.wait_ge(kv_ctx, 1)
                    dve.tensor_copy(ktC[0:NOPE, :, CTX * P:(CTX + 1) * P],
                                    bank(1, parts=NOPE).rearrange("p (h n) -> p h n", h=H))
                    dve.tensor_copy(vC[:, CTX, :], bank(2, GW))
                    dve.wait_ge(const_done, 16)
                    for h in range(H):
                        dve.tensor_tensor(toep[:, h, :, :], toep[:, h, :, :],
                                          natmask[:, :].unsqueeze(1).broadcast_to([P, NDR, GRID_W]), ALU.add)
                    dve.wait_ge(slots_free, 3 + ADA_PIECES)
                    dve.wait_ge(loaded, 16)
                    for s in range(2):
                        link(dve.tensor_tensor(mod[:, s, :], ps[:, 0:2 * MOD].rearrange("p (m s) -> p s m", s=2)[:, s, :],
                                               b_ada[:, :], ALU.add))
                    for c in (KD, 4 * KD):
                        last = dve.tensor_scalar_add(mod[:, :, c:c + KD], mod[:, :, c:c + KD], 1.0)
                    last.then_inc(mod_sb, 1)
                    dve.wait_ge(mod_sb, 1)
                    for b in range(NBLK):
                        dve.tensor_copy(modb[:, b, :], mod[:, min(b, 1), 0:2 * KD])
                    dve.wait_ge(modT_done, 1)
                    dve.tensor_copy(modT[:, :], bank(3, P, 2 * MOD)).then_inc(modT_sb, 1)
            end_step()

        def step_load_in(L):
            with nc.Block() as block:
                @block.sync
                def _(sp):
                    def lay(dst, src):
                        sp.dma_start(dst, src).then_inc(loaded, 16)
                    lay(W[:, 0:W_IN], a["w_in"][ds(L, 1), :, :].rearrange("l p n -> (l p) n"))
                    lay(w_uq, a["w_uq"][ds(L, 1), :, :].rearrange("l p (k n) -> (l p) k n", k=2))
                    lay(w_ukv, a["w_ukv"][ds(L, 1), :, :].rearrange("l p (h n) -> (l p) h n", h=H))
                    lay(a_wT, a["a_wT"][ds(L, 1), :, :, :].rearrange("l p h n -> (l p) h n"))
                    lay(a_g, row(a["a_g"][ds(L, 1), :]))
                    lay(a_bb, row(a["a_bb"][ds(L, 1), :]))
                    lay(mq_g, row(a["mq_g"][ds(L, 1), :]))
                    lay(mkv_g, row(a["mkv_g"][ds(L, 1), :]))
                    lay(rope_t, a["c_rope"])
                    sp.wait_ge(loaded, 16 * 9)

                @block.vector
                def _(dve):
                    dve.memset(kr[:, 0:NOPE], 0.0)
            end_step()

        def step_input(L, b, context):
            slot = ds(b * P, P)
            with nc.Block() as block:
                @block.sync
                def _(sp):
                    sp.dma_start(xs[:, :], x_dram[ds(b, 1), :, :].rearrange("b p n -> (b p) n")).then_inc(loaded, 16)
                    n_out = 0
                    if context:
                        sp.wait_ge(z_act, 1)
                        sp.dma_start(a["o_nat_k"][0:1, ds(L, 1), :, :, :].rearrange("a l h t d -> (a l t) h d"),
                                     z[:, C_B + GW:C_B + 2 * GW].rearrange("p (h d) -> p h d", h=H)).then_inc(stored, 16)
                        sp.wait_ge(z_dve, 1)
                        sp.dma_start(a["o_nat_v"][0:1, ds(L, 1), :, :, :].rearrange("a l h t d -> (a l t) h d"),
                                     z[:, C_B + 2 * GW:C_B + 3 * GW].rearrange("p (h d) -> p h d", h=H)).then_inc(stored, 16)
                        sp.wait_ge(z_act, 2)
                        sp.dma_start(a["o_krope"][0:1, ds(L, 1), :, :].rearrange("a l t d -> (a l t) d"),
                                     z[:, C_C + QR + KVR:C_D]).then_inc(stored, 16)
                        sp.wait_ge(z_dve, 2)
                        sp.dma_start(a["o_swa_k"][0:1, ds(L, 1), :, :, :].rearrange("a l h t d -> (a l t) h d"),
                                     z[:, C_D + GW:C_D + GW + 2 * HD].rearrange("p (h d) -> p h d", h=2)).then_inc(stored, 16)
                        sp.dma_start(a["o_swa_v"][0:1, ds(L, 1), :, :, :].rearrange("a l h t d -> (a l t) h d"),
                                     z[:, C_D + GW + 2 * HD:IN_COLS].rearrange("p (h d) -> p h d", h=2)).then_inc(stored, 16)
                        sp.wait_ge(latent_n, 2)
                        sp.dma_start(a["o_ckv"][0:1, ds(L, 1), :, :].rearrange("a l t d -> (a l t) d"), ckvn).then_inc(stored, 16)
                        n_out = 6
                    sp.wait_ge(spilled, 4)
                    sp.dma_start(spill_dram[ds(b, 1), :, 0:SP_C].rearrange("b p n -> (b p) n"), spill[:, 0:SP_C]).then_inc(stored, 16)
                    sp.dma_start(spill_dram[ds(b, 1), 0:CH, SP_C:SP_COLS].rearrange("b p n -> (b p) n"), spill[0:CH, SP_C:SP_COLS]).then_inc(stored, 16)
                    sp.wait_ge(stored, 16 * (n_out + 2))

                @block.tensor
                def _(pe):
                    pe.wait_ge(loaded, 16)
                    for k in range(KD):
                        last = pe.transpose(ps[:, 5 * 512 + k * P:5 * 512 + (k + 1) * P], xs[:, k * P:(k + 1) * P], ident[:, :])
                    last.then_inc(xT_done, 1)
                    pe.wait_ge(hT_sb, 1)
                    for c in range(5):
                        n = min(512, IN_COLS - c * 512)
                        for k in range(KD):
                            last = pe.matmul(bank(c, n), hT[:, k, :], w_in[:, k, c * 512:c * 512 + n], start=(k == 0), stop=(k == KD - 1))
                        last.then_inc(z_done, 1)
                    pe.wait_ge(z_act, 1)
                    for g in range(4):
                        last = pe.transpose(bank(5)[:, g * P:(g + 1) * P], z[:, C_B + g * P:C_B + (g + 1) * P], ident[:, :])
                    last.then_inc(qkB_T, 1)
                    pe.wait_ge(vn_done, 1)
                    for h in range(H):
                        last = pe.matmul(bank(7, GW)[:, h * HD:(h + 1) * HD], a_wT[:, h, :], vn[:, h * HD:(h + 1) * HD], start=True, stop=True)
                    last.then_inc(mix_done, 1)
                    pe.wait_ge(latent_n, 2)
                    pe.wait_ge(rope_done, 1)
                    for k in range(2):
                        pe.transpose(bank(0)[:, k * P:(k + 1) * P], cqn[:, k * P:(k + 1) * P], ident[:, :])
                    pe.transpose(bank(0)[:, 2 * P:3 * P], ckvn, ident[:, :])
                    pe.transpose(bank(0, parts=CH)[:, 3 * P:4 * P], kr, ident[:, :]).then_inc(latent_T, 1)
                    pe.wait_ge(latent_sb, 1)
                    pe.wait_ge(z_act, 2)
                    pe.wait_ge(z_dve, 2)
                    for k in range(2):
                        pe.matmul(bank(1, H * CH), cqT[:, k, :], w_uq[:, k, :], start=(k == 0), stop=(k == 1))
                    for h in range(H):
                        pe.matmul(bank(2, parts=NOPE)[:, h * P:(h + 1) * P], w_ukv[:, h, 0:NOPE], ckvT, start=True, stop=True)
                    pe.matmul(bank(3, GW).rearrange("p (h n) -> p h n", h=H), ckvT, w_ukv[:, :, NOPE:NOPE + VD],
                              start=True, stop=True).then_inc(up_done, 1)
                    pe.wait_ge(rope_done, 2)
                    for g in range(3):
                        last = pe.transpose(bank(6)[:, g * P:(g + 1) * P], zr[:, g * P:(g + 1) * P], ident[:, :])
                    last.then_inc(qkD_T, 1)
                    pe.wait_ge(qc_roped, 1)
                    for h in range(H):
                        last = pe.transpose(bank(4, parts=CH)[:, h * P:(h + 1) * P], qc[:, h * CH:(h + 1) * CH], ident[:, :])
                    last.then_inc(qcT_done, 1)

                @block.scalar
                def _(act):
                    act.wait_ge(z_done, 1)
                    act.activation(gz, bank(0), ACT.Gelu_apprx_tanh).then_inc(gelu_done, 1)
                    act.wait_ge(z_done, 2)
                    act.copy(z[:, 512:1024], bank(1)).then_inc(z_act, 1)
                    act.wait_ge(z_done, 4)
                    act.copy(z[:, 1536:2048], bank(3)).then_inc(z_act, 1)
                    act.wait_ge(qkB_T, 1)
                    act.copy(spill[:, SP_B:SP_B + 2 * P], bank(5)[:, 0:2 * P])
                    act.copy(ktB[:, :, slot], bank(5)[:, 2 * P:4 * P].rearrange("p (g n) -> p g n", g=2)).then_inc(spilled, 1)
                    act.wait_ge(up_done, 1)
                    act.copy(ktC[0:NOPE, :, slot], bank(2, parts=NOPE).rearrange("p (h n) -> p h n", h=H))
                    act.copy(vC[:, ds(b, 1), :], bank(3, GW).unsqueeze(1))
                    act.wait_ge(qkD_T, 1)
                    act.copy(spill[:, SP_D:SP_D + 2 * P], bank(6)[:, 0:2 * P])
                    act.copy(ktD[:, slot], bank(6)[:, 2 * P:3 * P]).then_inc(spilled, 1)
                    act.wait_ge(qcT_done, 1)
                    act.copy(spill[0:CH, SP_C:SP_COLS], bank(4, parts=CH)).then_inc(spilled, 1)

                @block.gpsimd
                def _(pool):
                    link = chain(pool, pool_chain)

                    def rope(out, src, nh, stride, half, first, tabs):
                        w = 2 * half
                        s4 = src.rearrange("p (h n) -> p h n", h=nh)
                        o4 = out.rearrange("p (h n) -> p h n", h=nh)
                        t4 = ropeA[:, 0:nh * w].rearrange("p (h n) -> p h n", h=nh)
                        u4 = ropeB[:, 0:nh * w].rearrange("p (h n) -> p h n", h=nh)
                        cos = rope_t[:, ds(b, 1), tabs:tabs + w].broadcast_to([P, nh, w])
                        sin = rope_t[:, ds(b, 1), tabs + w:tabs + 2 * w]
                        pool.tensor_tensor(u4, s4[:, :, first:first + w], cos, ALU.mult)
                        pool.tensor_tensor(t4[:, :, 0:half], s4[:, :, first + half:first + w],
                                           sin[:, :, 0:half].broadcast_to([P, nh, half]), ALU.mult)
                        link(pool.tensor_tensor(t4[:, :, half:w], s4[:, :, first:first + half],
                                                sin[:, :, half:w].broadcast_to([P, nh, half]), ALU.mult))
                        return pool.tensor_tensor(o4[:, :, first:first + w], u4, t4, ALU.add)

                    pool.wait_ge(var_done, 1)
                    pool.tensor_tensor(rstd[:, 0:1], ve[:, 0:1], neg_half[:, 0:1], ALU.pow).then_inc(rstd_done, 1)
                    pool.wait_ge(var_done, 2)
                    pool.tensor_tensor(rstd[:, 1:3], ve[:, 1:3], neg_half[:, 0:2], ALU.pow).then_inc(rstd_done, 1)
                    pool.wait_ge(z_act, 2)
                    rope(kr[:, NOPE:CH], z[:, C_C + QR + KVR:C_D], 1, CH, ROPE // 2, 0, 0).then_inc(rope_done, 1)
                    pool.wait_ge(rope_done, 1)
                    pool.wait_ge(z_dve, 2)
                    rope(zr, z[:, C_D:C_D + 6 * HD], 6, HD, HD // 2, 0, 2 * ROPE).then_inc(rope_done, 1)
                    pool.wait_ge(rope_done, 2)
                    pool.wait_ge(up_sb, 1)
                    rope(qc, qc, H, CH, ROPE // 2, NOPE, 0).then_inc(qc_roped, 1)

                @block.vector
                def _(dve):
                    link = chain(dve, dve_chain)
                    dve.wait_ge(xT_done, 1)
                    for k in range(KD):
                        last = dve.tensor_scalar(hT[:, k, :], ps[:, 5 * 512 + k * P:5 * 512 + (k + 1) * P],
                                                 modb[:, ds(b, 1), KD + k:KD + k + 1].rearrange("p b n -> p (b n)"),
                                                 modb[:, ds(b, 1), k:k + 1].rearrange("p b n -> p (b n)"), ALU.mult, ALU.add)
                    last.then_inc(hT_sb, 1)
                    dve.wait_ge(gelu_done, 1)
                    link(dve.bn_stats(st12[:, 0, :], gz[:, GW:2 * GW]))
                    link(dve.bn_aggr(mv[:, :], st12[:, 0, :]))
                    dve.tensor_scalar_add(ve[:, 0:1], mv[:, 1:2], EPS).then_inc(var_done, 1)
                    dve.wait_ge(rstd_done, 1)
                    link(dve.tensor_scalar(vn, gz[:, GW:2 * GW], mv[:, 0:1], rstd[:, 0:1], ALU.subtract, ALU.mult))
                    link(dve.tensor_tensor(vn, vn, a_g, ALU.mult))
                    dve.tensor_tensor(vn, vn, a_bb, ALU.add).then_inc(vn_done, 1)
                    dve.wait_ge(z_done, 3)
                    link(dve.tensor_copy(z[:, 1024:1536], bank(2)))
                    dve.sem_inc(z_dve, 1)
                    dve.wait_ge(z_done, 5)
                    dve.tensor_copy(z[:, 2048:IN_COLS], bank(4, IN_COLS - 2048)).then_inc(z_dve, 1)
                    dve.tensor_copy(vB[:, ds(b, 1), :], z[:, C_B + 2 * GW:C_B + 3 * GW].unsqueeze(1))
                    dve.wait_ge(z_act, 2)
                    link(dve.tensor_tensor_reduce(out=cqn, in0=z[:, C_C:C_C + QR], in1=z[:, C_C:C_C + QR], scale=1.0, scalar=0.0,
                                                  op0=ALU.mult, op1=ALU.add, accum_out=small[:, 1:2]))
                    link(dve.tensor_tensor_reduce(out=ckvn, in0=z[:, C_C + QR:C_C + QR + KVR], in1=z[:, C_C + QR:C_C + QR + KVR],
                                                  scale=1.0, scalar=0.0, op0=ALU.mult, op1=ALU.add, accum_out=small[:, 2:3]))
                    dve.tensor_scalar(ve[:, 1:2], small[:, 1:2], 1.0 / QR, EPS, ALU.mult, ALU.add)
                    dve.tensor_scalar(ve[:, 2:3], small[:, 2:3], 1.0 / KVR, EPS, ALU.mult, ALU.add).then_inc(var_done, 1)
                    dve.wait_ge(rstd_done, 2)
                    dve.scalar_tensor_tensor(cqn, z[:, C_C:C_C + QR], rstd[:, 1:2], mq_g, ALU.mult, ALU.mult).then_inc(latent_n, 1)
                    dve.scalar_tensor_tensor(ckvn, z[:, C_C + QR:C_C + QR + KVR], rstd[:, 2:3], mkv_g, ALU.mult, ALU.mult).then_inc(latent_n, 1)
                    dve.wait_ge(mix_done, 1)
                    for h in range(H):
                        last = dve.scalar_tensor_tensor(spill[:, SP_A + h * HD:SP_A + (h + 1) * HD], bank(7, GW)[:, h * HD:(h + 1) * HD],
                                                        a_b[:, h:h + 1], gz[:, h * HD:(h + 1) * HD], ALU.add, ALU.mult)
                    last.then_inc(spilled, 1)
                    dve.wait_ge(latent_T, 1)
                    dve.tensor_copy(cqT, bank(0)[:, 0:2 * P].rearrange("p (k n) -> p k n", k=2))
                    dve.tensor_copy(ckvT, bank(0)[:, 2 * P:3 * P])
                    dve.tensor_copy(ktC[NOPE:CH, :, slot], bank(0)[NOPE:CH, 3 * P:4 * P].unsqueeze(1).broadcast_to([ROPE, H, P])).then_inc(latent_sb, 1)
                    dve.wait_ge(z_dve, 2)
                    dve.tensor_copy(vD[:, ds(b, 1), :], z[:, C_D + GW + 2 * HD:IN_COLS].unsqueeze(1))
                    dve.wait_ge(up_done, 1)
                    dve.tensor_copy(qc, bank(1, H * CH)).then_inc(up_sb, 1)
            end_step()

        def layer_norm(dve, link, x, g, b_, tmp_done, pow_done, out):
            for i in range(2):
                link(dve.bn_stats(st12[:, i, :], x[:, i * 512:(i + 1) * 512]))
            link(dve.bn_aggr(mv[:, :], st12[:, :, :].rearrange("p a n -> p (a n)")))
            dve.tensor_scalar_add(ve[:, 0:1], mv[:, 1:2], EPS).then_inc(tmp_done[0], 1)
            dve.wait_ge(pow_done[0], pow_done[1])
            link(dve.tensor_scalar(x, x, mv[:, 0:1], rstd[:, 0:1], ALU.subtract, ALU.mult))
            link(dve.tensor_tensor(x, x, g, ALU.mult))
            return dve.tensor_tensor(out, x, b_, ALU.add)

        def step_load_out(L):
            with nc.Block() as block:
                @block.sync
                def _(sp):
                    sp.dma_start(W[:, 0:KD * D], a["w_out"][ds(L, 1), :, :].rearrange("l p n -> (l p) n")).then_inc(loaded, 16)
                    sp.dma_start(og_bc, row(a["out_g"][ds(L, 1), :])).then_inc(loaded, 16)
                    sp.dma_start(bc[:, 1, :], row(a["ln1_g"][ds(L, 1), :])).then_inc(loaded, 16)
                    sp.dma_start(bc[:, 2, :], row(a["ln1_b"][ds(L, 1), :])).then_inc(loaded, 16)
                    sp.wait_ge(loaded, 64)
            end_step()

        def step_attention(L, b, context):
            nk = 1 if context else NLAT + 1
            k0 = 0 if context else 1
            NH = 3 * H
            lat = NLAT * P

            def operands(i):
                g, h = divmod(i, H)
                if g == 1:
                    return qTC[:, h * P:(h + 1) * P], ktC[:, h, :]
                if g == 0:
                    r = slice((h % 2) * HD, (h % 2 + 1) * HD)
                    return qT[r, SP_B + (h // 2) * P:SP_B + (h // 2 + 1) * P], ktB[r, h // 2, :]
                r = slice((h // 2) * HD, (h // 2 + 1) * HD)
                return qT[r, SP_D + (h % 2) * P:SP_D + (h % 2 + 1) * P], ktD[r, :]

            def values(i, s):
                g, h = divmod(i, H)
                if g == 2:
                    return vD[:, s, (h // 2) * HD:(h // 2 + 1) * HD]
                return (vB, vC)[g][:, s, h * HD:(h + 1) * HD]

            with nc.Block() as block:
                @block.sync
                def _(sp):
                    def lay(dst, src, s):
                        sp.dma_start(dst, src).then_inc(s, 16)
                    lay(qT, spill_dram[ds(b, 1), :, 0:SP_A].rearrange("b p n -> (b p) n"), loaded)
                    lay(qTC, spill_dram[ds(b, 1), 0:CH, SP_C:SP_COLS].rearrange("b p n -> (b p) n"), loaded)
                    lay(ob[:, 0:GW], spill_dram[ds(b, 1), :, SP_A:SP_C].rearrange("b p n -> (b p) n"), loaded2)
                    lay(xs[:, :], x_dram[ds(b, 1), :, :].rearrange("b p n -> (b p) n"), loaded2)
                    for dst, m in ((bc[:, 0, :], 2), (sh2_bc, 3), (sc2_bc, 4)):
                        lay(dst, mod_dram[ds(b, 1), m * KD:(m + 1) * KD, :].rearrange("b c n -> b (c n)").broadcast_to([P, D]), loaded2)
                    sp.wait_ge(xnew_done, 1)
                    sp.dma_start(x_dram[ds(b, 1), :, :].rearrange("b p n -> (b p) n"), xs[:, :]).then_inc(stored, 16)
                    sp.wait_ge(x2_done, 1)
                    sp.dma_start(x2_dram[ds(b, 1), :, :].rearrange("b p n -> (b p) n"), ob[:, :]).then_inc(stored, 16)
                    sp.wait_ge(stored, 32)

                @block.tensor
                def _(pe):
                    def score(i):
                        q, k = operands(i)
                        if i >= 2:
                            pe.wait_ge(exp_done, i - 1)
                        o = (i % 2) * 1024
                        if nk > 1:
                            pe.matmul(ps[:, o:o + lat], q, k[:, k0 * P:k0 * P + lat], start=True, stop=True)
                            pe.matmul(ps[:, o + lat:o + lat + P], q, k[:, CTX * P:(CTX + 1) * P], start=True, stop=True).then_inc(s_done, 1)
                        else:
                            pe.matmul(ps[:, o:o + P], q, k[:, 0:P], start=True, stop=True).then_inc(s_done, 1)
                    pe.wait_ge(loaded, 32)
                    score(0)
                    for i in range(NH):
                        if i + 1 < NH:
                            score(i + 1)
                        pe.wait_ge(exp_done, i + 1)
                        if i >= 1:
                            pe.wait_ge(prT_sb, i)
                        for s in range(nk):
                            last = pe.transpose(ps[:, 2048 + s * P:2048 + (s + 1) * P], pr[:, i % 2, s * P:(s + 1) * P], ident[:, :])
                        last.then_inc(prT_done, 1)
                        pe.wait_ge(prT_sb, i + 1)
                        if i >= 2:
                            pe.wait_ge(pv_used, i - 1)
                        for s in range(nk):
                            last = pe.matmul(bank(6 + i % 2, HD), prT[:, i % 2, s * P:(s + 1) * P], values(i, k0 + s),
                                             start=(s == 0), stop=(s == nk - 1))
                        last.then_inc(pv_done, 1)
                    pe.wait_ge(on_done, 1)
                    for k in range(KD):
                        last = pe.transpose(ps[:, k * P:(k + 1) * P], ob[:, k * P:(k + 1) * P], ident[:, :])
                    last.then_inc(oT_done, 1)
                    pe.wait_ge(oT_sb, 1)
                    for c in range(2):
                        for k in range(KD):
                            last = pe.matmul(bank(2 + c), hT[:, k, :], w_out[:, k, c * 512:(c + 1) * 512], start=(k == 0), stop=(k == KD - 1))
                    last.then_inc(y_done, 1)

                @block.scalar
                def _(act):
                    for i in range(NH):
                        g, h = divmod(i, H)
                        o = (i % 2) * 1024
                        plain = nk == 1 or g == 1
                        src = ps[:, o:o + nk * P] if plain else sS[:, i % 2, :]
                        sc = (MLA_SCALE if g == 1 else SCALE) if plain else 1.0
                        act.wait_ge(negmax, i + 1)
                        if i >= 2:
                            act.wait_ge(prT_done, i - 1)
                        if g == 2:
                            act.activation(small[:, 32 + h:33 + h], sinks[:, h:h + 1], ACT.Exp, bias=small[:, 16 + i:17 + i]).then_inc(sink_done, 1)
                        act.activation(pr[:, i % 2, 0:nk * P], src, ACT.Exp, bias=small[:, 16 + i:17 + i], scale=sc,
                                       accum_out=small[:, 36 + i:37 + i]).then_inc(exp_done, 1)
                        act.wait_ge(prT_done, i + 1)
                        if i >= 2:
                            act.wait_ge(pv_done, i - 1)
                        act.copy(prT[:, i % 2, 0:nk * P], ps[:, 2048:2048 + nk * P]).then_inc(prT_sb, 1)

                @block.gpsimd
                def _(pool):
                    pool.wait_ge(var_done, 1)
                    pool.tensor_tensor(rstd[:, :], ve[:, :], neg_half[:, :], ALU.pow).then_inc(rstd_done, 1)
                    pool.wait_ge(var_done, 2)
                    pool.tensor_tensor(rstd[:, 0:1], ve[:, 0:1], neg_half[:, 0:1], ALU.pow).then_inc(rstd_done, 1)

                @block.vector
                def _(dve):
                    link = chain(dve, dve_chain)

                    def negate_max(i):
                        g, h = divmod(i, H)
                        o = (i % 2) * 1024
                        mx, nm = small[:, i:i + 1], small[:, 16 + i:17 + i]
                        dve.wait_ge(s_done, i + 1)
                        plain = nk == 1 or g == 1
                        sc = MLA_SCALE if g == 1 else SCALE
                        if not plain:
                            if i >= 2:
                                dve.wait_ge(exp_done, i - 1)
                            if g == 0:
                                bias = toep[:, h, ds(2 * NLAT - 2 * b, ROWS), :].rearrange("p r c -> p (r c)")
                            else:
                                bias = band[:, ds(NLAT * P - b * P, lat)]
                            dve.scalar_tensor_tensor(sS[:, i % 2, 0:lat], ps[:, o:o + lat], sc, bias, ALU.mult, ALU.add)
                            link(dve.tensor_scalar_mul(sS[:, i % 2, lat:lat + P], ps[:, o + lat:o + lat + P], sc))
                            link(dve.reduce_max(mx, sS[:, i % 2, :], AX))
                            sc = 1.0
                        else:
                            link(dve.reduce_max(mx, ps[:, o:o + nk * P], AX))
                        if g == 2:
                            link(dve.tensor_scalar(mx, mx, sc, sinks[:, h:h + 1], ALU.mult, ALU.max))
                            sc = 1.0
                        dve.tensor_scalar_mul(nm, mx, -sc).then_inc(negmax, 1)

                    def finish(i):
                        g, h = divmod(i, H)
                        l = small[:, 36 + i:37 + i]
                        dve.wait_ge(exp_done, i + 1)
                        if g == 2:
                            dve.wait_ge(sink_done, h + 1)
                            link(dve.tensor_tensor(l, l, small[:, 32 + h:33 + h], ALU.add))
                        link(dve.reciprocal(small[:, 48 + i:49 + i], l))
                        dve.wait_ge(pv_done, i + 1)
                        dve.tensor_scalar_mul(ob[:, GW + i * HD:GW + (i + 1) * HD], bank(6 + i % 2, HD), small[:, 48 + i:49 + i]).then_inc(pv_used, 1)

                    negate_max(0)
                    for i in range(NH):
                        if i + 1 < NH:
                            negate_max(i + 1)
                        finish(i)
                    dve.wait_ge(pv_used, NH)
                    dve.wait_ge(loaded2, 16 * 5)
                    for g in range(4):
                        o = ob[:, g * GW:(g + 1) * GW]
                        dve.tensor_tensor_reduce(out=xa[:, g * GW:(g + 1) * GW], in0=o, in1=o, scale=1.0, scalar=0.0,
                                                 op0=ALU.mult, op1=ALU.add, accum_out=small[:, g:g + 1])
                    link(dve.engine_nop())
                    dve.tensor_scalar(ve[:, :], small[:, 0:4], 1.0 / GW, EPS, ALU.mult, ALU.add).then_inc(var_done, 1)
                    dve.wait_ge(rstd_done, 1)
                    for g in range(4):
                        o = ob[:, g * GW:(g + 1) * GW]
                        last = dve.scalar_tensor_tensor(o, o, rstd[:, g:g + 1], og_bc[:, g * GW:(g + 1) * GW], ALU.mult, ALU.mult)
                    last.then_inc(on_done, 1)
                    dve.wait_ge(oT_done, 1)
                    dve.tensor_copy(hT[:, :, :].rearrange("p k n -> p (k n)"), ps[:, 0:KD * P]).then_inc(oT_sb, 1)
                    dve.wait_ge(y_done, 1)
                    link(dve.tensor_tensor(xa[:, :], ps[:, 2 * 512:4 * 512], bc[:, 0, :], ALU.mult))
                    link(dve.scalar_tensor_tensor(xa[:, :], xs[:, :], ALPHA, xa[:, :], ALU.mult, ALU.add))
                    layer_norm(dve, link, xa[:, :], bc[:, 1, :], bc[:, 2, :], [var_done], [rstd_done, 2], xs[:, :]).then_inc(xnew_done, 1)
                    dve.wait_ge(xnew_done, 1)
                    link(dve.tensor_tensor(ob[:, :], xs[:, :], sc2_bc, ALU.mult))
                    dve.tensor_tensor(ob[:, :], ob[:, :], sh2_bc, ALU.add).then_inc(x2_done, 1)
            end_step()

        def step_load_route(L):
            with nc.Block() as block:
                @block.sync
                def _(sp):
                    sp.dma_start(W[:, 0:KD * RC], a["w_q"][ds(L, 1), :, :].rearrange("l p n -> (l p) n")).then_inc(loaded, 16)
                    sp.dma_start(skT, a["skT"][ds(L, 1), :, :, :].rearrange("l p s n -> (l p) s n")).then_inc(loaded, 16)
                    sp.dma_start(first_row[:, :], a["c_first"][ds(L, 1), :].broadcast_to([P, 1])).then_inc(loaded, 16)
                    sp.wait_ge(loaded, 48)
            end_step()

        def step_route(L, b):
            G = 2 * PH
            with nc.Block() as block:
                @block.sync
                def _(sp):
                    sp.dma_start(xs[:, :], x2_dram[ds(b, 1), :, :].rearrange("b p n -> (b p) n")).then_inc(loaded, 16)
                    sp.wait_ge(route_done, 2)
                    sp.dma_start(eid_dram[ds(b, 1), :, :].rearrange("b p n -> (b p) n"), eid[:, :]).then_inc(stored, 16)
                    sp.dma_start(gate_dram[ds(b, 1), :, :].rearrange("b p n -> (b p) n"), gates[:, :]).then_inc(stored, 16)
                    sp.wait_ge(stored, 32)

                @block.tensor
                def _(pe):
                    pe.wait_ge(loaded, 16)
                    for k in range(KD):
                        last = pe.transpose(ps[:, k * P:(k + 1) * P], xs[:, k * P:(k + 1) * P], ident[:, :])
                    last.then_inc(xT_done, 1)
                    pe.wait_ge(hT_sb, 1)
                    for g in range(G):
                        for k in range(KD):
                            last = pe.matmul(ps[:, 1024 + g * P:1024 + (g + 1) * P], w_q[:, k, g * P:(g + 1) * P], hT[:, k, :],
                                             start=(k == 0), stop=(k == KD - 1))
                        if g % 4 == 3:
                            last.then_inc(q_done, 1)
                    for g in range(G):
                        if g % 4 == 0:
                            pe.wait_ge(q_sb, g // 4 + 1)
                            if g >= 8:
                                pe.wait_ge(sc_sb, g // 4 - 1)
                        last = pe.matmul(ps[:, (g % 8) * P:(g % 8 + 1) * P], qsel[:, g, :], skT[:, g % 2, :], start=True, stop=True)
                        if g % 4 == 3:
                            last.then_inc(sc_done, 1)

                @block.scalar
                def _(act):
                    for c in range(4):
                        act.wait_ge(q_done, c + 1)
                        act.copy(qsel[:, 4 * c:4 * c + 4, :], ps[:, 1024 + c * 512:1024 + (c + 1) * 512].rearrange("p (g t) -> p g t", t=P)).then_inc(q_sb, 1)
                    for c in range(4):
                        act.wait_ge(sc_done, c + 1)
                        act.copy(scores[:, 4 * c:4 * c + 4, :], ps[:, (c % 2) * 512:(c % 2 + 1) * 512].rearrange("p (g n) -> p g n", n=PK)).then_inc(sc_sb, 1)
                    act.wait_ge(cent_done, 1)
                    act.activation(fe, fe, ACT.Exp).then_inc(expf_done, 1)

                @block.vector
                def _(dve):
                    link = chain(dve, dve_chain)
                    dve.wait_ge(xT_done, 1)
                    dve.tensor_copy(hT[:, :, :].rearrange("p k n -> p (k n)"), ps[:, 0:KD * P]).then_inc(hT_sb, 1)

                    def top16(vals, idx, src, src2, n):
                        for g in range(n):
                            last = dve.max(vals[:, g, 0:8], src[:, g, :])
                        link(last)
                        for g in range(n):
                            dve.max_index(idx[:, g, 0:8], vals[:, g, 0:8], src[:, g, :])
                            last = dve.match_replace(src2[:, g, :], vals[:, g, 0:8], src[:, g, :], -3e38)
                        link(last)
                        for g in range(n):
                            last = dve.max(vals[:, g, 8:16], src2[:, g, :])
                        link(last)
                        for g in range(n):
                            last = dve.max_index(idx[:, g, 8:16], vals[:, g, 8:16], src2[:, g, :])
                        link(last)

                    dve.wait_ge(sc_sb, 4)
                    top16(sv, si, scores, scores2, G)
                    dve.tensor_copy(sif, si)
                    sv2 = sv.rearrange("p (h s) k -> p h s k", s=2)
                    link(dve.tensor_tensor(cand.rearrange("p h (i j) -> p h i j", i=TOPK),
                                           sv2[:, :, 0, :].unsqueeze(3).broadcast_to([P, PH, TOPK, TOPK]),
                                           sv2[:, :, 1, :].unsqueeze(2).broadcast_to([P, PH, TOPK, TOPK]), ALU.add))
                    top16(fv, fi, cand, cand2, PH)
                    dve.tensor_tensor(fe, fv, fv[:, :, 0:1].broadcast_to([P, PH, TOPK]), ALU.subtract).then_inc(cent_done, 1)
                    fis = fi.rearrange("p h k -> p (h k)")
                    dve.tensor_scalar(fpart[:, 0, :], fis, 4, None, ALU.logical_shift_right)
                    link(dve.tensor_scalar(fpart[:, 1, :], fis, TOPK - 1, None, ALU.bitwise_and))
                    sif2 = sif.rearrange("p (h s) k -> p h s k", s=2)
                    oh4 = onehot.rearrange("p (h k) j -> p h k j", h=PH)
                    for s in range(2):
                        link(dve.tensor_tensor(onehot, fpart[:, s, :].unsqueeze(2).broadcast_to([P, NSEL, TOPK]),
                                               iota16[:, :].unsqueeze(1).broadcast_to([P, NSEL, TOPK]), ALU.is_equal))
                        link(dve.tensor_tensor(oh4, oh4, sif2[:, :, s, :].unsqueeze(2).broadcast_to([P, PH, TOPK, TOPK]), ALU.mult))
                        link(dve.reduce_sum(id_rc[:, s, :], onehot, AX))
                    link(dve.scalar_tensor_tensor(eidf, id_rc[:, 0, :], float(PK), id_rc[:, 1, :], ALU.mult, ALU.add))
                    dve.tensor_scalar(eid[:, :], eidf, first_row[:, 0:1], None, ALU.add).then_inc(route_done, 1)
                    dve.wait_ge(expf_done, 1)
                    link(dve.reduce_sum(small[:, 0:PH], fe, AX))
                    link(dve.reciprocal(small[:, 8:8 + PH], small[:, 0:PH]))
                    dve.tensor_tensor(gates[:, :].rearrange("p (h k) -> p h k", h=PH), fe,
                                      small[:, 8:8 + PH].unsqueeze(2).broadcast_to([P, PH, TOPK]), ALU.mult).then_inc(route_done, 1)
            end_step()

        def step_experts(L, b):
            HEADS_PER_TURN = 2
            TURNS = PH // HEADS_PER_TURN
            ROWS_PER_TURN = HEADS_PER_TURN * 2 * TOPK
            GRP = 4
            slots = 16
            assert slots <= RING and ROWS_PER_TURN % slots == 0
            per_turn = ROWS_PER_TURN // slots
            with nc.Block() as block:
                @block.sync
                def _(sp):
                    sp.dma_start(eid[:, :], eid_dram[ds(b, 1), :, :].rearrange("b p n -> (b p) n")).then_inc(loaded, 16)
                    sp.dma_start(gates[:, :], gate_dram[ds(b, 1), :, :].rearrange("b p n -> (b p) n")).then_inc(loaded2, 16)
                    sp.dma_start(xs[:, :], x2_dram[ds(b, 1), :, :].rearrange("b p n -> (b p) n")).then_inc(loaded2, 16)
                    sp.dma_start(xa[:, :], x_dram[ds(b, 1), :, :].rearrange("b p n -> (b p) n")).then_inc(loaded2, 16)
                    sp.dma_start(bc[:, 0, :], mod_dram[ds(b, 1), 5 * KD:6 * KD, :].rearrange("b c n -> b (c n)").broadcast_to([P, D])).then_inc(loaded2, 16)
                    sp.dma_start(bc[:, 1, :], row(a["ln2_g"][ds(L, 1), :])).then_inc(loaded2, 16)
                    sp.dma_start(bc[:, 2, :], row(a["ln2_b"][ds(L, 1), :])).then_inc(loaded2, 16)
                    sp.wait_ge(xnew_done, 1)
                    sp.dma_start(x_dram[ds(b, 1), :, :].rearrange("b p n -> (b p) n"), xa[:, :]).then_inc(stored, 16)
                    sp.wait_ge(stored, 16)

                @block.gpsimd
                def _(pool):
                    pool.wait_ge(loaded, 16)
                    with pool.Fori(0, TURNS) as t:
                        for hh in range(HEADS_PER_TURN):
                            for j in range(2 * TOPK):
                                n = hh * 2 * TOPK + j
                                if j == 0:
                                    pool.wait_ge(slots_free, t * ROWS_PER_TURN + (n + GRP))
                                    pool.wait_ge(loaded, 16)
                                    pool.tensor_copy(eid_s[:, hh, :], eid[:, ds(t * (HEADS_PER_TURN * TOPK) + hh * TOPK, TOPK)]).then_inc(ids_staged, 1)
                                    pool.wait_ge(ids_staged, t * HEADS_PER_TURN + (hh + 1))
                                    pool.sem_inc(turn, 1)
                                elif j % GRP == 0:
                                    pool.wait_ge(slots_free, t * ROWS_PER_TURN + (n + GRP))
                                    pool.sem_inc(turn, 1)
                                table = a["peer_u"] if j < TOPK else a["peer_v"]
                                pool.indirect_dma_start(
                                    ring[:, n % slots, :], None, table,
                                    bass.IndirectOffsetOnAxis(ap=eid_s[:, hh, j % TOPK:j % TOPK + 1], axis=0),
                                ).then_inc(gath[n % slots], 16)
                    pool.wait_ge(var_done, 1)
                    pool.tensor_tensor(rstd[:, 0:1], ve[:, 0:1], neg_half[:, 0:1], ALU.pow).then_inc(rstd_done, 1)

                @block.scalar
                def _(act):
                    with act.Fori(0, TURNS) as t:
                        for hh in range(HEADS_PER_TURN):
                            act.wait_ge(dots_done, t * HEADS_PER_TURN + (hh + 1))
                            act.activation(gel[:, hh, :], dots[:, hh, :], ACT.Gelu_apprx_tanh).then_inc(gelu_sel, 1)

                @block.vector
                def _(dve):
                    link = chain(dve, dve_chain)
                    dve.sem_inc(slots_free, slots)
                    dve.memset(accs[:, 0, :], 0.0)
                    dve.memset(accs[:, 1, :], 0.0).then_inc(acc_step, 2)
                    dve.wait_ge(loaded2, 16 * 6)
                    with dve.Fori(0, TURNS) as t:
                        for hh in range(HEADS_PER_TURN):
                            for j in range(TOPK):
                                n = hh * 2 * TOPK + j
                                dve.wait_ge(gath[n % slots], L * (NBLK * TURNS * per_turn * 16) + b * (TURNS * per_turn * 16) + t * (per_turn * 16) + (n // slots + 1) * 16)
                                dve.wait_ge(slots_free, t * ROWS_PER_TURN + (slots + n - 1))
                                ins = dve.tensor_tensor_reduce(out=junk[:, j % 2, :], in0=ring[:, n % slots, :], in1=xs[:, :], scale=1.0, scalar=0.0,
                                                               op0=ALU.mult, op1=ALU.add, accum_out=dots[:, hh, j:j + 1])
                                ins.then_inc(slots_free, 1)
                            dve.wait_ge(slots_free, t * ROWS_PER_TURN + (slots + hh * 2 * TOPK + TOPK))
                            dve.sem_inc(dots_done, 1)
                            dve.wait_ge(gelu_sel, t * HEADS_PER_TURN + (hh + 1))
                            dve.tensor_tensor(wsel[:, hh, :], gel[:, hh, :], gates[:, ds(t * (HEADS_PER_TURN * TOPK) + hh * TOPK, TOPK)], ALU.mult).then_inc(w_ready, 1)
                            dve.wait_ge(w_ready, t * HEADS_PER_TURN + (hh + 1))
                            for j in range(TOPK):
                                n = hh * 2 * TOPK + TOPK + j
                                dve.wait_ge(gath[n % slots], L * (NBLK * TURNS * per_turn * 16) + b * (TURNS * per_turn * 16) + t * (per_turn * 16) + (n // slots + 1) * 16)
                                dve.wait_ge(slots_free, t * ROWS_PER_TURN + (slots + n - 1))
                                dve.scalar_tensor_tensor(accs[:, j % 2, :], ring[:, n % slots, :], wsel[:, hh, j:j + 1], accs[:, j % 2, :],
                                                         ALU.mult, ALU.add).then_inc(slots_free, 1)
                    dve.wait_ge(slots_free, slots + TURNS * ROWS_PER_TURN)
                    ac = accs[:, 0, :]
                    link(dve.tensor_tensor(ac, ac, accs[:, 1, :], ALU.add))
                    link(dve.tensor_tensor(ac, ac, bc[:, 0, :], ALU.mult))
                    link(dve.scalar_tensor_tensor(ac, xa[:, :], ALPHA, ac, ALU.mult, ALU.add))
                    layer_norm(dve, link, ac, bc[:, 1, :], bc[:, 2, :], [var_done], [rstd_done, 1], xa[:, :]).then_inc(xnew_done, 1)
            end_step()

        with nc.Fori(0, DEPTH) as L:
            step_modulation(L)
            step_load_in(L)
            step_input(L, 0, True)
            with nc.Fori(1, NBLK) as b:
                step_input(L, b, False)
            step_load_out(L)
            step_attention(L, 0, True)
            with nc.Fori(1, NBLK) as b:
                step_attention(L, b, False)
            step_load_route(L)
            with nc.Fori(0, NBLK) as b:
                step_route(L, b)
            with nc.Fori(0, NBLK) as b:
                step_experts(L, b)

        with nc.Block() as block:
            @block.sync
            def _(sp):
                sp.dma_start(a["o_y_prompt"].rearrange("a t d -> (a t) d"), x_dram[0, :, :]).then_inc(stored, 16)
                sp.dma_start(a["o_y_sample"].rearrange("a t d -> (a t) d"), x_dram[1:NBLK, :, :].rearrange("b p n -> (b p) n")).then_inc(stored, 16)
                sp.wait_ge(stored, 32)


def _constants():
    c = {"c_ident": np.eye(P, dtype=np.float32)}
    qc = np.arange(P)[:, None] % GRID_W
    kc = np.arange(GRID_W)[None, :]
    start = np.clip(qc - NA_KW // 2, 0, GRID_W - NA_KW)
    c["c_natmask"] = np.where((kc >= start) & (kc < start + NA_KW), 0.0, MASKED).astype(np.float32)
    off = np.arange(7 * P)[None, :] - 3 * P - np.arange(P)[:, None]
    c["c_band"] = np.where(np.abs(off) <= P, 0.0, MASKED).astype(np.float32)
    c["c_iota"] = np.tile(np.arange(TOPK, dtype=np.uint32), (P, 1))
    c["c_first"] = (np.arange(DEPTH, dtype=np.float32) * NEXP)[:, None]
    t = np.arange(DEC_SEQ)
    pos = [(t // GRID_W).astype(np.float32), (t % GRID_W).astype(np.float32)]
    tab = np.zeros((NBLK, P, ROPE_COLS), np.float32)
    at = 0
    for dim in (ROPE, HD):
        nf = dim // 4
        fr = (10000.0 ** (-np.arange(nf, dtype=np.float32) / nf)).astype(np.float32)
        ang = np.concatenate([pos[0][:, None] * fr, pos[1][:, None] * fr], -1)
        co, si = np.cos(ang), np.sin(ang)
        tab[0, :, at:at + dim] = 1.0
        tab[1:, :, at:at + dim] = np.concatenate([co, co], -1).reshape(NLAT, P, dim)
        tab[1:, :, at + dim:at + 2 * dim] = np.concatenate([-si, si], -1).reshape(NLAT, P, dim)
        at += 2 * dim
    c["c_rope"] = np.ascontiguousarray(tab.transpose(1, 0, 2))
    return c


def _layout(i):
    L = DEPTH

    def rows(w, n):
        return w.reshape(L, KD, P, n).transpose(0, 2, 1, 3).reshape(L, P, KD * n)

    g = {}
    g["x0"] = np.concatenate([i["x_prompt"].reshape(1, P, D), i["x_sample"].reshape(NLAT, P, D)])
    g["condT"] = np.stack([i["c_ctx"].reshape(KD, P), i["c"].reshape(KD, P)], -1).transpose(1, 0, 2)
    g["w_ada"] = i["w_ada"].reshape(L, KD, P, ADA_PIECES, ADA_COLS).transpose(0, 3, 2, 1, 4).reshape(L, ADA_PIECES, P, KD * ADA_COLS)
    g["b_ada"] = i["b_ada"].reshape(L, MOD, P).transpose(0, 2, 1)
    w = i["w_in"]
    dq = w[:, :, C_D:C_D + GW].reshape(L, D, H, HD)[:, :, [0, 2, 1, 3]].reshape(L, D, GW)
    g["w_in"] = rows(np.concatenate([w[:, :, :C_D], dq, w[:, :, C_D + GW:]], -1), IN_COLS)
    g["w_out"] = rows(i["w_out"], D)
    g["w_q"] = rows(i["peer_w_q"], 2 * PH * P)
    g["w_uq"] = i["mla_w_uq"].reshape(L, 2, P, H * CH).transpose(0, 2, 1, 3).reshape(L, P, 2 * H * CH)
    g["w_ukv"] = i["mla_w_ukv"]
    g["a_wT"] = i["a_w_s"].transpose(0, 3, 1, 2)
    g["a_bT"] = i["a_b_s"].transpose(0, 2, 1)
    g["a_g"], g["a_bb"] = i["a_norm_g"], i["a_norm_b"]
    g["mq_g"], g["mkv_g"] = i["mla_q_norm_g"], i["mla_kv_norm_g"]
    g["out_g"] = i["out_norm_g"]
    for n in ("ln1_g", "ln1_b", "ln2_g", "ln2_b"):
        g[n] = i[n]
    g["sinks"] = i["swa_sinks"]
    g["rpb"] = np.pad(i["nat_rpb"], ((0, 0), (0, 0), (0, 0), (RPB_PAD, RPB_ROW - RPB_PAD - 2 * NA_KW + 1)))
    g["natkT"] = i["cache_nat_k"][0].reshape(L, 2, 2, P, HD).transpose(0, 2, 4, 1, 3).reshape(L, P, 2, P)
    g["natv"] = i["cache_nat_v"][0].transpose(0, 2, 1, 3).reshape(L, P, GW)
    g["swakT"] = i["cache_swa_k"][0].transpose(0, 1, 3, 2).reshape(L, P, P)
    g["swav"] = i["cache_swa_v"][0].transpose(0, 2, 1, 3).reshape(L, P, 2 * HD)
    g["ckvT"] = i["cache_mla_ckv"][0].transpose(0, 2, 1)
    g["kropeT"] = i["cache_mla_krope"][0].transpose(0, 2, 1)
    g["skT"] = i["peer_sub_keys"].transpose(0, 3, 1, 2)
    g["peer_u"] = i["peer_u"].reshape(L * NEXP, D)
    g["peer_v"] = i["peer_v"].reshape(L * NEXP, D)
    return g


_OUTS = [("o_y_prompt", (1, SEQ, D)), ("o_y_sample", (1, DEC_SEQ, D)), ("o_nat_k", (1, DEPTH, H, SEQ, HD)),
         ("o_nat_v", (1, DEPTH, H, SEQ, HD)), ("o_ckv", (1, DEPTH, SEQ, KVR)), ("o_krope", (1, DEPTH, SEQ, ROPE)),
         ("o_swa_k", (1, DEPTH, 2, SEQ, HD)), ("o_swa_v", (1, DEPTH, 2, SEQ, HD))]


def kernel(**inputs):
    import concourse.bacc as bacc
    from concourse.bass_utils import run_bass_kernel_spmd

    nc = bacc.Bacc("TRN2", target_bir_lowering=False, num_devices=1)
    arrays, a = {}, {}
    for name, v in {**_constants(), **_layout({k: np.asarray(v) for k, v in inputs.items()})}.items():
        v = np.ascontiguousarray(v)
        arrays["in_" + name] = v
        a[name] = nc.dram_tensor("in_" + name, v.shape, mybir.dt.from_np(v.dtype), kind="ExternalInput").ap()
    for name, shape in _OUTS:
        a[name] = nc.dram_tensor(name, shape, F32, kind="ExternalOutput").ap()
    build(nc, a)
    r = run_bass_kernel_spmd(nc, [arrays], core_ids=[0])
    return tuple(r.results[0][name] for name, _ in _OUTS)
```

```python
from contextlib import ExitStack

import numpy as np

import concourse.bass as bass
from concourse import mybir

F32 = mybir.dt.float32
U32 = mybir.dt.uint32
ACT = mybir.ActivationFunctionType
ALU = mybir.AluOpType
AX = mybir.AxisListType.X
ds = bass.ds

P = 128
DEPTH, D = 2, 1024
KD = D // P
SEQ, DEC_SEQ, GRID_W = 128, 512, 64
NLAT = DEC_SEQ // P
NBLK = 1 + NLAT
NSLOT = NBLK + 1
CTX = NSLOT - 1
H, HD, GW = 4, 64, 256
QR, KVR, NOPE, ROPE, VD = 256, 128, 64, 32, 64
CH = NOPE + ROPE
IN_COLS = 2 * GW + 3 * GW + QR + KVR + ROPE + 8 * HD
C_B, C_C, C_D = 2 * GW, 5 * GW, 5 * GW + QR + KVR + ROPE
ROWS = DEC_SEQ // GRID_W
NA_KH, NA_KW = 8, 16
NDR = 2 * NA_KH - 2
RPB_PAD = GRID_W
RPB_ROW = 160
PH, PK, TOPK = 8, 128, 16
NSEL = PH * TOPK
NEXP = PK * PK
ALPHA = (2 * DEPTH) ** 0.25
EPS = 1e-5
SCALE = HD ** -0.5
MLA_SCALE = CH ** -0.5
MASKED = -1e30
MOD = 6 * KD
ADA_PIECES = 6 * D // 512
ROPE_COLS = 2 * ROPE + 2 * HD

SP_B, SP_D, SP_A, SP_C = 0, 2 * P, 4 * P, 4 * P + GW
SP_COLS = SP_C + H * P

W_IN = KD * IN_COLS
W_COLS = W_IN
PIECE = 512
WP = KD * PIECE
IN_PIECES = -(-IN_COLS // PIECE)
Q_PIECES = 2 * PH * P // PIECE

RING = 8
HEAD_ROWS = 2 * TOPK
BY_PE = 2
DIAGS = 4



def row_order(heads):
    order = []
    for h in range(heads + 1):
        if h < heads:
            order += [("u", h, k) for k in range(TOPK)]
        if h > 0:
            order += [("v", h - 1, k) for k in range(TOPK)]
    return order


def on_pe(kind, k):
    return kind == "v" and k % BY_PE == 0


class Experts:

    def __init__(self, layer, block, first, heads, begin=False, end=False):
        self.layer, self.block, self.first, self.heads = layer, block, first, heads
        self.begin, self.end = begin, end
        self.order = row_order(heads)
        self.by_dve, self.by_pe = [], []
        d = p = 0
        for kind, _, k in self.order:
            if on_pe(kind, k):
                p += 1
            else:
                d += 1
            self.by_dve.append(d)
            self.by_pe.append(p)
        self.before = block * PH + first + layer * (NBLK * PH)

    def target(self, share):
        return min(len(self.order), len(self.order) * share // 256)

    def landed(self, n):
        return self.before * (HEAD_ROWS // RING * 16) + (n // RING + 1) * 16


def build(nc, a):
    es = ExitStack()
    with es:
        def sb(name, shape, dt=F32):
            return es.enter_context(nc.sbuf_tensor(name, shape, dt))

        sems = []

        def sem(name):
            s = es.enter_context(nc.semaphore(name))
            sems.append(s)
            return s

        x_dram = nc.dram_tensor("x_state", [NBLK, P, D], F32).ap()
        x2_dram = nc.dram_tensor("x2_state", [NBLK, P, D], F32).ap()
        mod_dram = nc.dram_tensor("mod_rows", [DEPTH, 2, MOD, P], F32).ap()
        spill_dram = nc.dram_tensor("spill_state", [NBLK, P, SP_COLS], F32).ap()
        eid_dram = nc.dram_tensor("expert_ids", [NBLK, P, NSEL], U32).ap()
        toep_dram = nc.dram_tensor("bias_rows", [DEPTH, P, H * NDR * GRID_W], F32).ap()
        gate_dram = nc.dram_tensor("gate_state", [NBLK, P, NSEL], F32).ap()

        W = sb("W", [P, W_COLS])
        ktB = sb("ktB", [P, 2, NSLOT * P])
        ktC = sb("ktC", [CH, H, NSLOT * P])
        ktD = sb("ktD", [P, NSLOT * P])
        vB = sb("vB", [P, NSLOT, GW])
        vC = sb("vC", [P, NSLOT, GW])
        vD = sb("vD", [P, NSLOT, 2 * HD])
        toep = sb("toep", [P, H, ROWS * GRID_W])
        band = sb("band", [P, NLAT * P])
        ident = sb("ident", [P, P])
        iota16 = sb("iota16", [P, TOPK], U32)
        aux = sb("aux", [P, 5 * D])
        big = sb("big", [P, 3 * 2 * (NLAT + 1) * P + 32])
        hT = sb("hT", [P, KD, P])
        xs = sb("xs", [P, D])
        condT = sb("condT", [P, KD, 2])
        condS = sb("condS", [P, KD, 2])
        modr = sb("modr", [2 * MOD, P])
        modb = sb("modb", [P, 2, MOD])
        sinks = sb("sinks", [P, H])
        a_b = sb("a_b", [P, H])
        neg_half = sb("neg_half", [P, 4])
        small = sb("small", [P, 64])
        first_row = sb("first_row", [P, 1])
        st12 = sb("st12", [P, 2, 6])
        mv = sb("mv", [P, 2])
        ve = sb("ve", [P, 4])
        rstd = sb("rstd", [P, 4])
        gates = sb("gates", [P, NSEL])
        eid = sb("eid", [P, NSEL], U32)
        ring = sb("ring", [P, RING, D])
        x2e = sb("x2e", [P, D])
        acc = sb("acc", [P, D])
        diag = sb("diag", [P, DIAGS, P])
        gates_e = sb("gates_e", [P, NSEL])
        eid_e = sb("eid_e", [P, NSEL], U32)
        eid_s = sb("eid_s", [P, 4, TOPK], U32)
        dots = sb("dots", [P, 2, TOPK])
        gel = sb("gel", [P, 2, TOPK])
        wsel = sb("wsel", [P, 2, TOPK])
        st12e = sb("st12e", [P, 2, 6])
        mve = sb("mve", [P, 2])
        vee = sb("vee", [P, 1])
        rstde = sb("rstde", [P, 1])

        bc = aux[:, 0:3 * D].rearrange("p (a n) -> p a n", a=3)
        xa = aux[:, 3 * D:4 * D]
        ob = aux[:, 4 * D:5 * D]
        w_in = [W[:, c * WP:c * WP + KD * min(PIECE, IN_COLS - c * PIECE)].rearrange("p (k n) -> p k n", k=KD)
                for c in range(IN_PIECES)]
        at = [0]

        def part(n):
            v = aux[:, at[0]:at[0] + n]
            at[0] += n
            assert at[0] <= 5 * D
            return v

        w_uq = part(2 * H * CH).rearrange("p (k n) -> p k n", k=2)
        w_ukv = part(H * (NOPE + VD)).rearrange("p (h n) -> p h n", h=H)
        a_wT = part(H * P).rearrange("p (h n) -> p h n", h=H)
        a_g, a_bb = part(GW), part(GW)
        mq_g, mkv_g = part(QR), part(KVR)
        rope_t = part(ROPE_COLS)
        gz = part(2 * GW)
        vn = part(GW)
        ckvT = part(P)
        cqT = part(2 * P).rearrange("p (k n) -> p k n", k=2)
        kr = part(CH)
        cqn = part(QR)
        ckvn = part(KVR)
        ropeA = part(6 * HD)
        z = big[:, 0:IN_COLS]
        spill = big[:, IN_COLS:IN_COLS + SP_COLS]
        qc = big[:, IN_COLS + SP_COLS:IN_COLS + SP_COLS + H * CH]
        hflat = hT[:, :, :].rearrange("p k n -> p (k n)")
        ropeB = hflat[:, 0:6 * HD]
        zr = hflat[:, 6 * HD:12 * HD]
        KEYS = (NLAT + 1) * P
        qT = xs[:, 0:SP_A]
        qTC = xs[0:CH, SP_A:SP_A + H * P]
        sS = big[:, 0:2 * KEYS].rearrange("p (a n) -> p a n", a=2)
        pr = big[:, 2 * KEYS:4 * KEYS].rearrange("p (a n) -> p a n", a=2)
        prT = big[:, 4 * KEYS:6 * KEYS].rearrange("p (a n) -> p a n", a=2)
        w_out = W[:, 0:KD * D].rearrange("p (k n) -> p k n", k=KD)
        og_bc = W[:, KD * D:KD * D + D]
        sc2_bc = W[:, KD * D + D:KD * D + 2 * D]
        sh2_bc = W[:, KD * D + 2 * D:KD * D + 3 * D]
        RC = 2 * PH * P
        w_q = [W[:, c * WP:(c + 1) * WP].rearrange("p (k n) -> p k n", k=KD) for c in range(Q_PIECES)]
        Q_ORDER = [Q_PIECES - 1] + list(range(Q_PIECES - 1))
        assert (Q_PIECES - 1) * WP >= KD * D + 3 * D
        rt = W[:, 0:4 * RC].rearrange("p (a n) -> p a n", a=4)
        scores = rt[:, 0, :].rearrange("p (g n) -> p g n", n=PK)
        scores2 = rt[:, 1, :].rearrange("p (g n) -> p g n", n=PK)
        cand = rt[:, 2, :].rearrange("p (h n) -> p h n", h=PH)
        cand2 = rt[:, 3, :].rearrange("p (h n) -> p h n", h=PH)
        onehot = rt[:, 1, :].rearrange("p (s j) -> p s j", j=TOPK)
        qsel = bc[:, 0:2, :].rearrange("p a (g t) -> p (a g) t", t=P)
        skT = bc[:, 2, 0:2 * PK].rearrange("p (s n) -> p s n", s=2)
        sv = big[:, 0:256].rearrange("p (g k) -> p g k", k=TOPK)
        si = big[:, 256:512].bitcast(U32).rearrange("p (g k) -> p g k", k=TOPK)
        sif = big[:, 512:768].rearrange("p (g k) -> p g k", k=TOPK)
        fv = big[:, 768:896].rearrange("p (h k) -> p h k", k=TOPK)
        fi = big[:, 896:1024].bitcast(U32).rearrange("p (h k) -> p h k", k=TOPK)
        fpart = big[:, 1024:1280].bitcast(U32).rearrange("p (a s) -> p a s", a=2)
        id_rc = big[:, 1280:1536].rearrange("p (a s) -> p a s", a=2)
        eidf = big[:, 1536:1664]
        fe = big[:, 1664:1792].rearrange("p (h k) -> p h k", k=TOPK)

        ps = es.enter_context(nc.psum_tensor("ps", [P, 8 * 512], F32))

        def bank(i, n=512, parts=P):
            return ps[0:parts, i * 512:i * 512 + n]

        acc_ps = ps[:, 6 * 512:8 * 512]

        loaded = sem("loaded")
        loaded2 = sem("loaded2")
        x_loaded = sem("x_loaded")
        stored = sem("stored")
        x2_stored = sem("x2_stored")
        piece_in = [sem(f"piece_in{i}") for i in range(5)]
        cache_in = sem("cache_in")
        pieces_used = sem("pieces_used")
        rows_out = sem("rows_out")
        row_sb = sem("row_sb")
        modr_in = sem("modr_in")
        dve_chain = sem("dve_chain")
        pool_chain = sem("pool_chain")
        const_done = sem("const_done")
        modT_done = sem("modT_done")
        kv_ctx = sem("kv_ctx")
        kv_sb = sem("kv_sb")
        xT_done = sem("xT_done")
        hT_sb = sem("hT_sb")
        z_done = sem("z_done")
        gelu_done = sem("gelu_done")
        z_act = sem("z_act")
        z_dve = sem("z_dve")
        var_done = sem("var_done")
        rstd_done = sem("rstd_done")
        vn_done = sem("vn_done")
        mix_done = sem("mix_done")
        mix_used = sem("mix_used")
        qkB_T = sem("qkB_T")
        rope_done = sem("rope_done")
        qkD_T = sem("qkD_T")
        latent_n = sem("latent_n")
        latent_T = sem("latent_T")
        latent_sb = sem("latent_sb")
        up_done = sem("up_done")
        up_sb = sem("up_sb")
        qc_roped = sem("qc_roped")
        qcT_done = sem("qcT_done")
        spilled = sem("spilled")
        s_done = sem("s_done")
        negmax = sem("negmax")
        exp_done = sem("exp_done")
        sink_done = sem("sink_done")
        prT_done = sem("prT_done")
        prT_sb = sem("prT_sb")
        pv_done = sem("pv_done")
        pv_used = sem("pv_used")
        on_done = sem("on_done")
        oT_done = sem("oT_done")
        oT_sb = sem("oT_sb")
        y_done = sem("y_done")
        xnew_done = sem("xnew_done")
        x2_done = sem("x2_done")
        x2T_done = sem("x2T_done")
        x2T_sb = sem("x2T_sb")
        q_done = sem("q_done")
        q_sb = sem("q_sb")
        sc_done = sem("sc_done")
        sc_sb = sem("sc_sb")
        cent_done = sem("cent_done")
        expf_done = sem("expf_done")
        route_done = sem("route_done")
        ids_in = sem("ids_in")
        e_in = sem("e_in")
        ids_staged = sem("ids_staged")
        acc_zero = sem("acc_zero")
        used_dve = sem("used_dve")
        used_pe = sem("used_pe")
        gelu_sel = sem("gelu_sel")
        w_ready = sem("w_ready")
        diag_done = sem("diag_done")
        end_in = sem("end_in")
        end_chain = sem("end_chain")
        end_var = sem("end_var")
        end_rstd = sem("end_rstd")
        end_done = sem("end_done")
        end_stored = sem("end_stored")
        all_sems = range(sems[0].num, sems[-1].num + 1)
        assert [s.num for s in sems] == list(all_sems)
        bias_stored = es.enter_context(nc.semaphore("bias_stored"))
        gath = [es.enter_context(nc.semaphore(f"gathered{i}")) for i in range(RING)]

        def end_step():
            nc.all_engine_barrier(sems_to_clear=all_sems)

        def chain(eng, s):
            n = [0]

            def link(ins):
                n[0] += 1
                ins.then_inc(s, 1)
                eng.wait_ge(s, n[0])
            return link

        def row(ap):
            return ap.broadcast_to([P, ap.shape[-1]])

        def mod_row(L, s, m):
            return row(mod_dram[L, s:s + 1, m * KD:(m + 1) * KD, :].rearrange("b c n -> b (c n)"))

        def of_block(ap, b):
            return ap[ds(b, 1), :, :].rearrange("b p n -> (b p) n")

        def layer_norm(link, dve, x, g, b_, out, stats, agg, var, rs, var_sem, pow_sem, pow_n):
            for i in range(2):
                link(dve.bn_stats(stats[:, i, :], x[:, i * 512:(i + 1) * 512]))
            link(dve.bn_aggr(agg[:, :], stats[:, :, :].rearrange("p a n -> p (a n)")))
            dve.tensor_scalar_add(var, agg[:, 1:2], EPS).then_inc(var_sem, 1)
            dve.wait_ge(pow_sem, pow_n)
            link(dve.tensor_scalar(x, x, agg[:, 0:1], rs, ALU.subtract, ALU.mult))
            link(dve.tensor_tensor(x, x, g, ALU.mult))
            return dve.tensor_tensor(out, x, b_, ALU.add)


        def experts_sync(sp, E):
            if E is not None and E.begin:
                sp.dma_start(eid_e[:, :], of_block(eid_dram, E.block)).then_inc(ids_in, 16)
                sp.dma_start(x2e[:, :], of_block(x2_dram, E.block)).then_inc(e_in, 16)
                sp.dma_start(gates_e[:, :], of_block(gate_dram, E.block)).then_inc(e_in, 16)

        def experts_sync_end(sp, E):
            if E is not None and E.end:
                sp.wait_ge(used_dve, E.by_dve[-1])
                sp.wait_ge(used_pe, E.by_pe[-1])
                s = E.block if isinstance(E.block, int) and E.block == 0 else 1
                sp.dma_start(ring[:, 0, :], of_block(x_dram, E.block)).then_inc(end_in, 16)
                sp.dma_start(ring[:, 1, :], mod_row(E.layer, s, 5)).then_inc(end_in, 16)
                sp.dma_start(ring[:, 2, :], row(a["ln2_g"][E.layer:E.layer + 1, :])).then_inc(end_in, 16)
                sp.dma_start(ring[:, 3, :], row(a["ln2_b"][E.layer:E.layer + 1, :])).then_inc(end_in, 16)
                sp.wait_ge(end_done, 1)
                sp.dma_start(of_block(x_dram, E.block), ring[:, 4, :]).then_inc(end_stored, 16)
                sp.wait_ge(end_stored, 16)

        def experts_gpsimd(pool, E):
            if E is None:
                return lambda share: None, lambda: None
            at = [0]
            if E.begin:
                pool.wait_ge(ids_in, 16)

            def gather_until(n):
                while at[0] < min(n, len(E.order)):
                    r = at[0]
                    kind, h, k = E.order[r]
                    if kind == "u" and k == 0:
                        pool.tensor_copy(eid_s[:, h % 4, :], eid_e[:, ds((E.first + h) * TOPK, TOPK)]).then_inc(ids_staged, 1)
                        pool.wait_ge(ids_staged, h + 1)
                    if r >= RING:
                        q = E.order[r - RING]
                        if on_pe(q[0], q[2]):
                            pool.wait_ge(used_pe, E.by_pe[r - RING])
                        else:
                            pool.wait_ge(used_dve, E.by_dve[r - RING])
                    pool.indirect_dma_start(
                        ring[:, r % RING, :], None, a["peer_u"] if kind == "u" else a["peer_v"],
                        bass.IndirectOffsetOnAxis(ap=eid_s[:, h % 4, k:k + 1], axis=0)).then_inc(gath[r % RING], 16)
                    at[0] += 1

            gather_until(RING)

            def rows(share):
                gather_until(E.target(share) + RING)

            def finish():
                rows(256)
                if E.end:
                    pool.wait_ge(end_var, 1)
                    pool.tensor_tensor(rstde[:, :], vee[:, :], neg_half[:, 0:1], ALU.pow).then_inc(end_rstd, 1)
            return rows, finish

        def experts_scalar(act, E):
            if E is None:
                return lambda share: None
            at = [0, 0]

            def rows(share):
                while at[0] < E.target(share):
                    r = at[0]
                    kind, h, k = E.order[r]
                    if kind == "u" and k == TOPK - 1:
                        if h >= 2:
                            act.wait_ge(w_ready, h - 1)
                        act.wait_ge(used_dve, E.by_dve[r])
                        act.activation(gel[:, h % 2, :], dots[:, h % 2, :], ACT.Gelu_apprx_tanh).then_inc(gelu_sel, 1)
                    if on_pe(kind, k):
                        n = at[1]
                        if n >= DIAGS:
                            act.wait_ge(used_pe, n - DIAGS + 1)
                        act.wait_ge(w_ready, h + 1)
                        act.activation(diag[:, n % DIAGS, :], ident[:, :], ACT.Copy, scale=wsel[:, h % 2, k:k + 1]).then_inc(diag_done, 1)
                        at[1] += 1
                    at[0] += 1
            return rows

        def experts_tensor(pe, E):
            if E is None:
                return lambda share: None
            at = [0]
            if E.begin:
                pe.wait_ge(acc_zero, 1)
                for c in range(2):
                    zeroed = pe.matmul(acc_ps[:, c * 512:(c + 1) * 512], ident[:, :], acc[:, c * 512:(c + 1) * 512], start=True, stop=False,
                                       skip_group_check=True)
                zeroed.then_inc(acc_zero, 1)

            def rows(share):
                while at[0] < E.target(share):
                    r = at[0]
                    kind, h, k = E.order[r]
                    if on_pe(kind, k):
                        pe.wait_ge(gath[r % RING], E.landed(r))
                        pe.wait_ge(diag_done, E.by_pe[r])
                        for c in range(2):
                            last = pe.matmul(acc_ps[:, c * 512:(c + 1) * 512], diag[:, (E.by_pe[r] - 1) % DIAGS, :],
                                             ring[:, r % RING, c * 512:(c + 1) * 512], start=False, stop=False, skip_group_check=True)
                        last.then_inc(used_pe, 1)
                    at[0] += 1
            return rows

        def experts_vector(dve, E):
            if E is None:
                return lambda share: None, lambda: None
            at = [0, True]
            if E.begin:
                dve.memset(acc[:, :], 0.0).then_inc(acc_zero, 1)
                dve.wait_ge(acc_zero, 1)
                dve.wait_ge(e_in, 32)

            def rows(share):
                while at[0] < E.target(share):
                    r = at[0]
                    kind, h, k = E.order[r]
                    if kind == "v" and k == 0:
                        if h >= 2:
                            dve.wait_ge(diag_done, (h - 1) * TOPK // BY_PE)
                        dve.wait_ge(gelu_sel, h + 1)
                        dve.tensor_tensor(wsel[:, h % 2, :], gel[:, h % 2, :], gates_e[:, ds((E.first + h) * TOPK, TOPK)], ALU.mult).then_inc(w_ready, 1)
                        dve.wait_ge(w_ready, h + 1)
                    if not on_pe(kind, k):
                        dve.wait_ge(gath[r % RING], E.landed(r))
                        if kind == "u":
                            if k == 0 and h >= 2:
                                dve.wait_ge(gelu_sel, h - 1)
                            dve.tensor_tensor_reduce(out=ring[:, r % RING, :], in0=ring[:, r % RING, :], in1=x2e[:, :], scale=1.0, scalar=0.0,
                                                     op0=ALU.mult, op1=ALU.add, accum_out=dots[:, h % 2, k:k + 1]).then_inc(used_dve, 1)
                        else:
                            if E.begin and at[1]:
                                dve.wait_ge(acc_zero, 2)
                                at[1] = False
                            if E.by_dve[r] > 1:
                                dve.wait_ge(used_dve, E.by_dve[r] - 1)
                            dve.scalar_tensor_tensor(acc[:, :], ring[:, r % RING, :], wsel[:, h % 2, k:k + 1], acc[:, :],
                                                     ALU.mult, ALU.add).then_inc(used_dve, 1)
                    at[0] += 1

            def finish():
                rows(256)
                if E.end:
                    link = chain(dve, end_chain)
                    dve.wait_ge(used_dve, E.by_dve[-1])
                    dve.wait_ge(used_pe, E.by_pe[-1])
                    link(dve.tensor_tensor(acc[:, :], acc[:, :], acc_ps, ALU.add))
                    dve.wait_ge(end_in, 64)
                    link(dve.tensor_tensor(acc[:, :], acc[:, :], ring[:, 1, :], ALU.mult))
                    link(dve.scalar_tensor_tensor(acc[:, :], ring[:, 0, :], ALPHA, acc[:, :], ALU.mult, ALU.add))
                    layer_norm(link, dve, acc[:, :], ring[:, 2, :], ring[:, 3, :], ring[:, 4, :], st12e, mve, vee[:, :], rstde[:, :],
                               end_var, end_rstd, 1).then_inc(end_done, 1)
            return rows, finish

        toepf = W[:, 0:H * NDR * GRID_W]
        natmask = aux[:, 0:GRID_W]
        with nc.Block() as block:
            @block.sync
            def _(sp):
                sp.dma_start(ident[:, :], a["c_ident"]).then_inc(loaded, 16)
                sp.dma_start(iota16[:, :], a["c_iota"]).then_inc(loaded, 16)
                sp.dma_start(natmask, a["c_natmask"]).then_inc(loaded, 16)
                sp.dma_start(condT[:, :, :], a["condT"]).then_inc(loaded2, 16)
                sp.dma_start(x_dram, a["x0"]).then_inc(stored, 16)
                sp.wait_ge(bias_stored, 16 * DEPTH * H * 2)
                for l in range(DEPTH):
                    if l:
                        sp.wait_ge(rows_out, 16 * l)
                    sp.dma_start(toepf, toep_dram[l, :, :]).then_inc(cache_in, 16)
                    sp.wait_ge(const_done, l + 1)
                    sp.dma_start(toep_dram[l, :, :], toepf).then_inc(rows_out, 16)
                sp.wait_ge(rows_out, 16 * DEPTH)
                sp.wait_ge(loaded, 48)
                sp.wait_ge(stored, 16)

            @block.gpsimd
            def _(pool):
                for l in range(DEPTH):
                    for h in range(H):
                        for half in range(2):
                            first = ((l * H + h) * (2 * NA_KH - 1) + 1 - half) * RPB_ROW + RPB_PAD + NA_KW - 1
                            pool.dma_start(toep_dram[l, half * GRID_W:(half + 1) * GRID_W, h * NDR * GRID_W:(h + 1) * NDR * GRID_W]
                                           .rearrange("p (r c) -> r p c", c=GRID_W),
                                           bass.AP(a["rpb"].tensor, first, [[RPB_ROW, NDR], [-1, GRID_W], [1, GRID_W]])).then_inc(bias_stored, 16)
                pool.wait_ge(bias_stored, 16 * DEPTH * H * 2)

            @block.vector
            def _(dve):
                dve.memset(neg_half[:, :], -0.5)
                dve.wait_ge(loaded, 48)
                for l in range(DEPTH):
                    dve.wait_ge(cache_in, 16 * (l + 1))
                    t = toepf.rearrange("p (r c) -> p r c", c=GRID_W)
                    dve.tensor_tensor(t, t, natmask.unsqueeze(1).broadcast_to([P, H * NDR, GRID_W]), ALU.add).then_inc(const_done, 1)

            @block.scalar
            def _(act):
                act.wait_ge(loaded2, 16)
                act.activation(condS[:, :, :], condT[:, :, :], ACT.Silu)
        end_step()

        def step_modulation(L, E):
            NB = 3
            ada = W[:, 0:NB * WP].rearrange("p (r k n) -> p r k n", r=NB, k=KD)
            w_kv = W[:, NB * WP:NB * WP + H * P].rearrange("p (h n) -> p h n", h=H)
            ckvT_c = W[:, NB * WP + H * P:NB * WP + (H + 1) * P]
            o = NB * WP + (H + 1) * P
            brow = W[0:2, o:o + NB * PIECE].rearrange("p (r n) -> p r n", r=NB)
            mrow = W[0:2, o + NB * PIECE:o + 2 * NB * PIECE].rearrange("p (r n) -> p r n", r=NB)
            c0, c1 = CTX * P, (CTX + 1) * P
            SHARE = 240 // ADA_PIECES
            flat = mod_dram[L, :, :, :].rearrange("s m n -> s (m n)")
            with nc.Block() as block:
                @block.sync
                def _(sp):
                    experts_sync(sp, E)

                    def piece(c):
                        sp.dma_start(ada[:, c % NB, :, :].rearrange("p k n -> p (k n)"), a["w_ada"][L, c, :, :]).then_inc(piece_in[c % NB], 16)
                        sp.dma_start(brow[:, c % NB, :], a["b_ada"][L:L + 1, c * PIECE:(c + 1) * PIECE].broadcast_to([2, PIECE])).then_inc(piece_in[c % NB], 16)
                    for c in range(NB):
                        piece(c)
                    sp.dma_start(w_kv, a["w_ukv"][L, :, :].rearrange("p (h n) -> p h n", h=H)).then_inc(loaded2, 16)
                    sp.dma_start(ckvT_c, a["ckvT"][L, :, :]).then_inc(loaded2, 16)
                    sp.dma_start(ktB[:, :, c0:c1], a["natkT"][L, :, :, :]).then_inc(cache_in, 16)
                    sp.dma_start(vB[:, CTX, :], a["natv"][L, :, :]).then_inc(cache_in, 16)
                    sp.dma_start(ktD[:, c0:c1], a["swakT"][L, :, :]).then_inc(cache_in, 16)
                    sp.dma_start(vD[:, CTX, :], a["swav"][L, :, :]).then_inc(cache_in, 16)
                    sp.dma_start(sinks[:, :], row(a["sinks"][L:L + 1, :])).then_inc(cache_in, 16)
                    sp.dma_start(a_b[:, :], a["a_bT"][L, :, :]).then_inc(cache_in, 16)
                    sp.dma_start(first_row[:, :], row(a["c_first"][L:L + 1, :])).then_inc(cache_in, 16)
                    for h in range(H):
                        sp.dma_start(ktC[NOPE:CH, h, c0:c1], a["kropeT"][L, :, :]).then_inc(cache_in, 16)
                    for c in range(ADA_PIECES):
                        sp.wait_ge(row_sb, c + 1)
                        sp.dma_start(flat[:, c * PIECE:(c + 1) * PIECE], mrow[:, c % NB, :]).then_inc(rows_out, 16)
                        if c + NB < ADA_PIECES:
                            sp.wait_ge(rows_out, 16 * (c + 1))
                            piece(c + NB)
                    sp.wait_ge(rows_out, 16 * ADA_PIECES)
                    sp.dma_start(modr[:, :], mod_dram[L, :, :, :].rearrange("s m n -> (s m) n")).then_inc(modr_in, 16)
                    sp.wait_ge(cache_in, 16 * (7 + H))
                    experts_sync_end(sp, E)

                @block.tensor
                def _(pe):
                    rows = experts_tensor(pe, E)
                    pe.wait_ge(loaded2, 32)
                    for h in range(H):
                        pe.matmul(bank(3, parts=NOPE)[:, h * P:(h + 1) * P], w_kv[:, h, 0:NOPE], ckvT_c, start=True, stop=True)
                    pe.matmul(bank(4, GW).rearrange("p (h n) -> p h n", h=H), ckvT_c, w_kv[:, :, NOPE:NOPE + VD],
                              start=True, stop=True).then_inc(kv_ctx, 1)
                    for c in range(ADA_PIECES):
                        pe.wait_ge(piece_in[c % NB], 32 * (c // NB + 1))
                        if c >= NB:
                            pe.wait_ge(row_sb, c - NB + 1)
                        for k in range(KD):
                            last = pe.matmul(bank(c % NB, parts=2), condS[:, k, :], ada[:, c % NB, k, :], start=(k == 0), stop=(k == KD - 1))
                        last.then_inc(pieces_used, 1)
                        rows((c + 1) * SHARE)
                    pe.wait_ge(modr_in, 16)
                    pe.transpose(bank(5, 2 * MOD), modr[:, :], ident[0:2 * MOD, 0:2 * MOD]).then_inc(modT_done, 1)
                    rows(256)

                @block.scalar
                def _(act):
                    rows = experts_scalar(act, E)
                    for c in range(ADA_PIECES):
                        rows((c + 1) * SHARE)
                    rows(256)

                @block.gpsimd
                def _(pool):
                    rows, finish = experts_gpsimd(pool, E)
                    for c in range(ADA_PIECES):
                        rows((c + 1) * SHARE)
                    finish()

                @block.vector
                def _(dve):
                    link = chain(dve, dve_chain)
                    rows, finish = experts_vector(dve, E)
                    dve.wait_ge(kv_ctx, 1)
                    dve.tensor_copy(ktC[0:NOPE, :, c0:c1], bank(3, parts=NOPE).rearrange("p (h n) -> p h n", h=H))
                    dve.tensor_copy(vC[:, CTX, :], bank(4, GW))
                    for c in range(ADA_PIECES):
                        dve.wait_ge(pieces_used, c + 1)
                        if c >= NB:
                            dve.wait_ge(rows_out, 16 * (c - NB + 1))
                        ins = dve.tensor_tensor(mrow[:, c % NB, :], bank(c % NB, parts=2), brow[:, c % NB, :], ALU.add)
                        if c * PIECE // D in (1, 4):
                            link(ins)
                            ins = dve.tensor_scalar_add(mrow[:, c % NB, :], mrow[:, c % NB, :], 1.0)
                        ins.then_inc(row_sb, 1)
                        rows((c + 1) * SHARE)
                    dve.wait_ge(modT_done, 1)
                    dve.tensor_copy(modb[:, :, :].rearrange("p s m -> p (s m)"), bank(5, 2 * MOD))
                    finish()
            end_step()

        def step_input(L, b, context, weights, E):
            slot = ds(b * P, P)
            s = 0 if context else 1
            with nc.Block() as block:
                @block.sync
                def _(sp):
                    experts_sync(sp, E)
                    sp.dma_start(xs[:, :], of_block(x_dram, b)).then_inc(x_loaded, 16)
                    sp.dma_start(rope_t, a["c_rope"][:, ds(b, 1), :].rearrange("p b n -> p (b n)")).then_inc(loaded2, 16)
                    if weights:
                        for c in range(IN_PIECES):
                            sp.dma_start(w_in[c].rearrange("p k n -> p (k n)"), a[f"w_in{c}"][L, :, :]).then_inc(piece_in[c], 16)
                        for dst, src in ((w_uq, a["w_uq"][L, :, :].rearrange("p (k n) -> p k n", k=2)),
                                         (w_ukv, a["w_ukv"][L, :, :].rearrange("p (h n) -> p h n", h=H)),
                                         (a_wT, a["a_wT"][L, :, :, :]),
                                         (a_g, row(a["a_g"][L:L + 1, :])), (a_bb, row(a["a_bb"][L:L + 1, :])),
                                         (mq_g, row(a["mq_g"][L:L + 1, :])), (mkv_g, row(a["mkv_g"][L:L + 1, :]))):
                            sp.dma_start(dst, src).then_inc(loaded, 16)
                    n_out = 0
                    if context:
                        sp.wait_ge(z_act, 1)
                        sp.dma_start(a["o_nat_k"][0, L, :, :, :].rearrange("h t d -> t h d"),
                                     z[:, C_B + GW:C_B + 2 * GW].rearrange("p (h d) -> p h d", h=H)).then_inc(stored, 16)
                        sp.wait_ge(z_dve, 1)
                        sp.dma_start(a["o_nat_v"][0, L, :, :, :].rearrange("h t d -> t h d"),
                                     z[:, C_B + 2 * GW:C_B + 3 * GW].rearrange("p (h d) -> p h d", h=H)).then_inc(stored, 16)
                        sp.wait_ge(z_act, 2)
                        sp.dma_start(a["o_krope"][0, L, :, :], z[:, C_C + QR + KVR:C_D]).then_inc(stored, 16)
                        sp.wait_ge(z_dve, 2)
                        sp.dma_start(a["o_swa_k"][0, L, :, :, :].rearrange("h t d -> t h d"),
                                     z[:, C_D + GW:C_D + GW + 2 * HD].rearrange("p (h d) -> p h d", h=2)).then_inc(stored, 16)
                        sp.dma_start(a["o_swa_v"][0, L, :, :, :].rearrange("h t d -> t h d"),
                                     z[:, C_D + GW + 2 * HD:IN_COLS].rearrange("p (h d) -> p h d", h=2)).then_inc(stored, 16)
                        sp.wait_ge(latent_n, 2)
                        sp.dma_start(a["o_ckv"][0, L, :, :], ckvn).then_inc(stored, 16)
                        n_out = 6
                    sp.wait_ge(spilled, 4)
                    sp.dma_start(spill_dram[ds(b, 1), :, 0:SP_C].rearrange("b p n -> (b p) n"), spill[:, 0:SP_C]).then_inc(stored, 16)
                    sp.dma_start(spill_dram[ds(b, 1), 0:CH, SP_C:SP_COLS].rearrange("b p n -> (b p) n"), spill[0:CH, SP_C:SP_COLS]).then_inc(stored, 16)
                    experts_sync_end(sp, E)
                    sp.wait_ge(stored, 16 * (n_out + 2))

                @block.tensor
                def _(pe):
                    rows = experts_tensor(pe, E)
                    pe.wait_ge(x_loaded, 16)
                    for k in range(KD):
                        last = pe.transpose(ps[:, 4 * 512 + k * P:4 * 512 + (k + 1) * P], xs[:, k * P:(k + 1) * P], ident[:, :])
                    last.then_inc(xT_done, 1)
                    pe.wait_ge(hT_sb, 1)
                    rows(16)
                    for c in range(IN_PIECES):
                        n = min(PIECE, IN_COLS - c * PIECE)
                        if weights:
                            pe.wait_ge(piece_in[c], 16)
                        for k in range(KD):
                            last = pe.matmul(bank(c, n), hT[:, k, :], w_in[c][:, k, :], start=(k == 0), stop=(k == KD - 1))
                        last.then_inc(z_done, 1)
                        rows(16 + 32 * (c + 1))
                    pe.wait_ge(z_act, 1)
                    for g in range(4):
                        last = pe.transpose(bank(5)[:, g * P:(g + 1) * P], z[:, C_B + g * P:C_B + (g + 1) * P], ident[:, :])
                    last.then_inc(qkB_T, 1)
                    if weights:
                        pe.wait_ge(loaded, 16 * 7)
                    pe.wait_ge(vn_done, 1)
                    for h in range(H):
                        last = pe.matmul(bank(0, GW)[:, h * HD:(h + 1) * HD], a_wT[:, h, :], vn[:, h * HD:(h + 1) * HD], start=True, stop=True)
                    last.then_inc(mix_done, 1)
                    pe.wait_ge(latent_n, 2)
                    pe.wait_ge(rope_done, 1)
                    for k in range(2):
                        pe.transpose(bank(1)[:, k * P:(k + 1) * P], cqn[:, k * P:(k + 1) * P], ident[:, :])
                    pe.transpose(bank(1)[:, 2 * P:3 * P], ckvn, ident[:, :])
                    pe.transpose(bank(1, parts=CH)[:, 3 * P:4 * P], kr, ident[:, :]).then_inc(latent_T, 1)
                    rows(192)
                    pe.wait_ge(latent_sb, 1)
                    pe.wait_ge(z_act, 2)
                    pe.wait_ge(z_dve, 2)
                    for k in range(2):
                        pe.matmul(bank(2, H * CH), cqT[:, k, :], w_uq[:, k, :], start=(k == 0), stop=(k == 1))
                    for h in range(H):
                        pe.matmul(bank(3, parts=NOPE)[:, h * P:(h + 1) * P], w_ukv[:, h, 0:NOPE], ckvT, start=True, stop=True)
                    pe.matmul(bank(4, GW).rearrange("p (h n) -> p h n", h=H), ckvT, w_ukv[:, :, NOPE:NOPE + VD],
                              start=True, stop=True).then_inc(up_done, 1)
                    pe.wait_ge(rope_done, 2)
                    pe.wait_ge(spilled, 1)
                    pe.wait_ge(qkB_T, 2)
                    for g in range(3):
                        last = pe.transpose(bank(5)[:, g * P:(g + 1) * P], zr[:, g * P:(g + 1) * P], ident[:, :])
                    last.then_inc(qkD_T, 1)
                    rows(224)
                    pe.wait_ge(qc_roped, 1)
                    pe.wait_ge(mix_used, 1)
                    for h in range(H):
                        last = pe.transpose(bank(0, parts=CH)[:, h * P:(h + 1) * P], qc[:, h * CH:(h + 1) * CH], ident[:, :])
                    last.then_inc(qcT_done, 1)
                    rows(256)

                @block.scalar
                def _(act):
                    rows = experts_scalar(act, E)
                    rows(48)
                    act.wait_ge(z_done, 1)
                    act.activation(gz, bank(0), ACT.Gelu_apprx_tanh).then_inc(gelu_done, 1)
                    rows(80)
                    act.wait_ge(z_done, 2)
                    act.copy(z[:, 512:1024], bank(1)).then_inc(z_act, 1)
                    rows(144)
                    act.wait_ge(z_done, 4)
                    act.copy(z[:, 1536:2048], bank(3)).then_inc(z_act, 1)
                    rows(176)
                    act.wait_ge(qkB_T, 1)
                    act.copy(spill[:, SP_B:SP_B + 2 * P], bank(5)[:, 0:2 * P])
                    act.copy(ktB[:, :, slot], bank(5)[:, 2 * P:4 * P].rearrange("p (g n) -> p g n", g=2)).then_inc(qkB_T, 1)
                    act.wait_ge(qkB_T, 2)
                    act.sem_inc(spilled, 1)
                    rows(192)
                    act.wait_ge(up_done, 1)
                    act.copy(ktC[0:NOPE, :, slot], bank(3, parts=NOPE).rearrange("p (h n) -> p h n", h=H))
                    act.copy(vC[:, ds(b, 1), :], bank(4, GW).unsqueeze(1))
                    act.wait_ge(qkD_T, 1)
                    act.copy(spill[:, SP_D:SP_D + 2 * P], bank(5)[:, 0:2 * P])
                    act.copy(ktD[:, slot], bank(5)[:, 2 * P:3 * P]).then_inc(spilled, 1)
                    rows(224)
                    act.wait_ge(qcT_done, 1)
                    act.copy(spill[0:CH, SP_C:SP_COLS], bank(0, parts=CH)).then_inc(spilled, 1)
                    rows(256)

                @block.gpsimd
                def _(pool):
                    link = chain(pool, pool_chain)
                    rows, finish = experts_gpsimd(pool, E)

                    def rope(out, src, nh, stride, half, first, tabs):
                        w = 2 * half
                        s4 = src.rearrange("p (h n) -> p h n", h=nh)
                        o4 = out.rearrange("p (h n) -> p h n", h=nh)
                        t4 = ropeA[:, 0:nh * w].rearrange("p (h n) -> p h n", h=nh)
                        u4 = ropeB[:, 0:nh * w].rearrange("p (h n) -> p h n", h=nh)
                        cos = rope_t[:, tabs:tabs + w].unsqueeze(1).broadcast_to([P, nh, w])
                        sin = rope_t[:, tabs + w:tabs + 2 * w].unsqueeze(1)
                        pool.tensor_tensor(u4, s4[:, :, first:first + w], cos, ALU.mult)
                        pool.tensor_tensor(t4[:, :, 0:half], s4[:, :, first + half:first + w],
                                           sin[:, :, 0:half].broadcast_to([P, nh, half]), ALU.mult)
                        link(pool.tensor_tensor(t4[:, :, half:w], s4[:, :, first:first + half],
                                                sin[:, :, half:w].broadcast_to([P, nh, half]), ALU.mult))
                        return pool.tensor_tensor(o4[:, :, first:first + w], u4, t4, ALU.add)

                    rows(80)
                    pool.wait_ge(var_done, 1)
                    pool.tensor_tensor(rstd[:, 0:1], ve[:, 0:1], neg_half[:, 0:1], ALU.pow).then_inc(rstd_done, 1)
                    rows(176)
                    pool.wait_ge(var_done, 2)
                    pool.tensor_tensor(rstd[:, 1:3], ve[:, 1:3], neg_half[:, 0:2], ALU.pow).then_inc(rstd_done, 1)
                    pool.wait_ge(z_done, 5)
                    pool.wait_ge(z_act, 2)
                    pool.wait_ge(loaded2, 16)
                    rope(kr[:, NOPE:CH], z[:, C_C + QR + KVR:C_D], 1, CH, ROPE // 2, 0, 0).then_inc(rope_done, 1)
                    pool.wait_ge(rope_done, 1)
                    rows(192)
                    pool.wait_ge(z_dve, 2)
                    rope(zr, z[:, C_D:C_D + 6 * HD], 6, HD, HD // 2, 0, 2 * ROPE).then_inc(rope_done, 1)
                    pool.wait_ge(rope_done, 2)
                    rows(224)
                    pool.wait_ge(up_sb, 1)
                    rope(qc, qc, H, CH, ROPE // 2, NOPE, 0).then_inc(qc_roped, 1)
                    finish()

                @block.vector
                def _(dve):
                    link = chain(dve, dve_chain)
                    rows, finish = experts_vector(dve, E)
                    if weights:
                        link(dve.memset(kr[:, 0:NOPE], 0.0))
                    dve.wait_ge(xT_done, 1)
                    for k in range(KD):
                        last = dve.tensor_scalar(hT[:, k, :], ps[:, 4 * 512 + k * P:4 * 512 + (k + 1) * P],
                                                 modb[:, s, KD + k:KD + k + 1], modb[:, s, k:k + 1], ALU.mult, ALU.add)
                    last.then_inc(hT_sb, 1)
                    rows(64)
                    if weights:
                        dve.wait_ge(loaded, 16 * 7)
                    dve.wait_ge(gelu_done, 1)
                    link(dve.bn_stats(st12[:, 0, :], gz[:, GW:2 * GW]))
                    link(dve.bn_aggr(mv[:, :], st12[:, 0, :]))
                    dve.tensor_scalar_add(ve[:, 0:1], mv[:, 1:2], EPS).then_inc(var_done, 1)
                    rows(96)
                    dve.wait_ge(rstd_done, 1)
                    link(dve.tensor_scalar(vn, gz[:, GW:2 * GW], mv[:, 0:1], rstd[:, 0:1], ALU.subtract, ALU.mult))
                    link(dve.tensor_tensor(vn, vn, a_g, ALU.mult))
                    dve.tensor_tensor(vn, vn, a_bb, ALU.add).then_inc(vn_done, 1)
                    rows(112)
                    dve.wait_ge(z_done, 3)
                    dve.tensor_copy(z[:, 1024:1536], bank(2)).then_inc(z_dve, 1)
                    rows(176)
                    dve.wait_ge(z_done, 5)
                    dve.tensor_copy(z[:, 2048:IN_COLS], bank(4, IN_COLS - 2048)).then_inc(z_dve, 1)
                    dve.wait_ge(z_dve, 2)
                    dve.tensor_copy(vB[:, ds(b, 1), :], z[:, C_B + 2 * GW:C_B + 3 * GW].unsqueeze(1))
                    dve.wait_ge(z_act, 2)
                    link(dve.tensor_tensor_reduce(out=cqn, in0=z[:, C_C:C_C + QR], in1=z[:, C_C:C_C + QR], scale=1.0, scalar=0.0,
                                                  op0=ALU.mult, op1=ALU.add, accum_out=small[:, 1:2]))
                    link(dve.tensor_tensor_reduce(out=ckvn, in0=z[:, C_C + QR:C_C + QR + KVR], in1=z[:, C_C + QR:C_C + QR + KVR],
                                                  scale=1.0, scalar=0.0, op0=ALU.mult, op1=ALU.add, accum_out=small[:, 2:3]))
                    dve.tensor_scalar(ve[:, 1:2], small[:, 1:2], 1.0 / QR, EPS, ALU.mult, ALU.add)
                    dve.tensor_scalar(ve[:, 2:3], small[:, 2:3], 1.0 / KVR, EPS, ALU.mult, ALU.add).then_inc(var_done, 1)
                    dve.wait_ge(rstd_done, 2)
                    dve.scalar_tensor_tensor(cqn, z[:, C_C:C_C + QR], rstd[:, 1:2], mq_g, ALU.mult, ALU.mult).then_inc(latent_n, 1)
                    dve.scalar_tensor_tensor(ckvn, z[:, C_C + QR:C_C + QR + KVR], rstd[:, 2:3], mkv_g, ALU.mult, ALU.mult).then_inc(latent_n, 1)
                    dve.wait_ge(mix_done, 1)
                    for h in range(H):
                        last = dve.scalar_tensor_tensor(spill[:, SP_A + h * HD:SP_A + (h + 1) * HD], bank(0, GW)[:, h * HD:(h + 1) * HD],
                                                        a_b[:, h:h + 1], gz[:, h * HD:(h + 1) * HD], ALU.add, ALU.mult)
                    last.then_inc(mix_used, 1)
                    dve.wait_ge(mix_used, 1)
                    dve.sem_inc(spilled, 1)
                    dve.wait_ge(latent_T, 1)
                    dve.tensor_copy(cqT, bank(1)[:, 0:2 * P].rearrange("p (k n) -> p k n", k=2))
                    dve.tensor_copy(ckvT, bank(1)[:, 2 * P:3 * P])
                    dve.tensor_copy(ktC[NOPE:CH, :, slot], bank(1)[NOPE:CH, 3 * P:4 * P].unsqueeze(1).broadcast_to([ROPE, H, P])).then_inc(latent_sb, 1)
                    rows(192)
                    dve.tensor_copy(vD[:, ds(b, 1), :], z[:, C_D + GW + 2 * HD:IN_COLS].unsqueeze(1))
                    dve.wait_ge(up_done, 1)
                    dve.tensor_copy(qc, bank(2, H * CH)).then_inc(up_sb, 1)
                    rows(224)
                    finish()
            end_step()

        def step_attend_route(L, b, context, E):
            nk = 1 if context else NLAT + 1
            k0 = 0 if context else 1
            sm = 0 if context else 1
            NH = 3 * H
            lat = NLAT * P
            G = 2 * PH
            HEAD_SHARE = 9
            A_END = NH * HEAD_SHARE
            TAIL = [A_END + 8, A_END + 16, A_END + 40]
            ROUTE = [TAIL[-1] + 8 * (i + 1) for i in range(12)]
            assert ROUTE[-1] <= 256

            def operands(i):
                g, h = divmod(i, H)
                if g == 1:
                    return qTC[:, h * P:(h + 1) * P], ktC[:, h, :]
                if g == 0:
                    r = slice((h % 2) * HD, (h % 2 + 1) * HD)
                    return qT[r, SP_B + (h // 2) * P:SP_B + (h // 2 + 1) * P], ktB[r, h // 2, :]
                r = slice((h // 2) * HD, (h // 2 + 1) * HD)
                return qT[r, SP_D + (h % 2) * P:SP_D + (h % 2 + 1) * P], ktD[r, :]

            def values(i, s):
                g, h = divmod(i, H)
                if g == 2:
                    return vD[:, s, (h // 2) * HD:(h // 2 + 1) * HD]
                return (vB, vC)[g][:, s, h * HD:(h + 1) * HD]

            def out_of(i):
                o = (i % 2) * 1024 + 768
                return ps[:, o:o + HD]

            with nc.Block() as block:
                @block.sync
                def _(sp):
                    experts_sync(sp, E)

                    def lay(dst, src, s):
                        sp.dma_start(dst, src).then_inc(s, 16)
                    lay(qT, spill_dram[ds(b, 1), :, 0:SP_A].rearrange("b p n -> (b p) n"), loaded)
                    lay(qTC, spill_dram[ds(b, 1), 0:CH, SP_C:SP_COLS].rearrange("b p n -> (b p) n"), loaded)
                    if not context:
                        lay(toep[:, :, :], toep_dram[L, :, :].rearrange("p (h n) -> p h n", h=H)[:, :, ds((2 * NLAT - 2 * b) * GRID_W, lat)], x_loaded)
                        lay(band[:, :], a["c_band"][:, ds(NLAT * P - b * P, lat)], x_loaded)
                    lay(ob[:, 0:GW], spill_dram[ds(b, 1), :, SP_A:SP_C].rearrange("b p n -> (b p) n"), loaded2)
                    lay(W[:, 0:KD * D], a["w_out"][L, :, :], loaded2)
                    lay(og_bc, row(a["out_g"][L:L + 1, :]), loaded2)
                    lay(bc[:, 0, :], mod_row(L, sm, 2), loaded2)
                    lay(bc[:, 1, :], row(a["ln1_g"][L:L + 1, :]), loaded2)
                    lay(bc[:, 2, :], row(a["ln1_b"][L:L + 1, :]), loaded2)
                    lay(sh2_bc, mod_row(L, sm, 3), loaded2)
                    lay(sc2_bc, mod_row(L, sm, 4), loaded2)
                    c = Q_ORDER[0]
                    lay(W[:, c * WP:(c + 1) * WP], a["w_q"][L, c, :, :], piece_in[0])
                    sp.wait_ge(s_done, NH)
                    lay(xs[:, :], of_block(x_dram, b), loaded2)
                    sp.wait_ge(xnew_done, 1)
                    sp.dma_start(of_block(x_dram, b), xs[:, :]).then_inc(stored, 16)
                    sp.wait_ge(x2_done, 1)
                    sp.dma_start(of_block(x2_dram, b), ob[:, :]).then_inc(stored, 16)
                    for i, c in enumerate(Q_ORDER[1:]):
                        lay(W[:, c * WP:(c + 1) * WP], a["w_q"][L, c, :, :], piece_in[1 + i])
                    lay(skT, a["skT"][L, :, :, :], piece_in[Q_PIECES])
                    sp.wait_ge(route_done, 2)
                    sp.dma_start(of_block(eid_dram, b), eid[:, :]).then_inc(stored, 16)
                    sp.dma_start(of_block(gate_dram, b), gates[:, :]).then_inc(stored, 16)
                    experts_sync_end(sp, E)
                    sp.wait_ge(stored, 64)

                @block.tensor
                def _(pe):
                    rows = experts_tensor(pe, E)

                    def score(i):
                        q, k = operands(i)
                        if i >= 2:
                            pe.wait_ge(exp_done, i - 1)
                            pe.wait_ge(pv_used, i - 1)
                        o = (i % 2) * 1024
                        if nk > 1:
                            pe.matmul(ps[:, o:o + lat], q, k[:, k0 * P:k0 * P + lat], start=True, stop=True)
                            pe.matmul(ps[:, o + lat:o + lat + P], q, k[:, CTX * P:(CTX + 1) * P], start=True, stop=True).then_inc(s_done, 1)
                        else:
                            pe.matmul(ps[:, o:o + P], q, k[:, 0:P], start=True, stop=True).then_inc(s_done, 1)
                    pe.wait_ge(loaded, 32)
                    score(0)
                    for i in range(NH):
                        if i + 1 < NH:
                            score(i + 1)
                        rows(i * HEAD_SHARE)
                        pe.wait_ge(exp_done, i + 1)
                        if i >= 1:
                            pe.wait_ge(prT_sb, i)
                        for s in range(nk):
                            last = pe.transpose(ps[:, 2048 + s * P:2048 + (s + 1) * P], pr[:, i % 2, s * P:(s + 1) * P], ident[:, :])
                        last.then_inc(prT_done, 1)
                        pe.wait_ge(prT_sb, i + 1)
                        for s in range(nk):
                            last = pe.matmul(out_of(i), prT[:, i % 2, s * P:(s + 1) * P], values(i, k0 + s),
                                             start=(s == 0), stop=(s == nk - 1))
                        last.then_inc(pv_done, 1)
                    rows(A_END)
                    pe.wait_ge(on_done, 1)
                    for k in range(KD):
                        last = pe.transpose(ps[:, k * P:(k + 1) * P], ob[:, k * P:(k + 1) * P], ident[:, :])
                    last.then_inc(oT_done, 1)
                    rows(TAIL[0])
                    pe.wait_ge(oT_sb, 1)
                    for c in range(2):
                        for k in range(KD):
                            last = pe.matmul(bank(2 + c), hT[:, k, :], w_out[:, k, c * 512:(c + 1) * 512], start=(k == 0), stop=(k == KD - 1))
                    last.then_inc(y_done, 1)
                    rows(TAIL[2])
                    pe.wait_ge(x2_done, 1)
                    for k in range(KD):
                        last = pe.transpose(ps[:, k * P:(k + 1) * P], ob[:, k * P:(k + 1) * P], ident[:, :])
                    last.then_inc(x2T_done, 1)
                    pe.wait_ge(x2T_sb, 1)
                    for i, c in enumerate(Q_ORDER):
                        pe.wait_ge(piece_in[i], 16)
                        for g in range(4):
                            for k in range(KD):
                                last = pe.matmul(bank(2 + c)[:, g * P:(g + 1) * P], w_q[c][:, k, g * P:(g + 1) * P], hT[:, k, :],
                                                 start=(k == 0), stop=(k == KD - 1))
                        last.then_inc(q_done, 1)
                        rows(ROUTE[i])
                    pe.wait_ge(piece_in[Q_PIECES], 16)
                    for i, c in enumerate(Q_ORDER):
                        pe.wait_ge(q_sb, i + 1)
                        if i >= 2:
                            pe.wait_ge(sc_sb, i - 1)
                        for g in range(4):
                            last = pe.matmul(bank(i % 2)[:, g * P:(g + 1) * P], qsel[:, 4 * c + g, :], skT[:, g % 2, :], start=True, stop=True)
                        last.then_inc(sc_done, 1)
                    for i in range(4, 12):
                        rows(ROUTE[i])
                    rows(256)

                @block.scalar
                def _(act):
                    rows = experts_scalar(act, E)
                    for i in range(NH):
                        g, h = divmod(i, H)
                        o = (i % 2) * 1024
                        plain = nk == 1 or g == 1
                        src = ps[:, o:o + nk * P] if plain else sS[:, i % 2, :]
                        sc = (MLA_SCALE if g == 1 else SCALE) if plain else 1.0
                        rows(i * HEAD_SHARE)
                        act.wait_ge(negmax, i + 1)
                        if i >= 2:
                            act.wait_ge(prT_done, i - 1)
                        if g == 2:
                            act.activation(small[:, 32 + h:33 + h], sinks[:, h:h + 1], ACT.Exp, bias=small[:, 16 + i:17 + i]).then_inc(sink_done, 1)
                        act.activation(pr[:, i % 2, 0:nk * P], src, ACT.Exp, bias=small[:, 16 + i:17 + i], scale=sc,
                                       accum_out=small[:, 36 + i:37 + i]).then_inc(exp_done, 1)
                        act.wait_ge(prT_done, i + 1)
                        if i >= 2:
                            act.wait_ge(pv_done, i - 1)
                        act.copy(prT[:, i % 2, 0:nk * P], ps[:, 2048:2048 + nk * P]).then_inc(prT_sb, 1)
                    rows(TAIL[2])
                    act.wait_ge(x2_done, 1)
                    for i, c in enumerate(Q_ORDER):
                        act.wait_ge(q_done, i + 1)
                        act.copy(qsel[:, 4 * c:4 * c + 4, :], bank(2 + c).rearrange("p (g t) -> p g t", t=P)).then_inc(q_sb, 1)
                        rows(ROUTE[i])
                    for i, c in enumerate(Q_ORDER):
                        act.wait_ge(sc_done, i + 1)
                        act.copy(scores[:, 4 * c:4 * c + 4, :], bank(i % 2).rearrange("p (g n) -> p g n", n=PK)).then_inc(sc_sb, 1)
                    for i in range(4, 12):
                        rows(ROUTE[i])
                        if i == 10:
                            act.wait_ge(cent_done, 1)
                            act.activation(fe, fe, ACT.Exp).then_inc(expf_done, 1)
                    rows(256)

                @block.gpsimd
                def _(pool):
                    rows, finish = experts_gpsimd(pool, E)
                    for i in range(NH):
                        rows(i * HEAD_SHARE)
                    rows(A_END)
                    pool.wait_ge(var_done, 1)
                    pool.tensor_tensor(rstd[:, :], ve[:, :], neg_half[:, :], ALU.pow).then_inc(rstd_done, 1)
                    rows(TAIL[0])
                    rows(TAIL[1])
                    pool.wait_ge(var_done, 2)
                    pool.tensor_tensor(rstd[:, 0:1], ve[:, 0:1], neg_half[:, 0:1], ALU.pow).then_inc(rstd_done, 1)
                    rows(TAIL[2])
                    for i in range(12):
                        rows(ROUTE[i])
                    finish()

                @block.vector
                def _(dve):
                    link = chain(dve, dve_chain)
                    rows, finish_experts = experts_vector(dve, E)

                    def negate_max(i):
                        g, h = divmod(i, H)
                        o = (i % 2) * 1024
                        mx, nm = small[:, i:i + 1], small[:, 16 + i:17 + i]
                        dve.wait_ge(s_done, i + 1)
                        plain = nk == 1 or g == 1
                        sc = MLA_SCALE if g == 1 else SCALE
                        if not plain:
                            if i >= 2:
                                dve.wait_ge(exp_done, i - 1)
                            bias = toep[:, h, :] if g == 0 else band[:, :]
                            dve.scalar_tensor_tensor(sS[:, i % 2, 0:lat], ps[:, o:o + lat], sc, bias, ALU.mult, ALU.add)
                            link(dve.tensor_scalar_mul(sS[:, i % 2, lat:lat + P], ps[:, o + lat:o + lat + P], sc))
                            link(dve.reduce_max(mx, sS[:, i % 2, :], AX))
                            sc = 1.0
                        else:
                            link(dve.reduce_max(mx, ps[:, o:o + nk * P], AX))
                        if g == 2:
                            link(dve.tensor_scalar(mx, mx, sc, sinks[:, h:h + 1], ALU.mult, ALU.max))
                            sc = 1.0
                        dve.tensor_scalar_mul(nm, mx, -sc).then_inc(negmax, 1)

                    def finish(i):
                        g, h = divmod(i, H)
                        l = small[:, 36 + i:37 + i]
                        dve.wait_ge(exp_done, i + 1)
                        if g == 2:
                            dve.wait_ge(sink_done, h + 1)
                            link(dve.tensor_tensor(l, l, small[:, 32 + h:33 + h], ALU.add))
                        link(dve.reciprocal(small[:, 48 + i:49 + i], l))
                        dve.wait_ge(pv_done, i + 1)
                        dve.tensor_scalar_mul(ob[:, GW + i * HD:GW + (i + 1) * HD], out_of(i), small[:, 48 + i:49 + i]).then_inc(pv_used, 1)

                    if not context:
                        dve.wait_ge(x_loaded, 32)
                    negate_max(0)
                    for i in range(NH):
                        if i + 1 < NH:
                            negate_max(i + 1)
                        rows(i * HEAD_SHARE)
                        finish(i)
                    rows(A_END)
                    dve.wait_ge(pv_used, NH)
                    dve.wait_ge(loaded2, 16 * 9)
                    for g in range(4):
                        o = ob[:, g * GW:(g + 1) * GW]
                        last = dve.tensor_tensor_reduce(out=xa[:, g * GW:(g + 1) * GW], in0=o, in1=o, scale=1.0, scalar=0.0,
                                                        op0=ALU.mult, op1=ALU.add, accum_out=small[:, g:g + 1])
                    link(last)
                    dve.tensor_scalar(ve[:, :], small[:, 0:4], 1.0 / GW, EPS, ALU.mult, ALU.add).then_inc(var_done, 1)
                    dve.wait_ge(rstd_done, 1)
                    for g in range(4):
                        o = ob[:, g * GW:(g + 1) * GW]
                        last = dve.scalar_tensor_tensor(o, o, rstd[:, g:g + 1], og_bc[:, g * GW:(g + 1) * GW], ALU.mult, ALU.mult)
                    last.then_inc(on_done, 1)
                    dve.wait_ge(oT_done, 1)
                    dve.tensor_copy(hflat, ps[:, 0:KD * P]).then_inc(oT_sb, 1)
                    rows(TAIL[0])
                    rows(TAIL[1])
                    dve.wait_ge(y_done, 1)
                    link(dve.tensor_tensor(xa, ps[:, 2 * 512:4 * 512], bc[:, 0, :], ALU.mult))
                    link(dve.scalar_tensor_tensor(xa, xs[:, :], ALPHA, xa, ALU.mult, ALU.add))
                    layer_norm(link, dve, xa, bc[:, 1, :], bc[:, 2, :], xs[:, :], st12, mv, ve[:, 0:1], rstd[:, 0:1],
                               var_done, rstd_done, 2).then_inc(xnew_done, 1)
                    dve.wait_ge(xnew_done, 1)
                    link(dve.tensor_tensor(ob, xs[:, :], sc2_bc, ALU.mult))
                    dve.tensor_tensor(ob, ob, sh2_bc, ALU.add).then_inc(x2_done, 1)
                    rows(TAIL[2])
                    dve.wait_ge(x2T_done, 1)
                    dve.tensor_copy(hflat, ps[:, 0:KD * P]).then_inc(x2T_sb, 1)
                    for i in range(4):
                        rows(ROUTE[i])

                    def top16(vals, idx, src, src2, n, points):
                        for g in range(n):
                            last = dve.max(vals[:, g, 0:8], src[:, g, :])
                        link(last)
                        rows(points[0])
                        for g in range(n):
                            dve.max_index(idx[:, g, 0:8], vals[:, g, 0:8], src[:, g, :])
                            last = dve.match_replace(src2[:, g, :], vals[:, g, 0:8], src[:, g, :], -3e38)
                        link(last)
                        rows(points[1])
                        for g in range(n):
                            last = dve.max(vals[:, g, 8:16], src2[:, g, :])
                        link(last)
                        rows(points[2])
                        for g in range(n):
                            last = dve.max_index(idx[:, g, 8:16], vals[:, g, 8:16], src2[:, g, :])
                        link(last)

                    dve.wait_ge(sc_sb, 4)
                    top16(sv, si, scores, scores2, G, ROUTE[4:7])
                    dve.tensor_copy(sif, si)
                    sv2 = sv.rearrange("p (h s) k -> p h s k", s=2)
                    link(dve.tensor_tensor(cand.rearrange("p h (i j) -> p h i j", i=TOPK),
                                           sv2[:, :, 0, :].unsqueeze(3).broadcast_to([P, PH, TOPK, TOPK]),
                                           sv2[:, :, 1, :].unsqueeze(2).broadcast_to([P, PH, TOPK, TOPK]), ALU.add))
                    top16(fv, fi, cand, cand2, PH, ROUTE[7:10])
                    dve.tensor_tensor(fe, fv, fv[:, :, 0:1].broadcast_to([P, PH, TOPK]), ALU.subtract).then_inc(cent_done, 1)
                    rows(ROUTE[10])
                    fis = fi.rearrange("p h k -> p (h k)")
                    dve.tensor_scalar(fpart[:, 0, :], fis, 4, None, ALU.logical_shift_right)
                    link(dve.tensor_scalar(fpart[:, 1, :], fis, TOPK - 1, None, ALU.bitwise_and))
                    sif2 = sif.rearrange("p (h s) k -> p h s k", s=2)
                    oh4 = onehot.rearrange("p (h k) j -> p h k j", h=PH)
                    for s in range(2):
                        link(dve.tensor_tensor(onehot, fpart[:, s, :].unsqueeze(2).broadcast_to([P, NSEL, TOPK]),
                                               iota16[:, :].unsqueeze(1).broadcast_to([P, NSEL, TOPK]), ALU.is_equal))
                        link(dve.tensor_tensor(oh4, oh4, sif2[:, :, s, :].unsqueeze(2).broadcast_to([P, PH, TOPK, TOPK]), ALU.mult))
                        link(dve.reduce_sum(id_rc[:, s, :], onehot, AX))
                    link(dve.scalar_tensor_tensor(eidf, id_rc[:, 0, :], float(PK), id_rc[:, 1, :], ALU.mult, ALU.add))
                    dve.tensor_scalar(eid[:, :], eidf, first_row[:, 0:1], None, ALU.add).then_inc(route_done, 1)
                    dve.wait_ge(expf_done, 1)
                    link(dve.reduce_sum(small[:, 0:PH], fe, AX))
                    link(dve.reciprocal(small[:, 8:8 + PH], small[:, 0:PH]))
                    dve.tensor_tensor(gates[:, :].rearrange("p (h k) -> p h k", h=PH), fe,
                                      small[:, 8:8 + PH].unsqueeze(2).broadcast_to([P, PH, TOPK]), ALU.mult).then_inc(route_done, 1)
                    rows(ROUTE[11])
                    finish_experts()
            end_step()

        def step_experts_only(E):
            with nc.Block() as block:
                @block.sync
                def _(sp):
                    experts_sync(sp, E)
                    experts_sync_end(sp, E)

                @block.tensor
                def _(pe):
                    experts_tensor(pe, E)(256)

                @block.scalar
                def _(act):
                    experts_scalar(act, E)(256)

                @block.gpsimd
                def _(pool):
                    experts_gpsimd(pool, E)[1]()

                @block.vector
                def _(dve):
                    experts_vector(dve, E)[1]()
            end_step()

        LAST = NBLK - 1
        step_modulation(0, None)
        step_input(0, 0, True, True, None)
        step_attend_route(0, 0, True, None)
        for L in range(DEPTH):
            step_input(L, 1, False, True, Experts(L, 0, 0, 1, begin=True))
            with nc.Fori(2, NBLK) as b:
                step_input(L, b, False, False, Experts(L, 0, b - 1, 1))
            step_attend_route(L, 1, False, Experts(L, 0, NLAT, PH - NLAT, end=True))
            with nc.Fori(1, LAST) as b:
                step_attend_route(L, b + 1, False, Experts(L, b, 0, PH, begin=True, end=True))
            if L + 1 < DEPTH:
                step_modulation(L + 1, Experts(L, LAST, 0, 2, begin=True))
                step_input(L + 1, 0, True, True, Experts(L, LAST, 2, 1))
                step_attend_route(L + 1, 0, True, Experts(L, LAST, 3, PH - 3, end=True))
            else:
                step_experts_only(Experts(L, LAST, 0, PH, begin=True, end=True))

        with nc.Block() as block:
            @block.sync
            def _(sp):
                sp.dma_start(a["o_y_prompt"].rearrange("a t d -> (a t) d"), x_dram[0, :, :]).then_inc(stored, 16)
                sp.dma_start(a["o_y_sample"].rearrange("a t d -> (a t) d"), x_dram[1:NBLK, :, :].rearrange("b p n -> (b p) n")).then_inc(stored, 16)
                sp.wait_ge(stored, 32)


def _constants():
    c = {"c_ident": np.eye(P, dtype=np.float32)}
    qc = np.arange(P)[:, None] % GRID_W
    kc = np.arange(GRID_W)[None, :]
    start = np.clip(qc - NA_KW // 2, 0, GRID_W - NA_KW)
    c["c_natmask"] = np.where((kc >= start) & (kc < start + NA_KW), 0.0, MASKED).astype(np.float32)
    off = np.arange(7 * P)[None, :] - 3 * P - np.arange(P)[:, None]
    c["c_band"] = np.where(np.abs(off) <= P, 0.0, MASKED).astype(np.float32)
    c["c_iota"] = np.tile(np.arange(TOPK, dtype=np.uint32), (P, 1))
    c["c_first"] = (np.arange(DEPTH, dtype=np.float32) * NEXP)[:, None]
    t = np.arange(DEC_SEQ)
    pos = [(t // GRID_W).astype(np.float32), (t % GRID_W).astype(np.float32)]
    tab = np.zeros((NBLK, P, ROPE_COLS), np.float32)
    at = 0
    for dim in (ROPE, HD):
        nf = dim // 4
        fr = (10000.0 ** (-np.arange(nf, dtype=np.float32) / nf)).astype(np.float32)
        ang = np.concatenate([pos[0][:, None] * fr, pos[1][:, None] * fr], -1)
        co, si = np.cos(ang), np.sin(ang)
        tab[0, :, at:at + dim] = 1.0
        tab[1:, :, at:at + dim] = np.concatenate([co, co], -1).reshape(NLAT, P, dim)
        tab[1:, :, at + dim:at + 2 * dim] = np.concatenate([-si, si], -1).reshape(NLAT, P, dim)
        at += 2 * dim
    c["c_rope"] = np.ascontiguousarray(tab.transpose(1, 0, 2))
    return c


def _layout(i):
    L = DEPTH

    def rows(w, n):
        return w.reshape(L, KD, P, n).transpose(0, 2, 1, 3).reshape(L, P, KD * n)

    g = {}
    g["x0"] = np.concatenate([i["x_prompt"].reshape(1, P, D), i["x_sample"].reshape(NLAT, P, D)])
    g["condT"] = np.stack([i["c_ctx"].reshape(KD, P), i["c"].reshape(KD, P)], -1).transpose(1, 0, 2)
    g["w_ada"] = i["w_ada"].reshape(L, KD, P, ADA_PIECES, PIECE).transpose(0, 3, 2, 1, 4).reshape(L, ADA_PIECES, P, WP)
    g["b_ada"] = i["b_ada"]
    w = i["w_in"]
    dq = w[:, :, C_D:C_D + GW].reshape(L, D, H, HD)[:, :, [0, 2, 1, 3]].reshape(L, D, GW)
    w = np.concatenate([w[:, :, :C_D], dq, w[:, :, C_D + GW:]], -1)
    for c in range(IN_PIECES):
        p = w[:, :, c * PIECE:(c + 1) * PIECE]
        g[f"w_in{c}"] = rows(p, p.shape[-1])
    g["w_out"] = rows(i["w_out"], D)
    g["w_q"] = i["peer_w_q"].reshape(L, KD, P, Q_PIECES, PIECE).transpose(0, 3, 2, 1, 4).reshape(L, Q_PIECES, P, WP)
    g["w_uq"] = i["mla_w_uq"].reshape(L, 2, P, H * CH).transpose(0, 2, 1, 3).reshape(L, P, 2 * H * CH)
    g["w_ukv"] = i["mla_w_ukv"]
    g["a_wT"] = i["a_w_s"].transpose(0, 3, 1, 2)
    g["a_bT"] = i["a_b_s"].transpose(0, 2, 1)
    g["a_g"], g["a_bb"] = i["a_norm_g"], i["a_norm_b"]
    g["mq_g"], g["mkv_g"] = i["mla_q_norm_g"], i["mla_kv_norm_g"]
    g["out_g"] = i["out_norm_g"]
    for n in ("ln1_g", "ln1_b", "ln2_g", "ln2_b"):
        g[n] = i[n]
    g["sinks"] = i["swa_sinks"]
    g["rpb"] = np.pad(i["nat_rpb"], ((0, 0), (0, 0), (0, 0), (RPB_PAD, RPB_ROW - RPB_PAD - 2 * NA_KW + 1)))
    g["natkT"] = i["cache_nat_k"][0].reshape(L, 2, 2, P, HD).transpose(0, 2, 4, 1, 3).reshape(L, P, 2, P)
    g["natv"] = i["cache_nat_v"][0].transpose(0, 2, 1, 3).reshape(L, P, GW)
    g["swakT"] = i["cache_swa_k"][0].transpose(0, 1, 3, 2).reshape(L, P, P)
    g["swav"] = i["cache_swa_v"][0].transpose(0, 2, 1, 3).reshape(L, P, 2 * HD)
    g["ckvT"] = i["cache_mla_ckv"][0].transpose(0, 2, 1)
    g["kropeT"] = i["cache_mla_krope"][0].transpose(0, 2, 1)
    g["skT"] = i["peer_sub_keys"].transpose(0, 3, 1, 2)
    g["peer_u"] = i["peer_u"].reshape(L * NEXP, D)
    g["peer_v"] = i["peer_v"].reshape(L * NEXP, D)
    return g


_OUTS = [("o_y_prompt", (1, SEQ, D)), ("o_y_sample", (1, DEC_SEQ, D)), ("o_nat_k", (1, DEPTH, H, SEQ, HD)),
         ("o_nat_v", (1, DEPTH, H, SEQ, HD)), ("o_ckv", (1, DEPTH, SEQ, KVR)), ("o_krope", (1, DEPTH, SEQ, ROPE)),
         ("o_swa_k", (1, DEPTH, 2, SEQ, HD)), ("o_swa_v", (1, DEPTH, 2, SEQ, HD))]


def kernel(**inputs):
    import concourse.bacc as bacc
    from concourse.bass_utils import run_bass_kernel_spmd

    nc = bacc.Bacc("TRN2", target_bir_lowering=False, num_devices=1)
    arrays, a = {}, {}
    for name, v in {**_constants(), **_layout({k: np.asarray(v) for k, v in inputs.items()})}.items():
        v = np.ascontiguousarray(v)
        arrays["in_" + name] = v
        a[name] = nc.dram_tensor("in_" + name, v.shape, mybir.dt.from_np(v.dtype), kind="ExternalInput").ap()
    for name, shape in _OUTS:
        a[name] = nc.dram_tensor(name, shape, F32, kind="ExternalOutput").ap()
    build(nc, a)
    r = run_bass_kernel_spmd(nc, [arrays], core_ids=[0])
    return tuple(r.results[0][name] for name, _ in _OUTS)
```

```python
from contextlib import ExitStack

import numpy as np

import concourse.bass as bass
from concourse import mybir

F32 = mybir.dt.float32
U32 = mybir.dt.uint32
ACT = mybir.ActivationFunctionType
ALU = mybir.AluOpType
AX = mybir.AxisListType.X
ds = bass.ds

P = 128
DEPTH, D = 2, 1024
KD = D // P
SEQ, DEC_SEQ, GRID_W = 128, 512, 64
NLAT = DEC_SEQ // P
NBLK = 1 + NLAT
NSLOT = NBLK + 1
CTX = NSLOT - 1
H, HD, GW = 4, 64, 256
QR, KVR, NOPE, ROPE, VD = 256, 128, 64, 32, 64
CH = NOPE + ROPE
IN_COLS = 2 * GW + 3 * GW + QR + KVR + ROPE + 8 * HD
C_B, C_C, C_D = 2 * GW, 5 * GW, 5 * GW + QR + KVR + ROPE
ROWS = DEC_SEQ // GRID_W
NA_KH, NA_KW = 8, 16
NDR = 2 * NA_KH - 2
RPB_PAD = GRID_W
RPB_ROW = 160
PH, PK, TOPK = 8, 128, 16
NSEL = PH * TOPK
NEXP = PK * PK
ALPHA = (2 * DEPTH) ** 0.25
EPS = 1e-5
SCALE = HD ** -0.5
MLA_SCALE = CH ** -0.5
MASKED = -1e30
MOD = 6 * KD
ADA_PIECES = 6 * D // 512
ROPE_COLS = 2 * ROPE + 2 * HD

SP_B, SP_D, SP_A, SP_C = 0, 2 * P, 4 * P, 4 * P + GW
SP_COLS = SP_C + H * P

W_IN = KD * IN_COLS
W_COLS = W_IN
PIECE = 512
WP = KD * PIECE
IN_PIECES = -(-IN_COLS // PIECE)
Q_PIECES = 2 * PH * P // PIECE

RING = 8
HEAD_ROWS = 2 * TOPK
BY_PE = 2
DIAGS = 4
SHORT_TURN = 4
SHARES = {
    8: (9, (8, 16, 24, 40), 8, 9),
    4: (7, (16, 32, 40, 52), 14, 8),
    5: (5, (16, 32, 36, 44), 20, 8),
}



def row_order(heads, turn):
    u = [("u", h, k) for h in range(heads) for k in range(TOPK)]
    v = [("v", h, k) for h in range(heads) for k in range(TOPK)]
    order, u = u[:TOPK], u[TOPK:]
    while v:
        order += u[:turn] + v[:turn]
        u, v = u[turn:], v[turn:]
    return order


def on_pe(kind, k):
    return kind == "v" and k % BY_PE == 0


class Experts:

    def __init__(self, layer, block, first, heads, begin=False, end=False, ended=None):
        self.layer, self.block, self.first, self.heads = layer, block, first, heads
        self.begin, self.end, self.ended = begin, end, ended
        self.order = row_order(heads, SHORT_TURN if heads == PH else TOPK)
        self.by_dve, self.by_pe = [], []
        d = p = 0
        for kind, _, k in self.order:
            if on_pe(kind, k):
                p += 1
            else:
                d += 1
            self.by_dve.append(d)
            self.by_pe.append(p)
        self.before = block * PH + first + layer * (NBLK * PH)

    def target(self, share):
        return min(len(self.order), len(self.order) * share // 256)

    def landed(self, n):
        return self.before * (HEAD_ROWS // RING * 16) + (n // RING + 1) * 16


def build(nc, a):
    es = ExitStack()
    with es:
        def sb(name, shape, dt=F32):
            return es.enter_context(nc.sbuf_tensor(name, shape, dt))

        sems = []

        def sem(name):
            s = es.enter_context(nc.semaphore(name))
            sems.append(s)
            return s

        x_dram = nc.dram_tensor("x_state", [NBLK, P, D], F32).ap()
        x2_dram = nc.dram_tensor("x2_state", [NBLK, P, D], F32).ap()
        mod_dram = nc.dram_tensor("mod_rows", [DEPTH, 2, MOD, P], F32).ap()
        spill_dram = nc.dram_tensor("spill_state", [NBLK, P, SP_COLS], F32).ap()
        eid_dram = nc.dram_tensor("expert_ids", [NBLK, P, NSEL], U32).ap()
        toep_dram = nc.dram_tensor("bias_rows", [DEPTH, P, H * NDR * GRID_W], F32).ap()
        gate_dram = nc.dram_tensor("gate_state", [NBLK, P, NSEL], F32).ap()

        W = sb("W", [P, W_COLS])
        ktB = sb("ktB", [P, 2, NSLOT * P])
        ktC = sb("ktC", [CH, H, NSLOT * P])
        ktD = sb("ktD", [P, NSLOT * P])
        vB = sb("vB", [P, NSLOT, GW])
        vC = sb("vC", [P, NSLOT, GW])
        vD = sb("vD", [P, NSLOT, 2 * HD])
        toep = sb("toep", [P, H, ROWS * GRID_W])
        band = sb("band", [P, NLAT * P])
        ident = sb("ident", [P, P])
        iota16 = sb("iota16", [P, TOPK], U32)
        aux = sb("aux", [P, 5 * D])
        big = sb("big", [P, 3 * 2 * (NLAT + 1) * P + 32])
        hT = sb("hT", [P, KD, P])
        xs = sb("xs", [P, D])
        condT = sb("condT", [P, KD, 2])
        condS = sb("condS", [P, KD, 2])
        modr = sb("modr", [2 * MOD, P])
        modb = sb("modb", [P, 2, MOD])
        sinks = sb("sinks", [P, H])
        a_b = sb("a_b", [P, H])
        neg_half = sb("neg_half", [P, 4])
        small = sb("small", [P, 64])
        first_row = sb("first_row", [P, 1])
        st12 = sb("st12", [P, 2, 6])
        mv = sb("mv", [P, 2])
        ve = sb("ve", [P, 4])
        rstd = sb("rstd", [P, 4])
        gates = sb("gates", [P, NSEL])
        eid = sb("eid", [P, NSEL], U32)
        ring = sb("ring", [P, RING, D])
        x2e = sb("x2e", [P, D])
        acc = sb("acc", [P, D])
        diag = sb("diag", [P, DIAGS, P])
        gates_e = sb("gates_e", [P, NSEL])
        eid_e = sb("eid_e", [P, NSEL], U32)
        eid_s = sb("eid_s", [P, 4, TOPK], U32)
        dots = sb("dots", [P, 2, TOPK])
        gel = sb("gel", [P, 2, TOPK])
        wsel = sb("wsel", [P, 2, TOPK])
        st12e = sb("st12e", [P, 2, 6])
        mve = sb("mve", [P, 2])
        vee = sb("vee", [P, 1])
        rstde = sb("rstde", [P, 1])

        bc = aux[:, 0:3 * D].rearrange("p (a n) -> p a n", a=3)
        xa = aux[:, 3 * D:4 * D]
        ob = aux[:, 4 * D:5 * D]
        ended_tiles = [xa, bc[:, 0, :], bc[:, 1, :], bc[:, 2, :]]
        w_in = [W[:, c * WP:c * WP + KD * min(PIECE, IN_COLS - c * PIECE)].rearrange("p (k n) -> p k n", k=KD)
                for c in range(IN_PIECES)]
        at = [0]

        def part(n):
            v = aux[:, at[0]:at[0] + n]
            at[0] += n
            assert at[0] <= 5 * D
            return v

        w_uq = part(2 * H * CH).rearrange("p (k n) -> p k n", k=2)
        w_ukv = part(H * (NOPE + VD)).rearrange("p (h n) -> p h n", h=H)
        a_wT = part(H * P).rearrange("p (h n) -> p h n", h=H)
        a_g, a_bb = part(GW), part(GW)
        mq_g, mkv_g = part(QR), part(KVR)
        rope_t = part(ROPE_COLS)
        gz = part(2 * GW)
        vn = part(GW)
        ckvT = part(P)
        cqT = part(2 * P).rearrange("p (k n) -> p k n", k=2)
        kr = part(CH)
        cqn = part(QR)
        ckvn = part(KVR)
        ropeA = part(6 * HD)
        z = big[:, 0:IN_COLS]
        spill = big[:, IN_COLS:IN_COLS + SP_COLS]
        qc = big[:, IN_COLS + SP_COLS:IN_COLS + SP_COLS + H * CH]
        ropeB = xs[:, 0:6 * HD]
        zr = xs[:, 6 * HD:12 * HD]
        hflat = hT[:, :, :].rearrange("p k n -> p (k n)")
        IN_ORDER = [2, 3, 4, 0, 1]
        KEYS = (NLAT + 1) * P
        qT = xs[:, 0:SP_A]
        qTC = xs[0:CH, SP_A:SP_A + H * P]
        sS = big[:, 0:2 * KEYS].rearrange("p (a n) -> p a n", a=2)
        pr = big[:, 2 * KEYS:4 * KEYS].rearrange("p (a n) -> p a n", a=2)
        prT = big[:, 4 * KEYS:6 * KEYS].rearrange("p (a n) -> p a n", a=2)
        w_out = W[:, 0:KD * D].rearrange("p (k n) -> p k n", k=KD)
        og_bc = W[:, Q_PIECES * WP:Q_PIECES * WP + D]
        sc2_bc = toep[:, 0:2, :].rearrange("p h n -> p (h n)")
        sh2_bc = toep[:, 2:4, :].rearrange("p h n -> p (h n)")
        RC = 2 * PH * P
        w_q = [W[:, c * WP:(c + 1) * WP].rearrange("p (k n) -> p k n", k=KD) for c in range(Q_PIECES)]
        Q_KEPT = 2
        Q_ORDER = list(range(Q_PIECES - Q_KEPT, Q_PIECES)) + list(range(Q_PIECES - Q_KEPT))
        assert (Q_PIECES - Q_KEPT) * WP >= KD * D and Q_PIECES * WP + D <= W_COLS
        rt = W[:, 0:4 * RC].rearrange("p (a n) -> p a n", a=4)
        scores = rt[:, 0, :].rearrange("p (g n) -> p g n", n=PK)
        scores2 = rt[:, 1, :].rearrange("p (g n) -> p g n", n=PK)
        cand = rt[:, 2, :].rearrange("p (h n) -> p h n", h=PH)
        cand2 = rt[:, 3, :].rearrange("p (h n) -> p h n", h=PH)
        onehot = rt[:, 1, :].rearrange("p (s j) -> p s j", j=TOPK)
        qsel = bc[:, 0:2, :].rearrange("p a (g t) -> p (a g) t", t=P)
        skT = bc[:, 2, 0:2 * PK].rearrange("p (s n) -> p s n", s=2)
        sv = big[:, 0:256].rearrange("p (g k) -> p g k", k=TOPK)
        si = big[:, 256:512].bitcast(U32).rearrange("p (g k) -> p g k", k=TOPK)
        sif = big[:, 512:768].rearrange("p (g k) -> p g k", k=TOPK)
        fv = big[:, 768:896].rearrange("p (h k) -> p h k", k=TOPK)
        fi = big[:, 896:1024].bitcast(U32).rearrange("p (h k) -> p h k", k=TOPK)
        fpart = big[:, 1024:1280].bitcast(U32).rearrange("p (a s) -> p a s", a=2)
        id_rc = big[:, 1280:1536].rearrange("p (a s) -> p a s", a=2)
        eidf = big[:, 1536:1664]
        fe = big[:, 1664:1792].rearrange("p (h k) -> p h k", k=TOPK)

        ps = es.enter_context(nc.psum_tensor("ps", [P, 8 * 512], F32))

        def bank(i, n=512, parts=P):
            return ps[0:parts, i * 512:i * 512 + n]

        acc_ps = ps[:, 6 * 512:8 * 512]

        loaded = sem("loaded")
        loaded2 = sem("loaded2")
        x_loaded = sem("x_loaded")
        stored = sem("stored")
        x2_stored = sem("x2_stored")
        piece_in = [sem(f"piece_in{i}") for i in range(5)]
        cache_in = sem("cache_in")
        pieces_used = sem("pieces_used")
        rows_out = sem("rows_out")
        row_sb = sem("row_sb")
        modr_in = sem("modr_in")
        dve_chain = sem("dve_chain")
        pool_chain = sem("pool_chain")
        const_done = sem("const_done")
        cond_in = sem("cond_in")
        cond_done = sem("cond_done")
        modT_done = sem("modT_done")
        kv_ctx = sem("kv_ctx")
        kv_sb = sem("kv_sb")
        xT_done = sem("xT_done")
        hT_sb = sem("hT_sb")
        z_done = sem("z_done")
        gelu_done = sem("gelu_done")
        z_act = sem("z_act")
        z_dve = sem("z_dve")
        var_done = sem("var_done")
        rstd_done = sem("rstd_done")
        vn_done = sem("vn_done")
        mix_done = sem("mix_done")
        mix_used = sem("mix_used")
        qkB_T = sem("qkB_T")
        rope_done = sem("rope_done")
        qkD_T = sem("qkD_T")
        latent_n = sem("latent_n")
        latent_T = sem("latent_T")
        latent_sb = sem("latent_sb")
        up_done = sem("up_done")
        up_sb = sem("up_sb")
        qc_roped = sem("qc_roped")
        qcT_done = sem("qcT_done")
        spilled = sem("spilled")
        s_done = sem("s_done")
        negmax = sem("negmax")
        exp_done = sem("exp_done")
        sink_done = sem("sink_done")
        prT_done = sem("prT_done")
        prT_sb = sem("prT_sb")
        pv_done = sem("pv_done")
        pv_used = sem("pv_used")
        on_done = sem("on_done")
        oT_done = sem("oT_done")
        oT_sb = sem("oT_sb")
        y_done = sem("y_done")
        xnew_done = sem("xnew_done")
        x2_done = sem("x2_done")
        x2T_done = sem("x2T_done")
        x2T_sb = sem("x2T_sb")
        q_done = sem("q_done")
        q_sb = sem("q_sb")
        sc_done = sem("sc_done")
        sc_sb = sem("sc_sb")
        cent_done = sem("cent_done")
        expf_done = sem("expf_done")
        route_done = sem("route_done")
        ids_in = sem("ids_in")
        e_in = sem("e_in")
        ids_staged = sem("ids_staged")
        acc_zero = sem("acc_zero")
        used_dve = sem("used_dve")
        used_pe = sem("used_pe")
        gelu_sel = sem("gelu_sel")
        w_ready = sem("w_ready")
        diag_done = sem("diag_done")
        end_in = sem("end_in")
        end_chain = sem("end_chain")
        end_var = sem("end_var")
        end_rstd = sem("end_rstd")
        end_done = sem("end_done")
        end_stored = sem("end_stored")
        all_sems = range(sems[0].num, sems[-1].num + 1)
        assert [s.num for s in sems] == list(all_sems)
        bias_stored = es.enter_context(nc.semaphore("bias_stored"))
        gath = [es.enter_context(nc.semaphore(f"gathered{i}")) for i in range(RING)]

        def end_step():
            nc.all_engine_barrier(sems_to_clear=all_sems)

        def chain(eng, s):
            n = [0]

            def link(ins):
                n[0] += 1
                ins.then_inc(s, 1)
                eng.wait_ge(s, n[0])
            return link

        def row(ap):
            return ap.broadcast_to([P, ap.shape[-1]])

        def mod_row(L, s, m):
            return row(mod_dram[L, s:s + 1, m * KD:(m + 1) * KD, :].rearrange("b c n -> b (c n)"))

        def of_block(ap, b):
            return ap[ds(b, 1), :, :].rearrange("b p n -> (b p) n")

        def layer_norm(link, dve, x, g, b_, out, stats, agg, var, rs, var_sem, pow_sem, pow_n):
            for i in range(2):
                link(dve.bn_stats(stats[:, i, :], x[:, i * 512:(i + 1) * 512]))
            link(dve.bn_aggr(agg[:, :], stats[:, :, :].rearrange("p a n -> p (a n)")))
            dve.tensor_scalar_add(var, agg[:, 1:2], EPS).then_inc(var_sem, 1)
            dve.wait_ge(pow_sem, pow_n)
            link(dve.tensor_scalar(x, x, agg[:, 0:1], rs, ALU.subtract, ALU.mult))
            link(dve.tensor_tensor(x, x, g, ALU.mult))
            return dve.tensor_tensor(out, x, b_, ALU.add)


        def experts_sync(sp, E):
            if E is not None and E.begin:
                sp.dma_start(eid_e[:, :], of_block(eid_dram, E.block)).then_inc(ids_in, 16)
                if E.ended is not None:
                    last_sum_in(sp, E.layer, E.ended, ended_tiles)
                sp.dma_start(x2e[:, :], of_block(x2_dram, E.block)).then_inc(e_in, 16)
                sp.dma_start(gates_e[:, :], of_block(gate_dram, E.block)).then_inc(e_in, 16)

        def last_sum_in(sp, layer, block, tiles):
            s = 0 if isinstance(block, int) and block == 0 else 1
            sp.dma_start(tiles[0], of_block(x_dram, block)).then_inc(end_in, 16)
            sp.dma_start(tiles[1], mod_row(layer, s, 5)).then_inc(end_in, 16)
            sp.dma_start(tiles[2], row(a["ln2_g"][layer:layer + 1, :])).then_inc(end_in, 16)
            sp.dma_start(tiles[3], row(a["ln2_b"][layer:layer + 1, :])).then_inc(end_in, 16)

        def last_sum(dve, tiles):
            link = chain(dve, end_chain)
            link(dve.tensor_tensor(acc[:, :], acc[:, :], acc_ps, ALU.add))
            dve.wait_ge(end_in, 64)
            link(dve.tensor_tensor(acc[:, :], acc[:, :], tiles[1], ALU.mult))
            link(dve.scalar_tensor_tensor(acc[:, :], tiles[0], ALPHA, acc[:, :], ALU.mult, ALU.add))
            layer_norm(link, dve, acc[:, :], tiles[2], tiles[3], tiles[0], st12e, mve, vee[:, :], rstde[:, :],
                       end_var, end_rstd, 1).then_inc(end_done, 1)

        def last_sum_rstd(pool):
            pool.wait_ge(end_var, 1)
            pool.tensor_tensor(rstde[:, :], vee[:, :], neg_half[:, 0:1], ALU.pow).then_inc(end_rstd, 1)

        def experts_sync_ended(sp, E):
            if E is not None and E.ended is not None:
                sp.wait_ge(end_done, 1)
                sp.dma_start(of_block(x_dram, E.ended), ended_tiles[0]).then_inc(end_stored, 16)

        def experts_gpsimd_ended(pool, E):
            if E is not None and E.ended is not None:
                last_sum_rstd(pool)

        def experts_vector_ended(dve, E):
            if E is not None and E.begin:
                if E.ended is not None:
                    last_sum(dve, ended_tiles)
                    dve.wait_ge(end_done, 1)
                dve.memset(acc[:, :], 0.0).then_inc(acc_zero, 1)

        def experts_sync_end(sp, E):
            if E is None:
                return
            if E.end:
                sp.wait_ge(used_dve, E.by_dve[-1])
                sp.wait_ge(used_pe, E.by_pe[-1])
                tiles = [ring[:, i, :] for i in range(4)]
                last_sum_in(sp, E.layer, E.block, tiles)
                sp.wait_ge(end_done, 1)
                sp.dma_start(of_block(x_dram, E.block), tiles[0]).then_inc(end_stored, 16)
            if E.end or E.ended is not None:
                sp.wait_ge(end_stored, 16)

        def experts_gpsimd(pool, E):
            if E is None:
                return lambda share: None, lambda: None
            at = [0]
            if E.begin:
                pool.wait_ge(ids_in, 16)

            def gather_until(n):
                while at[0] < min(n, len(E.order)):
                    r = at[0]
                    kind, h, k = E.order[r]
                    if kind == "u" and k == 0:
                        pool.tensor_copy(eid_s[:, h % 4, :], eid_e[:, ds((E.first + h) * TOPK, TOPK)]).then_inc(ids_staged, 1)
                        pool.wait_ge(ids_staged, h + 1)
                    if r >= RING:
                        q = E.order[r - RING]
                        if on_pe(q[0], q[2]):
                            pool.wait_ge(used_pe, E.by_pe[r - RING])
                        else:
                            pool.wait_ge(used_dve, E.by_dve[r - RING])
                    pool.indirect_dma_start(
                        ring[:, r % RING, :], None, a["peer_u"] if kind == "u" else a["peer_v"],
                        bass.IndirectOffsetOnAxis(ap=eid_s[:, h % 4, k:k + 1], axis=0)).then_inc(gath[r % RING], 16)
                    at[0] += 1

            gather_until(RING)

            def rows(share):
                gather_until(E.target(share) + RING)

            def finish():
                rows(256)
                if E.end:
                    last_sum_rstd(pool)
            return rows, finish

        def experts_scalar(act, E):
            if E is None:
                return lambda share: None
            at = [0, 0]

            def rows(share):
                while at[0] < E.target(share):
                    r = at[0]
                    kind, h, k = E.order[r]
                    if kind == "u" and k == TOPK - 1:
                        if h >= 2:
                            act.wait_ge(w_ready, h - 1)
                        act.wait_ge(used_dve, E.by_dve[r])
                        act.activation(gel[:, h % 2, :], dots[:, h % 2, :], ACT.Gelu_apprx_tanh).then_inc(gelu_sel, 1)
                    if on_pe(kind, k):
                        n = at[1]
                        if n >= DIAGS:
                            act.wait_ge(used_pe, n - DIAGS + 1)
                        act.wait_ge(w_ready, h + 1)
                        act.activation(diag[:, n % DIAGS, :], ident[:, :], ACT.Copy, scale=wsel[:, h % 2, k:k + 1]).then_inc(diag_done, 1)
                        at[1] += 1
                    at[0] += 1
            return rows

        def experts_tensor(pe, E):
            if E is None:
                return lambda share: None
            at = [0, E.begin]

            def rows(share):
                while at[0] < E.target(share):
                    r = at[0]
                    kind, h, k = E.order[r]
                    if on_pe(kind, k):
                        if at[1]:
                            at[1] = False
                            pe.wait_ge(acc_zero, 1)
                            for c in range(2):
                                zeroed = pe.matmul(acc_ps[:, c * 512:(c + 1) * 512], ident[:, :], acc[:, c * 512:(c + 1) * 512],
                                                   start=True, stop=False, skip_group_check=True)
                            zeroed.then_inc(acc_zero, 1)
                        pe.wait_ge(gath[r % RING], E.landed(r))
                        pe.wait_ge(diag_done, E.by_pe[r])
                        for c in range(2):
                            last = pe.matmul(acc_ps[:, c * 512:(c + 1) * 512], diag[:, (E.by_pe[r] - 1) % DIAGS, :],
                                             ring[:, r % RING, c * 512:(c + 1) * 512], start=False, stop=False, skip_group_check=True)
                        last.then_inc(used_pe, 1)
                    at[0] += 1
            return rows

        def experts_vector(dve, E):
            if E is None:
                return lambda share: None, lambda: None
            at = [0, E.begin]

            def rows(share):
                while at[0] < E.target(share):
                    r = at[0]
                    kind, h, k = E.order[r]
                    if r == 0 and E.begin:
                        dve.wait_ge(e_in, 32)
                    if kind == "v" and k == 0:
                        if h >= 2:
                            dve.wait_ge(diag_done, (h - 1) * TOPK // BY_PE)
                        dve.wait_ge(gelu_sel, h + 1)
                        dve.tensor_tensor(wsel[:, h % 2, :], gel[:, h % 2, :], gates_e[:, ds((E.first + h) * TOPK, TOPK)], ALU.mult).then_inc(w_ready, 1)
                        dve.wait_ge(w_ready, h + 1)
                    if not on_pe(kind, k):
                        dve.wait_ge(gath[r % RING], E.landed(r))
                        if kind == "u":
                            if k == 0 and h >= 2:
                                dve.wait_ge(gelu_sel, h - 1)
                            dve.tensor_tensor_reduce(out=ring[:, r % RING, :], in0=ring[:, r % RING, :], in1=x2e[:, :], scale=1.0, scalar=0.0,
                                                     op0=ALU.mult, op1=ALU.add, accum_out=dots[:, h % 2, k:k + 1]).then_inc(used_dve, 1)
                        else:
                            if at[1]:
                                dve.wait_ge(acc_zero, 2)
                                at[1] = False
                            if E.by_dve[r] > 1:
                                dve.wait_ge(used_dve, E.by_dve[r] - 1)
                            dve.scalar_tensor_tensor(acc[:, :], ring[:, r % RING, :], wsel[:, h % 2, k:k + 1], acc[:, :],
                                                     ALU.mult, ALU.add).then_inc(used_dve, 1)
                    at[0] += 1

            def finish():
                rows(256)
                if E.end:
                    dve.wait_ge(used_dve, E.by_dve[-1])
                    dve.wait_ge(used_pe, E.by_pe[-1])
                    last_sum(dve, [ring[:, i, :] for i in range(4)])

            return rows, finish

        TOEP = H * NDR * GRID_W
        ring_flat = ring[:, :, :].rearrange("p r n -> p (r n)")
        toepf = [ring_flat[:, l * TOEP:(l + 1) * TOEP] for l in range(DEPTH)]
        natmask = aux[:, 0:GRID_W]
        TOEP_IN, TOEP_MASK, TOEP_OUT = 6, 8, 9

        def start_sync(sp):
            sp.dma_start(condT[:, :, :], a["condT"]).then_inc(cond_in, 16)
            sp.dma_start(ident[:, :], a["c_ident"]).then_inc(loaded, 16)

        def start_sync_more(sp):
            sp.dma_start(iota16[:, :], a["c_iota"]).then_inc(loaded, 16)
            sp.dma_start(natmask, a["c_natmask"]).then_inc(loaded, 16)
            sp.dma_start(x_dram, a["x0"]).then_inc(stored, 16)

        def start_sync_piece(sp, c):
            if c == TOEP_IN:
                sp.wait_ge(bias_stored, 16 * DEPTH * H * 2)
                for l in range(DEPTH):
                    sp.dma_start(toepf[l], toep_dram[l, :, :]).then_inc(loaded, 16)
            if c == TOEP_OUT:
                sp.wait_ge(const_done, DEPTH)
                for l in range(DEPTH):
                    sp.dma_start(toep_dram[l, :, :], toepf[l]).then_inc(stored, 16)

        def start_gpsimd(pool):
            for l in range(DEPTH):
                for h in range(H):
                    for half in range(2):
                        first = ((l * H + h) * (2 * NA_KH - 1) + 1 - half) * RPB_ROW + RPB_PAD + NA_KW - 1
                        pool.dma_start(toep_dram[l, half * GRID_W:(half + 1) * GRID_W, h * NDR * GRID_W:(h + 1) * NDR * GRID_W]
                                       .rearrange("p (r c) -> r p c", c=GRID_W),
                                       bass.AP(a["rpb"].tensor, first, [[RPB_ROW, NDR], [-1, GRID_W], [1, GRID_W]])).then_inc(bias_stored, 16)
            pool.wait_ge(bias_stored, 16 * DEPTH * H * 2)

        def start_vector_piece(dve, c):
            if c == 0:
                dve.memset(neg_half[:, :], -0.5)
            if c == TOEP_MASK:
                dve.wait_ge(loaded, 16 * (3 + DEPTH))
                for l in range(DEPTH):
                    t = toepf[l].rearrange("p (r c) -> p r c", c=GRID_W)
                    dve.tensor_tensor(t, t, natmask.unsqueeze(1).broadcast_to([P, H * NDR, GRID_W]), ALU.add).then_inc(const_done, 1)

        def start_scalar(act):
            act.wait_ge(cond_in, 16)
            act.activation(condS[:, :, :], condT[:, :, :], ACT.Silu).then_inc(cond_done, 1)

        def step_modulation(L, E, first=False):
            NB = 3
            ada = W[:, 0:NB * WP].rearrange("p (r k n) -> p r k n", r=NB, k=KD)
            w_kv = W[:, NB * WP:NB * WP + H * P].rearrange("p (h n) -> p h n", h=H)
            ckvT_c = W[:, NB * WP + H * P:NB * WP + (H + 1) * P]
            o = NB * WP + (H + 1) * P
            brow = W[0:2, o:o + NB * PIECE].rearrange("p (r n) -> p r n", r=NB)
            mrow = W[0:2, o + NB * PIECE:o + 2 * NB * PIECE].rearrange("p (r n) -> p r n", r=NB)
            c0, c1 = CTX * P, (CTX + 1) * P
            SHARE = 240 // ADA_PIECES
            flat = mod_dram[L, :, :, :].rearrange("s m n -> s (m n)")
            with nc.Block() as block:
                @block.sync
                def _(sp):
                    experts_sync(sp, E)
                    if first:
                        start_sync(sp)

                    def piece(c):
                        sp.dma_start(ada[:, c % NB, :, :].rearrange("p k n -> p (k n)"), a["w_ada"][L, c, :, :]).then_inc(piece_in[c % NB], 16)
                        sp.dma_start(brow[:, c % NB, :], a["b_ada"][L:L + 1, c * PIECE:(c + 1) * PIECE].broadcast_to([2, PIECE])).then_inc(piece_in[c % NB], 16)
                    for c in range(NB):
                        piece(c)
                    if first:
                        start_sync_more(sp)
                    sp.dma_start(w_kv, a["w_ukv"][L, :, :].rearrange("p (h n) -> p h n", h=H)).then_inc(loaded2, 16)
                    sp.dma_start(ckvT_c, a["ckvT"][L, :, :]).then_inc(loaded2, 16)
                    sp.dma_start(ktB[:, :, c0:c1], a["natkT"][L, :, :, :]).then_inc(cache_in, 16)
                    sp.dma_start(vB[:, CTX, :], a["natv"][L, :, :]).then_inc(cache_in, 16)
                    sp.dma_start(ktD[:, c0:c1], a["swakT"][L, :, :]).then_inc(cache_in, 16)
                    sp.dma_start(vD[:, CTX, :], a["swav"][L, :, :]).then_inc(cache_in, 16)
                    sp.dma_start(sinks[:, :], row(a["sinks"][L:L + 1, :])).then_inc(cache_in, 16)
                    sp.dma_start(a_b[:, :], a["a_bT"][L, :, :]).then_inc(cache_in, 16)
                    sp.dma_start(first_row[:, :], row(a["c_first"][L:L + 1, :])).then_inc(cache_in, 16)
                    for h in range(H):
                        sp.dma_start(ktC[NOPE:CH, h, c0:c1], a["kropeT"][L, :, :]).then_inc(cache_in, 16)
                    experts_sync_ended(sp, E)
                    for c in range(ADA_PIECES):
                        if first:
                            start_sync_piece(sp, c)
                        sp.wait_ge(row_sb, c + 1)
                        sp.dma_start(flat[:, c * PIECE:(c + 1) * PIECE], mrow[:, c % NB, :]).then_inc(rows_out, 16)
                        if c + NB < ADA_PIECES:
                            sp.wait_ge(rows_out, 16 * (c + 1))
                            piece(c + NB)
                    sp.wait_ge(rows_out, 16 * ADA_PIECES)
                    sp.dma_start(modr[:, :], mod_dram[L, :, :, :].rearrange("s m n -> (s m) n")).then_inc(modr_in, 16)
                    sp.wait_ge(cache_in, 16 * (7 + H))
                    if first:
                        sp.wait_ge(stored, 16 * (1 + DEPTH))
                    experts_sync_end(sp, E)

                @block.tensor
                def _(pe):
                    rows = experts_tensor(pe, E)
                    pe.wait_ge(loaded2, 32)
                    for h in range(H):
                        pe.matmul(bank(3, parts=NOPE)[:, h * P:(h + 1) * P], w_kv[:, h, 0:NOPE], ckvT_c, start=True, stop=True)
                    pe.matmul(bank(4, GW).rearrange("p (h n) -> p h n", h=H), ckvT_c, w_kv[:, :, NOPE:NOPE + VD],
                              start=True, stop=True).then_inc(kv_ctx, 1)
                    if first:
                        pe.wait_ge(cond_done, 1)
                    for c in range(ADA_PIECES):
                        pe.wait_ge(piece_in[c % NB], 32 * (c // NB + 1))
                        if c >= NB:
                            pe.wait_ge(row_sb, c - NB + 1)
                        for k in range(KD):
                            last = pe.matmul(bank(c % NB, parts=2), condS[:, k, :], ada[:, c % NB, k, :], start=(k == 0), stop=(k == KD - 1))
                        last.then_inc(pieces_used, 1)
                        rows((c + 1) * SHARE)
                    if first:
                        pe.wait_ge(loaded, 16 * (3 + DEPTH))
                    pe.wait_ge(modr_in, 16)
                    pe.transpose(bank(5, 2 * MOD), modr[:, :], ident[0:2 * MOD, 0:2 * MOD]).then_inc(modT_done, 1)
                    rows(256)

                @block.scalar
                def _(act):
                    rows = experts_scalar(act, E)
                    if first:
                        start_scalar(act)
                    for c in range(ADA_PIECES):
                        rows((c + 1) * SHARE)
                    rows(256)

                @block.gpsimd
                def _(pool):
                    rows, finish = experts_gpsimd(pool, E)
                    experts_gpsimd_ended(pool, E)
                    if first:
                        start_gpsimd(pool)
                    for c in range(ADA_PIECES):
                        rows((c + 1) * SHARE)
                    finish()

                @block.vector
                def _(dve):
                    link = chain(dve, dve_chain)
                    rows, finish = experts_vector(dve, E)
                    dve.wait_ge(kv_ctx, 1)
                    dve.tensor_copy(ktC[0:NOPE, :, c0:c1], bank(3, parts=NOPE).rearrange("p (h n) -> p h n", h=H))
                    dve.tensor_copy(vC[:, CTX, :], bank(4, GW))
                    experts_vector_ended(dve, E)
                    for c in range(ADA_PIECES):
                        if first:
                            start_vector_piece(dve, c)
                        dve.wait_ge(pieces_used, c + 1)
                        if c >= NB:
                            dve.wait_ge(rows_out, 16 * (c - NB + 1))
                        ins = dve.tensor_tensor(mrow[:, c % NB, :], bank(c % NB, parts=2), brow[:, c % NB, :], ALU.add)
                        if c * PIECE // D in (1, 4):
                            link(ins)
                            ins = dve.tensor_scalar_add(mrow[:, c % NB, :], mrow[:, c % NB, :], 1.0)
                        ins.then_inc(row_sb, 1)
                        rows((c + 1) * SHARE)
                    dve.wait_ge(modT_done, 1)
                    dve.tensor_copy(modb[:, :, :].rearrange("p s m -> p (s m)"), bank(5, 2 * MOD))
                    finish()
            end_step()

        def step_input(L, b, context, weights, E):
            slot = ds(b * P, P)
            s = 0 if context else 1
            with nc.Block() as block:
                @block.sync
                def _(sp):
                    experts_sync(sp, E)
                    sp.dma_start(xs[:, :], of_block(x_dram, b)).then_inc(x_loaded, 16)
                    sp.dma_start(rope_t, a["c_rope"][:, ds(b, 1), :].rearrange("p b n -> p (b n)")).then_inc(loaded2, 16)
                    if weights:
                        def piece(c):
                            sp.dma_start(w_in[c].rearrange("p k n -> p (k n)"), a[f"w_in{c}"][L, :, :]).then_inc(piece_in[c], 16)
                        for c in IN_ORDER[:2]:
                            piece(c)
                        for dst, src in ((w_uq, a["w_uq"][L, :, :].rearrange("p (k n) -> p k n", k=2)),
                                         (w_ukv, a["w_ukv"][L, :, :].rearrange("p (h n) -> p h n", h=H)),
                                         (a_wT, a["a_wT"][L, :, :, :]),
                                         (a_g, row(a["a_g"][L:L + 1, :])), (a_bb, row(a["a_bb"][L:L + 1, :])),
                                         (mq_g, row(a["mq_g"][L:L + 1, :])), (mkv_g, row(a["mkv_g"][L:L + 1, :]))):
                            sp.dma_start(dst, src).then_inc(loaded, 16)
                        for c in IN_ORDER[2:]:
                            piece(c)
                    n_out = 0
                    if context:
                        sp.wait_ge(z_dve, 1)
                        sp.dma_start(a["o_nat_v"][0, L, :, :, :].rearrange("h t d -> t h d"),
                                     z[:, C_B + 2 * GW:C_B + 3 * GW].rearrange("p (h d) -> p h d", h=H)).then_inc(stored, 16)
                        sp.wait_ge(z_act, 1)
                        sp.dma_start(a["o_krope"][0, L, :, :], z[:, C_C + QR + KVR:C_D]).then_inc(stored, 16)
                        sp.wait_ge(z_dve, 2)
                        sp.dma_start(a["o_swa_k"][0, L, :, :, :].rearrange("h t d -> t h d"),
                                     z[:, C_D + GW:C_D + GW + 2 * HD].rearrange("p (h d) -> p h d", h=2)).then_inc(stored, 16)
                        sp.dma_start(a["o_swa_v"][0, L, :, :, :].rearrange("h t d -> t h d"),
                                     z[:, C_D + GW + 2 * HD:IN_COLS].rearrange("p (h d) -> p h d", h=2)).then_inc(stored, 16)
                        sp.wait_ge(latent_n, 2)
                        sp.dma_start(a["o_ckv"][0, L, :, :], ckvn).then_inc(stored, 16)
                        sp.wait_ge(z_act, 2)
                        sp.dma_start(a["o_nat_k"][0, L, :, :, :].rearrange("h t d -> t h d"),
                                     z[:, C_B + GW:C_B + 2 * GW].rearrange("p (h d) -> p h d", h=H)).then_inc(stored, 16)
                        n_out = 6
                    sp.wait_ge(spilled, 4)
                    sp.dma_start(spill_dram[ds(b, 1), :, 0:SP_C].rearrange("b p n -> (b p) n"), spill[:, 0:SP_C]).then_inc(stored, 16)
                    sp.dma_start(spill_dram[ds(b, 1), 0:CH, SP_C:SP_COLS].rearrange("b p n -> (b p) n"), spill[0:CH, SP_C:SP_COLS]).then_inc(stored, 16)
                    experts_sync_end(sp, E)
                    sp.wait_ge(stored, 16 * (n_out + 2))

                @block.tensor
                def _(pe):
                    rows = experts_tensor(pe, E)
                    pe.wait_ge(x_loaded, 16)
                    for k in range(KD):
                        last = pe.transpose(ps[:, 4 * 512 + k * P:4 * 512 + (k + 1) * P], xs[:, k * P:(k + 1) * P], ident[:, :])
                    last.then_inc(xT_done, 1)
                    pe.wait_ge(hT_sb, 1)
                    rows(16)
                    for i, c in enumerate(IN_ORDER):
                        n = min(PIECE, IN_COLS - c * PIECE)
                        if weights:
                            pe.wait_ge(piece_in[c], 16)
                        for k in range(KD):
                            last = pe.matmul(bank(c, n), hT[:, k, :], w_in[c][:, k, :], start=(k == 0), stop=(k == KD - 1))
                        last.then_inc(z_done, 1)
                        rows(16 + 32 * (i + 1))
                        if i == 3:
                            pe.wait_ge(latent_n, 2)
                            pe.wait_ge(rope_done, 1)
                            for k in range(2):
                                pe.transpose(bank(5)[:, k * P:(k + 1) * P], cqn[:, k * P:(k + 1) * P], ident[:, :])
                            pe.transpose(bank(5)[:, 2 * P:3 * P], ckvn, ident[:, :])
                            pe.transpose(bank(5, parts=CH)[:, 3 * P:4 * P], kr, ident[:, :]).then_inc(latent_T, 1)
                    if weights:
                        pe.wait_ge(loaded, 16 * 7)
                    pe.wait_ge(latent_sb, 1)
                    pe.wait_ge(z_act, 1)
                    pe.wait_ge(z_dve, 2)
                    for k in range(2):
                        pe.matmul(bank(2, H * CH), cqT[:, k, :], w_uq[:, k, :], start=(k == 0), stop=(k == 1))
                    for h in range(H):
                        pe.matmul(bank(3, parts=NOPE)[:, h * P:(h + 1) * P], w_ukv[:, h, 0:NOPE], ckvT, start=True, stop=True)
                    pe.matmul(bank(4, GW).rearrange("p (h n) -> p h n", h=H), ckvT, w_ukv[:, :, NOPE:NOPE + VD],
                              start=True, stop=True).then_inc(up_done, 1)
                    pe.wait_ge(rope_done, 2)
                    for g in range(3):
                        last = pe.transpose(bank(5)[:, g * P:(g + 1) * P], zr[:, g * P:(g + 1) * P], ident[:, :])
                    last.then_inc(qkD_T, 1)
                    pe.wait_ge(vn_done, 1)
                    for h in range(H):
                        last = pe.matmul(bank(0, GW)[:, h * HD:(h + 1) * HD], a_wT[:, h, :], vn[:, h * HD:(h + 1) * HD], start=True, stop=True)
                    last.then_inc(mix_done, 1)
                    pe.wait_ge(z_act, 2)
                    for g in range(4):
                        last = pe.transpose(bank(1)[:, g * P:(g + 1) * P], z[:, C_B + g * P:C_B + (g + 1) * P], ident[:, :])
                    last.then_inc(qkB_T, 1)
                    rows(224)
                    pe.wait_ge(qc_roped, 1)
                    pe.wait_ge(mix_used, 1)
                    for h in range(H):
                        last = pe.transpose(bank(0, parts=CH)[:, h * P:(h + 1) * P], qc[:, h * CH:(h + 1) * CH], ident[:, :])
                    last.then_inc(qcT_done, 1)
                    rows(256)

                @block.scalar
                def _(act):
                    rows = experts_scalar(act, E)
                    rows(80)
                    act.wait_ge(z_done, 2)
                    act.copy(z[:, 1536:2048], bank(3)).then_inc(z_act, 1)
                    rows(144)
                    act.wait_ge(z_done, 4)
                    act.activation(gz, bank(0), ACT.Gelu_apprx_tanh).then_inc(gelu_done, 1)
                    rows(176)
                    act.wait_ge(z_done, 5)
                    act.copy(z[:, 512:1024], bank(1)).then_inc(z_act, 1)
                    act.wait_ge(up_done, 1)
                    act.copy(ktC[0:NOPE, :, slot], bank(3, parts=NOPE).rearrange("p (h n) -> p h n", h=H))
                    act.copy(vC[:, ds(b, 1), :], bank(4, GW).unsqueeze(1))
                    act.wait_ge(qkD_T, 1)
                    act.copy(spill[:, SP_D:SP_D + 2 * P], bank(5)[:, 0:2 * P])
                    act.copy(ktD[:, slot], bank(5)[:, 2 * P:3 * P]).then_inc(spilled, 1)
                    act.wait_ge(qkB_T, 1)
                    act.copy(spill[:, SP_B:SP_B + 2 * P], bank(1)[:, 0:2 * P])
                    act.copy(ktB[:, :, slot], bank(1)[:, 2 * P:4 * P].rearrange("p (g n) -> p g n", g=2)).then_inc(spilled, 1)
                    rows(224)
                    act.wait_ge(qcT_done, 1)
                    act.copy(spill[0:CH, SP_C:SP_COLS], bank(0, parts=CH)).then_inc(spilled, 1)
                    rows(256)

                @block.gpsimd
                def _(pool):
                    link = chain(pool, pool_chain)
                    rows, finish = experts_gpsimd(pool, E)

                    def rope(out, src, nh, stride, half, first, tabs):
                        w = 2 * half
                        s4 = src.rearrange("p (h n) -> p h n", h=nh)
                        o4 = out.rearrange("p (h n) -> p h n", h=nh)
                        t4 = ropeA[:, 0:nh * w].rearrange("p (h n) -> p h n", h=nh)
                        u4 = ropeB[:, 0:nh * w].rearrange("p (h n) -> p h n", h=nh)
                        cos = rope_t[:, tabs:tabs + w].unsqueeze(1).broadcast_to([P, nh, w])
                        sin = rope_t[:, tabs + w:tabs + 2 * w].unsqueeze(1)
                        pool.tensor_tensor(u4, s4[:, :, first:first + w], cos, ALU.mult)
                        pool.tensor_tensor(t4[:, :, 0:half], s4[:, :, first + half:first + w],
                                           sin[:, :, 0:half].broadcast_to([P, nh, half]), ALU.mult)
                        link(pool.tensor_tensor(t4[:, :, half:w], s4[:, :, first:first + half],
                                                sin[:, :, half:w].broadcast_to([P, nh, half]), ALU.mult))
                        return pool.tensor_tensor(o4[:, :, first:first + w], u4, t4, ALU.add)

                    rows(96)
                    pool.wait_ge(var_done, 1)
                    pool.tensor_tensor(rstd[:, 1:3], ve[:, 1:3], neg_half[:, 0:2], ALU.pow).then_inc(rstd_done, 1)
                    pool.wait_ge(xT_done, 1)
                    pool.wait_ge(z_act, 1)
                    pool.wait_ge(loaded2, 16)
                    rope(kr[:, NOPE:CH], z[:, C_C + QR + KVR:C_D], 1, CH, ROPE // 2, 0, 0).then_inc(rope_done, 1)
                    pool.wait_ge(rope_done, 1)
                    pool.wait_ge(z_dve, 2)
                    rope(zr, z[:, C_D:C_D + 6 * HD], 6, HD, HD // 2, 0, 2 * ROPE).then_inc(rope_done, 1)
                    pool.wait_ge(rope_done, 2)
                    rows(144)
                    pool.wait_ge(var_done, 2)
                    pool.tensor_tensor(rstd[:, 0:1], ve[:, 0:1], neg_half[:, 0:1], ALU.pow).then_inc(rstd_done, 1)
                    rows(176)
                    pool.wait_ge(up_sb, 1)
                    rope(qc, qc, H, CH, ROPE // 2, NOPE, 0).then_inc(qc_roped, 1)
                    finish()

                @block.vector
                def _(dve):
                    link = chain(dve, dve_chain)
                    rows, finish = experts_vector(dve, E)
                    experts_vector_ended(dve, E)
                    if weights:
                        link(dve.memset(kr[:, 0:NOPE], 0.0))
                    dve.wait_ge(xT_done, 1)
                    for k in range(KD):
                        last = dve.tensor_scalar(hT[:, k, :], ps[:, 4 * 512 + k * P:4 * 512 + (k + 1) * P],
                                                 modb[:, s, KD + k:KD + k + 1], modb[:, s, k:k + 1], ALU.mult, ALU.add)
                    last.then_inc(hT_sb, 1)
                    rows(48)
                    dve.wait_ge(z_done, 1)
                    dve.tensor_copy(z[:, 1024:1536], bank(2)).then_inc(z_dve, 1)
                    rows(96)
                    dve.wait_ge(z_dve, 1)
                    dve.wait_ge(z_act, 1)
                    link(dve.tensor_tensor_reduce(out=cqn, in0=z[:, C_C:C_C + QR], in1=z[:, C_C:C_C + QR], scale=1.0, scalar=0.0,
                                                  op0=ALU.mult, op1=ALU.add, accum_out=small[:, 1:2]))
                    link(dve.tensor_tensor_reduce(out=ckvn, in0=z[:, C_C + QR:C_C + QR + KVR], in1=z[:, C_C + QR:C_C + QR + KVR],
                                                  scale=1.0, scalar=0.0, op0=ALU.mult, op1=ALU.add, accum_out=small[:, 2:3]))
                    dve.tensor_scalar(ve[:, 1:2], small[:, 1:2], 1.0 / QR, EPS, ALU.mult, ALU.add)
                    dve.tensor_scalar(ve[:, 2:3], small[:, 2:3], 1.0 / KVR, EPS, ALU.mult, ALU.add).then_inc(var_done, 1)
                    dve.tensor_copy(vB[:, ds(b, 1), :], z[:, C_B + 2 * GW:C_B + 3 * GW].unsqueeze(1))
                    dve.wait_ge(z_done, 3)
                    dve.tensor_copy(z[:, 2048:IN_COLS], bank(4, IN_COLS - 2048)).then_inc(z_dve, 1)
                    if weights:
                        dve.wait_ge(loaded, 16 * 7)
                    dve.wait_ge(rstd_done, 1)
                    dve.scalar_tensor_tensor(cqn, z[:, C_C:C_C + QR], rstd[:, 1:2], mq_g, ALU.mult, ALU.mult).then_inc(latent_n, 1)
                    dve.scalar_tensor_tensor(ckvn, z[:, C_C + QR:C_C + QR + KVR], rstd[:, 2:3], mkv_g, ALU.mult, ALU.mult).then_inc(latent_n, 1)
                    dve.wait_ge(z_dve, 2)
                    dve.tensor_copy(vD[:, ds(b, 1), :], z[:, C_D + GW + 2 * HD:IN_COLS].unsqueeze(1))
                    rows(144)
                    dve.wait_ge(gelu_done, 1)
                    link(dve.bn_stats(st12[:, 0, :], gz[:, GW:2 * GW]))
                    link(dve.bn_aggr(mv[:, :], st12[:, 0, :]))
                    dve.tensor_scalar_add(ve[:, 0:1], mv[:, 1:2], EPS).then_inc(var_done, 1)
                    dve.wait_ge(latent_T, 1)
                    dve.tensor_copy(cqT, bank(5)[:, 0:2 * P].rearrange("p (k n) -> p k n", k=2))
                    dve.tensor_copy(ckvT, bank(5)[:, 2 * P:3 * P])
                    dve.tensor_copy(ktC[NOPE:CH, :, slot], bank(5)[NOPE:CH, 3 * P:4 * P].unsqueeze(1).broadcast_to([ROPE, H, P])).then_inc(latent_sb, 1)
                    dve.wait_ge(rstd_done, 2)
                    link(dve.tensor_scalar(vn, gz[:, GW:2 * GW], mv[:, 0:1], rstd[:, 0:1], ALU.subtract, ALU.mult))
                    link(dve.tensor_tensor(vn, vn, a_g, ALU.mult))
                    dve.tensor_tensor(vn, vn, a_bb, ALU.add).then_inc(vn_done, 1)
                    rows(176)
                    dve.wait_ge(up_done, 1)
                    dve.tensor_copy(qc, bank(2, H * CH)).then_inc(up_sb, 1)
                    dve.wait_ge(mix_done, 1)
                    for h in range(H):
                        last = dve.scalar_tensor_tensor(spill[:, SP_A + h * HD:SP_A + (h + 1) * HD], bank(0, GW)[:, h * HD:(h + 1) * HD],
                                                        a_b[:, h:h + 1], gz[:, h * HD:(h + 1) * HD], ALU.add, ALU.mult)
                    last.then_inc(mix_used, 1)
                    dve.wait_ge(mix_used, 1)
                    dve.sem_inc(spilled, 1)
                    rows(224)
                    finish()
            end_step()

        def step_attend_route(L, b, context, weights, E):
            nk = 1 if context else NLAT + 1
            k0 = 0 if context else 1
            sm = 0 if context else 1
            NH = 3 * H
            lat = NLAT * P
            G = 2 * PH
            HEAD_SHARE, tail, q_share, route_share = SHARES[E.heads if E is not None else PH]
            A_END = NH * HEAD_SHARE
            TAIL = [A_END + n for n in tail]
            HEAD_MID = HEAD_SHARE // 2
            ROUTE = [TAIL[-1] + min(i + 1, 4) * q_share + max(i - 3, 0) * route_share for i in range(12)]
            assert ROUTE[-1] <= 256

            def before(i):
                return ((ROUTE[i - 1] if i else TAIL[-1]) + ROUTE[i]) // 2

            def operands(i):
                g, h = divmod(i, H)
                if g == 1:
                    return qTC[:, h * P:(h + 1) * P], ktC[:, h, :]
                if g == 0:
                    r = slice((h % 2) * HD, (h % 2 + 1) * HD)
                    return qT[r, SP_B + (h // 2) * P:SP_B + (h // 2 + 1) * P], ktB[r, h // 2, :]
                r = slice((h // 2) * HD, (h // 2 + 1) * HD)
                return qT[r, SP_D + (h % 2) * P:SP_D + (h % 2 + 1) * P], ktD[r, :]

            def values(i, s):
                g, h = divmod(i, H)
                if g == 2:
                    return vD[:, s, (h // 2) * HD:(h // 2 + 1) * HD]
                return (vB, vC)[g][:, s, h * HD:(h + 1) * HD]

            def out_of(i):
                o = (i % 2) * 1024 + 768
                return ps[:, o:o + HD]

            with nc.Block() as block:
                @block.sync
                def _(sp):
                    experts_sync(sp, E)

                    def lay(dst, src, s):
                        sp.dma_start(dst, src).then_inc(s, 16)
                    lay(qT, spill_dram[ds(b, 1), :, 0:SP_A].rearrange("b p n -> (b p) n"), loaded)
                    lay(qTC, spill_dram[ds(b, 1), 0:CH, SP_C:SP_COLS].rearrange("b p n -> (b p) n"), loaded)
                    if not context:
                        lay(toep[:, :, :], toep_dram[L, :, :].rearrange("p (h n) -> p h n", h=H)[:, :, ds((2 * NLAT - 2 * b) * GRID_W, lat)], x_loaded)
                        lay(band[:, :], a["c_band"][:, ds(NLAT * P - b * P, lat)], x_loaded)
                    lay(ob[:, 0:GW], spill_dram[ds(b, 1), :, SP_A:SP_C].rearrange("b p n -> (b p) n"), loaded2)
                    lay(W[:, 0:KD * D], a["w_out"][L, :, :], loaded2)
                    experts_sync_ended(sp, E)
                    lay(og_bc, row(a["out_g"][L:L + 1, :]), loaded2)
                    lay(bc[:, 0, :], mod_row(L, sm, 2), loaded2)
                    lay(bc[:, 1, :], row(a["ln1_g"][L:L + 1, :]), loaded2)
                    lay(bc[:, 2, :], row(a["ln1_b"][L:L + 1, :]), loaded2)
                    if weights:
                        for i, c in enumerate(Q_ORDER[:Q_KEPT]):
                            lay(W[:, c * WP:(c + 1) * WP], a["w_q"][L, c, :, :], piece_in[i])
                    sp.wait_ge(negmax, H)
                    lay(sh2_bc, mod_row(L, sm, 3), loaded2)
                    lay(sc2_bc, mod_row(L, sm, 4), loaded2)
                    sp.wait_ge(s_done, NH)
                    lay(xs[:, :], of_block(x_dram, b), loaded2)
                    sp.wait_ge(xnew_done, 1)
                    sp.dma_start(of_block(x_dram, b), xs[:, :]).then_inc(stored, 16)
                    sp.wait_ge(x2_done, 1)
                    sp.dma_start(of_block(x2_dram, b), ob[:, :]).then_inc(stored, 16)
                    for i, c in enumerate(Q_ORDER[Q_KEPT:]):
                        lay(W[:, c * WP:(c + 1) * WP], a["w_q"][L, c, :, :], piece_in[Q_KEPT + i])
                    lay(skT, a["skT"][L, :, :, :], piece_in[Q_PIECES])
                    sp.wait_ge(route_done, 2)
                    sp.dma_start(of_block(eid_dram, b), eid[:, :]).then_inc(stored, 16)
                    sp.dma_start(of_block(gate_dram, b), gates[:, :]).then_inc(stored, 16)
                    experts_sync_end(sp, E)
                    sp.wait_ge(stored, 64)

                @block.tensor
                def _(pe):
                    rows = experts_tensor(pe, E)

                    def score(i):
                        q, k = operands(i)
                        if i >= 2:
                            pe.wait_ge(exp_done, i - 1)
                            pe.wait_ge(pv_used, i - 1)
                        o = (i % 2) * 1024
                        if nk > 1:
                            pe.matmul(ps[:, o:o + lat], q, k[:, k0 * P:k0 * P + lat], start=True, stop=True)
                            pe.matmul(ps[:, o + lat:o + lat + P], q, k[:, CTX * P:(CTX + 1) * P], start=True, stop=True).then_inc(s_done, 1)
                        else:
                            pe.matmul(ps[:, o:o + P], q, k[:, 0:P], start=True, stop=True).then_inc(s_done, 1)
                    pe.wait_ge(loaded, 32)
                    score(0)
                    for i in range(NH):
                        if i + 1 < NH:
                            score(i + 1)
                        rows(i * HEAD_SHARE)
                        pe.wait_ge(exp_done, i + 1)
                        if i >= 1:
                            pe.wait_ge(prT_sb, i)
                        for s in range(nk):
                            last = pe.transpose(ps[:, 2048 + s * P:2048 + (s + 1) * P], pr[:, i % 2, s * P:(s + 1) * P], ident[:, :])
                        last.then_inc(prT_done, 1)
                        rows(i * HEAD_SHARE + HEAD_MID)
                        pe.wait_ge(prT_sb, i + 1)
                        for s in range(nk):
                            last = pe.matmul(out_of(i), prT[:, i % 2, s * P:(s + 1) * P], values(i, k0 + s),
                                             start=(s == 0), stop=(s == nk - 1))
                        last.then_inc(pv_done, 1)
                    rows(A_END)
                    pe.wait_ge(on_done, 1)
                    for k in range(KD):
                        last = pe.transpose(ps[:, k * P:(k + 1) * P], ob[:, k * P:(k + 1) * P], ident[:, :])
                    last.then_inc(oT_done, 1)
                    rows(TAIL[0])
                    pe.wait_ge(oT_sb, 1)
                    for c in range(2):
                        for k in range(KD):
                            last = pe.matmul(bank(2 + c), hT[:, k, :], w_out[:, k, c * 512:(c + 1) * 512], start=(k == 0), stop=(k == KD - 1))
                        if c == 0:
                            rows(TAIL[1])
                    last.then_inc(y_done, 1)
                    rows(TAIL[3])
                    pe.wait_ge(x2_done, 1)
                    for k in range(KD):
                        last = pe.transpose(ps[:, k * P:(k + 1) * P], ob[:, k * P:(k + 1) * P], ident[:, :])
                    last.then_inc(x2T_done, 1)
                    pe.wait_ge(x2T_sb, 1)
                    for i, c in enumerate(Q_ORDER):
                        if weights or i >= Q_KEPT:
                            pe.wait_ge(piece_in[i], 16)
                        for g in range(4):
                            for k in range(KD):
                                last = pe.matmul(bank(2 + c)[:, g * P:(g + 1) * P], w_q[c][:, k, g * P:(g + 1) * P], hT[:, k, :],
                                                 start=(k == 0), stop=(k == KD - 1))
                            if g == 1:
                                rows(before(i))
                        last.then_inc(q_done, 1)
                        rows(ROUTE[i])
                    pe.wait_ge(piece_in[Q_PIECES], 16)
                    for i, c in enumerate(Q_ORDER):
                        pe.wait_ge(q_sb, i + 1)
                        if i >= 2:
                            pe.wait_ge(sc_sb, i - 1)
                        for g in range(4):
                            last = pe.matmul(bank(i % 2)[:, g * P:(g + 1) * P], qsel[:, 4 * c + g, :], skT[:, g % 2, :], start=True, stop=True)
                        last.then_inc(sc_done, 1)
                    for i in range(4, 12):
                        rows(ROUTE[i])
                    rows(256)

                @block.scalar
                def _(act):
                    rows = experts_scalar(act, E)
                    for i in range(NH):
                        g, h = divmod(i, H)
                        o = (i % 2) * 1024
                        plain = nk == 1 or g == 1
                        src = ps[:, o:o + nk * P] if plain else sS[:, i % 2, :]
                        sc = (MLA_SCALE if g == 1 else SCALE) if plain else 1.0
                        rows(i * HEAD_SHARE)
                        act.wait_ge(negmax, i + 1)
                        if i >= 2:
                            act.wait_ge(prT_done, i - 1)
                        if g == 2:
                            act.activation(small[:, 32 + h:33 + h], sinks[:, h:h + 1], ACT.Exp, bias=small[:, 16 + i:17 + i]).then_inc(sink_done, 1)
                        act.activation(pr[:, i % 2, 0:nk * P], src, ACT.Exp, bias=small[:, 16 + i:17 + i], scale=sc,
                                       accum_out=small[:, 36 + i:37 + i]).then_inc(exp_done, 1)
                        act.wait_ge(prT_done, i + 1)
                        if i >= 2:
                            act.wait_ge(pv_done, i - 1)
                        act.copy(prT[:, i % 2, 0:nk * P], ps[:, 2048:2048 + nk * P]).then_inc(prT_sb, 1)
                        rows(i * HEAD_SHARE + HEAD_MID)
                    rows(A_END)
                    act.wait_ge(oT_done, 1)
                    act.copy(hflat, ps[:, 0:KD * P]).then_inc(oT_sb, 1)
                    rows(TAIL[3])
                    act.wait_ge(x2_done, 1)
                    act.wait_ge(x2T_done, 1)
                    act.copy(hflat, ps[:, 0:KD * P]).then_inc(x2T_sb, 1)
                    for i, c in enumerate(Q_ORDER):
                        rows(before(i))
                        act.wait_ge(q_done, i + 1)
                        act.copy(qsel[:, 4 * c:4 * c + 4, :], bank(2 + c).rearrange("p (g t) -> p g t", t=P)).then_inc(q_sb, 1)
                        rows(ROUTE[i])
                    for i, c in enumerate(Q_ORDER):
                        act.wait_ge(sc_done, i + 1)
                        act.copy(scores[:, 4 * c:4 * c + 4, :], bank(i % 2).rearrange("p (g n) -> p g n", n=PK)).then_inc(sc_sb, 1)
                    for i in range(4, 12):
                        rows(ROUTE[i])
                        if i == 10:
                            act.wait_ge(cent_done, 1)
                            act.activation(fe, fe, ACT.Exp).then_inc(expf_done, 1)
                    rows(256)

                @block.gpsimd
                def _(pool):
                    rows, finish = experts_gpsimd(pool, E)
                    for i in range(NH):
                        if i == 1:
                            rows(HEAD_MID)
                            experts_gpsimd_ended(pool, E)
                        rows(i * HEAD_SHARE)
                    rows(A_END)
                    pool.wait_ge(var_done, 1)
                    pool.tensor_tensor(rstd[:, :], ve[:, :], neg_half[:, :], ALU.pow).then_inc(rstd_done, 1)
                    rows(TAIL[0])
                    rows(TAIL[2])
                    pool.wait_ge(var_done, 2)
                    pool.tensor_tensor(rstd[:, 0:1], ve[:, 0:1], neg_half[:, 0:1], ALU.pow).then_inc(rstd_done, 1)
                    for i in range(12):
                        rows(ROUTE[i])
                    finish()

                @block.vector
                def _(dve):
                    link = chain(dve, dve_chain)
                    rows, finish_experts = experts_vector(dve, E)

                    def negate_max(i):
                        g, h = divmod(i, H)
                        o = (i % 2) * 1024
                        mx, nm = small[:, i:i + 1], small[:, 16 + i:17 + i]
                        dve.wait_ge(s_done, i + 1)
                        plain = nk == 1 or g == 1
                        sc = MLA_SCALE if g == 1 else SCALE
                        if not plain:
                            if i >= 2:
                                dve.wait_ge(exp_done, i - 1)
                            bias = toep[:, h, :] if g == 0 else band[:, :]
                            dve.scalar_tensor_tensor(sS[:, i % 2, 0:lat], ps[:, o:o + lat], sc, bias, ALU.mult, ALU.add)
                            link(dve.tensor_scalar_mul(sS[:, i % 2, lat:lat + P], ps[:, o + lat:o + lat + P], sc))
                            link(dve.reduce_max(mx, sS[:, i % 2, :], AX))
                            sc = 1.0
                        else:
                            link(dve.reduce_max(mx, ps[:, o:o + nk * P], AX))
                        if g == 2:
                            link(dve.tensor_scalar(mx, mx, sc, sinks[:, h:h + 1], ALU.mult, ALU.max))
                            sc = 1.0
                        dve.tensor_scalar_mul(nm, mx, -sc).then_inc(negmax, 1)

                    def finish(i):
                        g, h = divmod(i, H)
                        l = small[:, 36 + i:37 + i]
                        dve.wait_ge(exp_done, i + 1)
                        if g == 2:
                            dve.wait_ge(sink_done, h + 1)
                            link(dve.tensor_tensor(l, l, small[:, 32 + h:33 + h], ALU.add))
                        link(dve.reciprocal(small[:, 48 + i:49 + i], l))
                        dve.wait_ge(pv_done, i + 1)
                        dve.tensor_scalar_mul(ob[:, GW + i * HD:GW + (i + 1) * HD], out_of(i), small[:, 48 + i:49 + i]).then_inc(pv_used, 1)

                    if not context:
                        dve.wait_ge(x_loaded, 32)
                    negate_max(0)
                    for i in range(NH):
                        if i + 1 < NH:
                            negate_max(i + 1)
                        if i == 1:
                            experts_vector_ended(dve, E)
                        rows(i * HEAD_SHARE)
                        rows(i * HEAD_SHARE + HEAD_MID)
                        finish(i)
                    rows(A_END)
                    dve.wait_ge(pv_used, NH)
                    dve.wait_ge(loaded2, 16 * 9)
                    if E is not None and E.ended is not None:
                        dve.wait_ge(end_stored, 16)
                    for g in range(4):
                        o = ob[:, g * GW:(g + 1) * GW]
                        last = dve.tensor_tensor_reduce(out=xa[:, g * GW:(g + 1) * GW], in0=o, in1=o, scale=1.0, scalar=0.0,
                                                        op0=ALU.mult, op1=ALU.add, accum_out=small[:, g:g + 1])
                    link(last)
                    dve.tensor_scalar(ve[:, :], small[:, 0:4], 1.0 / GW, EPS, ALU.mult, ALU.add).then_inc(var_done, 1)
                    dve.wait_ge(rstd_done, 1)
                    for g in range(4):
                        o = ob[:, g * GW:(g + 1) * GW]
                        last = dve.scalar_tensor_tensor(o, o, rstd[:, g:g + 1], og_bc[:, g * GW:(g + 1) * GW], ALU.mult, ALU.mult)
                    last.then_inc(on_done, 1)
                    rows(TAIL[0])
                    rows(TAIL[1])
                    dve.wait_ge(y_done, 1)
                    link(dve.tensor_tensor(xa, ps[:, 2 * 512:4 * 512], bc[:, 0, :], ALU.mult))
                    link(dve.scalar_tensor_tensor(xa, xs[:, :], ALPHA, xa, ALU.mult, ALU.add))
                    rows(TAIL[2])
                    layer_norm(link, dve, xa, bc[:, 1, :], bc[:, 2, :], xs[:, :], st12, mv, ve[:, 0:1], rstd[:, 0:1],
                               var_done, rstd_done, 2).then_inc(xnew_done, 1)
                    dve.wait_ge(xnew_done, 1)
                    link(dve.tensor_tensor(ob, xs[:, :], sc2_bc, ALU.mult))
                    dve.tensor_tensor(ob, ob, sh2_bc, ALU.add).then_inc(x2_done, 1)
                    rows(TAIL[3])
                    for i in range(4):
                        rows(ROUTE[i])

                    def top16(vals, idx, src, src2, n, points):
                        for g in range(n):
                            last = dve.max(vals[:, g, 0:8], src[:, g, :])
                        link(last)
                        rows(points[0])
                        for g in range(n):
                            dve.max_index(idx[:, g, 0:8], vals[:, g, 0:8], src[:, g, :])
                            last = dve.match_replace(src2[:, g, :], vals[:, g, 0:8], src[:, g, :], -3e38)
                            if g + 1 == n // 2:
                                rows((points[0] + points[1]) // 2)
                        link(last)
                        rows(points[1])
                        for g in range(n):
                            last = dve.max(vals[:, g, 8:16], src2[:, g, :])
                        link(last)
                        rows(points[2])
                        for g in range(n):
                            last = dve.max_index(idx[:, g, 8:16], vals[:, g, 8:16], src2[:, g, :])
                        link(last)

                    dve.wait_ge(sc_sb, 4)
                    top16(sv, si, scores, scores2, G, ROUTE[4:7])
                    dve.tensor_copy(sif, si)
                    sv2 = sv.rearrange("p (h s) k -> p h s k", s=2)
                    link(dve.tensor_tensor(cand.rearrange("p h (i j) -> p h i j", i=TOPK),
                                           sv2[:, :, 0, :].unsqueeze(3).broadcast_to([P, PH, TOPK, TOPK]),
                                           sv2[:, :, 1, :].unsqueeze(2).broadcast_to([P, PH, TOPK, TOPK]), ALU.add))
                    top16(fv, fi, cand, cand2, PH, ROUTE[7:10])
                    dve.tensor_tensor(fe, fv, fv[:, :, 0:1].broadcast_to([P, PH, TOPK]), ALU.subtract).then_inc(cent_done, 1)
                    rows(ROUTE[10])
                    fis = fi.rearrange("p h k -> p (h k)")
                    dve.tensor_scalar(fpart[:, 0, :], fis, 4, None, ALU.logical_shift_right)
                    link(dve.tensor_scalar(fpart[:, 1, :], fis, TOPK - 1, None, ALU.bitwise_and))
                    sif2 = sif.rearrange("p (h s) k -> p h s k", s=2)
                    oh4 = onehot.rearrange("p (h k) j -> p h k j", h=PH)
                    for s in range(2):
                        link(dve.tensor_tensor(onehot, fpart[:, s, :].unsqueeze(2).broadcast_to([P, NSEL, TOPK]),
                                               iota16[:, :].unsqueeze(1).broadcast_to([P, NSEL, TOPK]), ALU.is_equal))
                        link(dve.tensor_tensor(oh4, oh4, sif2[:, :, s, :].unsqueeze(2).broadcast_to([P, PH, TOPK, TOPK]), ALU.mult))
                        link(dve.reduce_sum(id_rc[:, s, :], onehot, AX))
                        if s == 0:
                            rows(before(11))
                    link(dve.scalar_tensor_tensor(eidf, id_rc[:, 0, :], float(PK), id_rc[:, 1, :], ALU.mult, ALU.add))
                    dve.tensor_scalar(eid[:, :], eidf, first_row[:, 0:1], None, ALU.add).then_inc(route_done, 1)
                    dve.wait_ge(expf_done, 1)
                    link(dve.reduce_sum(small[:, 0:PH], fe, AX))
                    link(dve.reciprocal(small[:, 8:8 + PH], small[:, 0:PH]))
                    dve.tensor_tensor(gates[:, :].rearrange("p (h k) -> p h k", h=PH), fe,
                                      small[:, 8:8 + PH].unsqueeze(2).broadcast_to([P, PH, TOPK]), ALU.mult).then_inc(route_done, 1)
                    rows(ROUTE[11])
                    finish_experts()
            end_step()

        def step_experts_only(E):
            with nc.Block() as block:
                @block.sync
                def _(sp):
                    experts_sync(sp, E)
                    experts_sync_ended(sp, E)
                    sp.wait_ge(end_stored, 16)

                @block.tensor
                def _(pe):
                    experts_tensor(pe, E)(256)

                @block.scalar
                def _(act):
                    experts_scalar(act, E)(256)

                @block.gpsimd
                def _(pool):
                    rows, finish = experts_gpsimd(pool, E)
                    experts_gpsimd_ended(pool, E)
                    finish()

                @block.vector
                def _(dve):
                    rows, finish = experts_vector(dve, E)
                    experts_vector_ended(dve, E)
                    finish()
            end_step()

        def step_last_sum(L, b):
            tiles = ended_tiles
            with nc.Block() as block:
                @block.sync
                def _(sp):
                    last_sum_in(sp, L, b, tiles)
                    sp.wait_ge(end_done, 1)
                    sp.dma_start(of_block(x_dram, b), tiles[0]).then_inc(end_stored, 16)
                    sp.wait_ge(end_stored, 16)

                @block.gpsimd
                def _(pool):
                    last_sum_rstd(pool)

                @block.vector
                def _(dve):
                    last_sum(dve, tiles)
            end_step()

        LAST = NBLK - 1
        step_modulation(0, None, first=True)
        step_input(0, 0, True, True, None)
        step_attend_route(0, 0, True, True, None)
        for L in range(DEPTH):
            step_input(L, 1, False, True, Experts(L, 0, 0, 1, begin=True))
            with nc.Fori(2, NBLK) as b:
                step_input(L, b, False, False, Experts(L, 0, b - 1, 1))
            step_attend_route(L, 1, False, True, Experts(L, 0, NLAT, PH - NLAT))
            step_attend_route(L, 2, False, False, Experts(L, 1, 0, PH, begin=True, ended=0))
            with nc.Fori(2, LAST) as b:
                step_attend_route(L, b + 1, False, False, Experts(L, b, 0, PH, begin=True, ended=b - 1))
            if L + 1 < DEPTH:
                step_modulation(L + 1, Experts(L, LAST, 0, 2, begin=True, ended=LAST - 1))
                step_input(L + 1, 0, True, True, Experts(L, LAST, 2, 1))
                step_attend_route(L + 1, 0, True, True, Experts(L, LAST, 3, PH - 3, end=True))
            else:
                step_experts_only(Experts(L, LAST, 0, PH, begin=True, ended=LAST - 1))
                step_last_sum(L, LAST)

        with nc.Block() as block:
            @block.sync
            def _(sp):
                sp.dma_start(a["o_y_prompt"].rearrange("a t d -> (a t) d"), x_dram[0, :, :]).then_inc(stored, 16)
                sp.dma_start(a["o_y_sample"].rearrange("a t d -> (a t) d"), x_dram[1:NBLK, :, :].rearrange("b p n -> (b p) n")).then_inc(stored, 16)
                sp.wait_ge(stored, 32)


def _constants():
    c = {"c_ident": np.eye(P, dtype=np.float32)}
    qc = np.arange(P)[:, None] % GRID_W
    kc = np.arange(GRID_W)[None, :]
    start = np.clip(qc - NA_KW // 2, 0, GRID_W - NA_KW)
    c["c_natmask"] = np.where((kc >= start) & (kc < start + NA_KW), 0.0, MASKED).astype(np.float32)
    off = np.arange(7 * P)[None, :] - 3 * P - np.arange(P)[:, None]
    c["c_band"] = np.where(np.abs(off) <= P, 0.0, MASKED).astype(np.float32)
    c["c_iota"] = np.tile(np.arange(TOPK, dtype=np.uint32), (P, 1))
    c["c_first"] = (np.arange(DEPTH, dtype=np.float32) * NEXP)[:, None]
    t = np.arange(DEC_SEQ)
    pos = [(t // GRID_W).astype(np.float32), (t % GRID_W).astype(np.float32)]
    tab = np.zeros((NBLK, P, ROPE_COLS), np.float32)
    at = 0
    for dim in (ROPE, HD):
        nf = dim // 4
        fr = (10000.0 ** (-np.arange(nf, dtype=np.float32) / nf)).astype(np.float32)
        ang = np.concatenate([pos[0][:, None] * fr, pos[1][:, None] * fr], -1)
        co, si = np.cos(ang), np.sin(ang)
        tab[0, :, at:at + dim] = 1.0
        tab[1:, :, at:at + dim] = np.concatenate([co, co], -1).reshape(NLAT, P, dim)
        tab[1:, :, at + dim:at + 2 * dim] = np.concatenate([-si, si], -1).reshape(NLAT, P, dim)
        at += 2 * dim
    c["c_rope"] = np.ascontiguousarray(tab.transpose(1, 0, 2))
    return c


def _layout(i):
    L = DEPTH

    def rows(w, n):
        return w.reshape(L, KD, P, n).transpose(0, 2, 1, 3).reshape(L, P, KD * n)

    g = {}
    g["x0"] = np.concatenate([i["x_prompt"].reshape(1, P, D), i["x_sample"].reshape(NLAT, P, D)])
    g["condT"] = np.stack([i["c_ctx"].reshape(KD, P), i["c"].reshape(KD, P)], -1).transpose(1, 0, 2)
    g["w_ada"] = i["w_ada"].reshape(L, KD, P, ADA_PIECES, PIECE).transpose(0, 3, 2, 1, 4).reshape(L, ADA_PIECES, P, WP)
    g["b_ada"] = i["b_ada"]
    w = i["w_in"]
    dq = w[:, :, C_D:C_D + GW].reshape(L, D, H, HD)[:, :, [0, 2, 1, 3]].reshape(L, D, GW)
    w = np.concatenate([w[:, :, :C_D], dq, w[:, :, C_D + GW:]], -1)
    for c in range(IN_PIECES):
        p = w[:, :, c * PIECE:(c + 1) * PIECE]
        g[f"w_in{c}"] = rows(p, p.shape[-1])
    g["w_out"] = rows(i["w_out"], D)
    g["w_q"] = i["peer_w_q"].reshape(L, KD, P, Q_PIECES, PIECE).transpose(0, 3, 2, 1, 4).reshape(L, Q_PIECES, P, WP)
    g["w_uq"] = i["mla_w_uq"].reshape(L, 2, P, H * CH).transpose(0, 2, 1, 3).reshape(L, P, 2 * H * CH)
    g["w_ukv"] = i["mla_w_ukv"]
    g["a_wT"] = i["a_w_s"].transpose(0, 3, 1, 2)
    g["a_bT"] = i["a_b_s"].transpose(0, 2, 1)
    g["a_g"], g["a_bb"] = i["a_norm_g"], i["a_norm_b"]
    g["mq_g"], g["mkv_g"] = i["mla_q_norm_g"], i["mla_kv_norm_g"]
    g["out_g"] = i["out_norm_g"]
    for n in ("ln1_g", "ln1_b", "ln2_g", "ln2_b"):
        g[n] = i[n]
    g["sinks"] = i["swa_sinks"]
    g["rpb"] = np.pad(i["nat_rpb"], ((0, 0), (0, 0), (0, 0), (RPB_PAD, RPB_ROW - RPB_PAD - 2 * NA_KW + 1)))
    g["natkT"] = i["cache_nat_k"][0].reshape(L, 2, 2, P, HD).transpose(0, 2, 4, 1, 3).reshape(L, P, 2, P)
    g["natv"] = i["cache_nat_v"][0].transpose(0, 2, 1, 3).reshape(L, P, GW)
    g["swakT"] = i["cache_swa_k"][0].transpose(0, 1, 3, 2).reshape(L, P, P)
    g["swav"] = i["cache_swa_v"][0].transpose(0, 2, 1, 3).reshape(L, P, 2 * HD)
    g["ckvT"] = i["cache_mla_ckv"][0].transpose(0, 2, 1)
    g["kropeT"] = i["cache_mla_krope"][0].transpose(0, 2, 1)
    g["skT"] = i["peer_sub_keys"].transpose(0, 3, 1, 2)
    g["peer_u"] = i["peer_u"].reshape(L * NEXP, D)
    g["peer_v"] = i["peer_v"].reshape(L * NEXP, D)
    return g


_OUTS = [("o_y_prompt", (1, SEQ, D)), ("o_y_sample", (1, DEC_SEQ, D)), ("o_nat_k", (1, DEPTH, H, SEQ, HD)),
         ("o_nat_v", (1, DEPTH, H, SEQ, HD)), ("o_ckv", (1, DEPTH, SEQ, KVR)), ("o_krope", (1, DEPTH, SEQ, ROPE)),
         ("o_swa_k", (1, DEPTH, 2, SEQ, HD)), ("o_swa_v", (1, DEPTH, 2, SEQ, HD))]


def kernel(**inputs):
    import concourse.bacc as bacc
    from concourse.bass_utils import run_bass_kernel_spmd

    nc = bacc.Bacc("TRN2", target_bir_lowering=False, num_devices=1)
    arrays, a = {}, {}
    for name, v in {**_constants(), **_layout({k: np.asarray(v) for k, v in inputs.items()})}.items():
        v = np.ascontiguousarray(v)
        arrays["in_" + name] = v
        a[name] = nc.dram_tensor("in_" + name, v.shape, mybir.dt.from_np(v.dtype), kind="ExternalInput").ap()
    for name, shape in _OUTS:
        a[name] = nc.dram_tensor(name, shape, F32, kind="ExternalOutput").ap()
    build(nc, a)
    r = run_bass_kernel_spmd(nc, [arrays], core_ids=[0])
    return tuple(r.results[0][name] for name, _ in _OUTS)
```
